# Optimizing a Trainium2 kernel written in Bass

```python
import math
import jax, jax.numpy as jnp
from jax import lax
import numpy as np

D_MODEL = 1024
BATCH = 1
SEQ = 512
DEPTH = 1

D_MIX = D_MODEL
GLA_HEADS = 4
GLA_DV = D_MIX // 2 // GLA_HEADS
GLA_DK = GLA_DV // 2
GLA_LOWRANK = 16
GLA_TAU = 16.0
GLA_CHUNK = 64
SWA_HEADS = 8
SWA_KV_HEADS = 2
SWA_HD = (D_MIX - GLA_HEADS * GLA_DV) // SWA_HEADS
SWA_WINDOW = 128
D_FF = 2816
CONV_K = 3
EPS = 1e-6

GLA_Q = GLA_HEADS * GLA_DK
GLA_K = GLA_HEADS * GLA_DK
GLA_V = GLA_HEADS * GLA_DV
GLA_R = GLA_HEADS * GLA_DV
SWA_Q = SWA_HEADS * SWA_HD
SWA_K = SWA_KV_HEADS * SWA_HD
SWA_V = SWA_KV_HEADS * SWA_HD
SPLITS = (GLA_Q, GLA_K, GLA_V, GLA_R, GLA_LOWRANK, SWA_Q, SWA_K, SWA_V)
P_IN = sum(SPLITS)


def alibi_slopes(n_heads):
    return np.array([2.0 ** (-8.0 * (h + 1) / n_heads) for h in range(n_heads)], dtype=np.float32)

def rms_norm(x, g):
    xf = x.astype(jnp.float32)
    y = xf * lax.rsqrt(jnp.mean(xf * xf, axis=-1, keepdims=True) + EPS)
    return (y * g.astype(jnp.float32)).astype(x.dtype)

def split_cols(z, sizes):
    idx = np.cumsum(sizes)[:-1].tolist()
    return jnp.split(z, idx, axis=-1)

def gla_chunked(q, k, v, log_a):
    B, L, H, dk = q.shape
    dv = v.shape[-1]
    C = GLA_CHUNK
    n = L // C

    def chunk(t):
        return t.astype(jnp.float32).reshape(B, n, C, H, t.shape[-1]).transpose(0, 3, 1, 2, 4)

    q, k, v, log_a = chunk(q), chunk(k), chunk(v), chunk(log_a)
    b = jnp.cumsum(log_a, axis=-2)
    b_last = b[..., -1:, :]
    qe = q * jnp.exp(b)
    ke = k * jnp.exp(-b)
    causal = jnp.tril(jnp.ones((C, C), dtype=bool))
    A = jnp.einsum('bhncd,bhnsd->bhncs', qe, ke)
    A = jnp.where(causal, A, 0.0)
    o_intra = jnp.einsum('bhncs,bhnsv->bhncv', A, v)
    kd = k * jnp.exp(b_last - b)
    chunk_state = jnp.einsum('bhncd,bhncv->bhndv', kd, v)
    decay = jnp.exp(b_last[..., 0, :])

    def step(S, inp):
        dec, cs = inp
        return S * dec[..., None] + cs, S

    S0 = jnp.zeros((B, H, dk, dv), jnp.float32)
    _, S_prev = lax.scan(step, S0, (jnp.moveaxis(decay, 2, 0), jnp.moveaxis(chunk_state, 2, 0)))
    S_prev = jnp.moveaxis(S_prev, 0, 2)
    o_inter = jnp.einsum('bhncd,bhndv->bhncv', qe, S_prev)
    o = o_intra + o_inter
    return o.transpose(0, 2, 3, 1, 4).reshape(B, L, H, dv)

def swa_sink_attention(q, k, v, sinks):
    B, L, Hq, hd = q.shape
    Hkv = k.shape[2]
    G = Hq // Hkv
    W = SWA_WINDOW
    nb = L // W
    qb = q.reshape(B, nb, W, Hkv, G, hd)
    kb = k.reshape(B, nb, W, Hkv, hd)
    vb = v.reshape(B, nb, W, Hkv, hd)
    pad = ((0, 0), (1, 0), (0, 0), (0, 0), (0, 0))
    kk = jnp.concatenate([jnp.pad(kb, pad)[:, :-1], kb], axis=2)
    vv = jnp.concatenate([jnp.pad(vb, pad)[:, :-1], vb], axis=2)
    s = jnp.einsum('bnqkgd,bnskd->bnkgqs', qb, kk,
                   preferred_element_type=jnp.float32) * (1.0 / math.sqrt(hd))
    i = jnp.arange(W)[:, None]
    j = jnp.arange(2 * W)[None, :]
    dist = (W + i - j).astype(jnp.float32)
    key_abs = (jnp.arange(nb)[:, None, None] - 1) * W + j[None]
    mask = (dist >= 0) & (dist < W) & (key_abs >= 0)
    slopes = jnp.asarray(alibi_slopes(Hq)).reshape(Hkv, G)
    s = s - slopes[:, :, None, None] * dist
    s = jnp.where(mask[None, :, None, None], s, -jnp.inf)
    sink = sinks.astype(jnp.float32).reshape(Hkv, G)[None, None, :, :, None, None]
    m = jnp.maximum(jnp.max(s, axis=-1, keepdims=True), sink)
    p = jnp.exp(s - m)
    denom = jnp.sum(p, axis=-1, keepdims=True) + jnp.exp(sink - m)
    p = p / denom
    o = jnp.einsum('bnkgqs,bnskd->bnqkgd', p, vv.astype(jnp.float32))
    return o.reshape(B, L, Hq * hd)

def causal_dwconv(u, w, b):
    K = w.shape[0]
    L = u.shape[1]
    up = jnp.pad(u, ((0, 0), (K - 1, 0), (0, 0)))
    out = up[:, 0:L] * w[0]
    for j in range(1, K):
        out = out + up[:, j:j + L] * w[j]
    return out + b

def hybrid_layer(x, mix_norm, w_in, w_alpha2, b_alpha, gla_norm, q_norm, k_norm, sinks,
                 w_out, ffn_norm, w_up, conv_w, conv_b, w_down):
    B, L, _ = x.shape
    dt = x.dtype
    h = rms_norm(x, mix_norm)
    z = h @ w_in
    gq, gk, gv, gr, glr, sq, sk, sv = split_cols(z, SPLITS)

    log_a = jax.nn.log_sigmoid((glr @ w_alpha2 + b_alpha).astype(jnp.float32)) / GLA_TAU
    gq = gq.reshape(B, L, GLA_HEADS, GLA_DK) * (GLA_DK ** -0.5)
    gk = gk.reshape(B, L, GLA_HEADS, GLA_DK)
    gv = gv.reshape(B, L, GLA_HEADS, GLA_DV)
    o_gla = gla_chunked(gq, gk, gv, log_a.reshape(B, L, GLA_HEADS, GLA_DK))
    o_gla = rms_norm(o_gla, gla_norm).reshape(B, L, GLA_V)
    o_gla = (o_gla * jax.nn.silu(gr.astype(jnp.float32))).astype(dt)

    sq = rms_norm(sq.reshape(B, L, SWA_HEADS, SWA_HD), q_norm)
    sk = rms_norm(sk.reshape(B, L, SWA_KV_HEADS, SWA_HD), k_norm)
    sv = sv.reshape(B, L, SWA_KV_HEADS, SWA_HD)
    o_swa = swa_sink_attention(sq, sk, sv, sinks).astype(dt)

    x = x + jnp.concatenate([o_gla, o_swa], axis=-1) @ w_out

    h2 = rms_norm(x, ffn_norm)
    u = causal_dwconv(h2 @ w_up, conv_w, conv_b)
    a, bval = jnp.split(u, 2, axis=-1)
    return x + (jax.nn.silu(a) * bval) @ w_down

def first_inputs(seed: int = 0) -> dict:
    key = jax.random.key(seed)
    ks = jax.random.split(key, 16)
    f = jnp.float32

    def nrm(k, shape, scale):
        return jax.random.normal(k, shape, f) * scale

    return {
        "x": nrm(ks[0], (BATCH, SEQ, D_MODEL), 1.0),
        "mix_norm": 1.0 + nrm(ks[1], (DEPTH, D_MODEL), 0.02),
        "w_in": nrm(ks[2], (DEPTH, D_MODEL, P_IN), D_MODEL ** -0.5),
        "w_alpha2": nrm(ks[3], (DEPTH, GLA_LOWRANK, GLA_Q), GLA_LOWRANK ** -0.5),
        "b_alpha": nrm(ks[4], (DEPTH, GLA_Q), 0.1),
        "gla_norm": 1.0 + nrm(ks[5], (DEPTH, GLA_DV), 0.02),
        "q_norm": 1.0 + nrm(ks[6], (DEPTH, SWA_HD), 0.02),
        "k_norm": 1.0 + nrm(ks[7], (DEPTH, SWA_HD), 0.02),
        "sinks": nrm(ks[8], (DEPTH, SWA_HEADS), 0.5),
        "w_out": nrm(ks[9], (DEPTH, D_MIX, D_MODEL), (2.0 * D_MIX) ** -0.5),
        "ffn_norm": 1.0 + nrm(ks[10], (DEPTH, D_MODEL), 0.02),
        "w_up": nrm(ks[11], (DEPTH, D_MODEL, 2 * D_FF), D_MODEL ** -0.5),
        "conv_w": nrm(ks[12], (DEPTH, CONV_K, 2 * D_FF), CONV_K ** -0.5),
        "conv_b": nrm(ks[13], (DEPTH, 2 * D_FF), 0.02),
        "w_down": nrm(ks[14], (DEPTH, D_FF, D_MODEL), (2.0 * D_FF) ** -0.5),
    }

def first_block(x, mix_norm, w_in, w_alpha2, b_alpha, gla_norm, q_norm, k_norm, sinks,
              w_out, ffn_norm, w_up, conv_w, conv_b, w_down):
    for l in range(DEPTH):
        x = hybrid_layer(x, mix_norm[l], w_in[l], w_alpha2[l], b_alpha[l], gla_norm[l],
                         q_norm[l], k_norm[l], sinks[l], w_out[l], ffn_norm[l], w_up[l],
                         conv_w[l], conv_b[l], w_down[l])
    return x


DEPTH_2 = 2

N_MIXERS = 3
HEAD_DIM = 64
BLOCK = 128
D_FF_2 = 4 * D_MODEL

A_HEADS = D_MODEL // HEAD_DIM
A_GROUPS = ((128, 1, 6), (512, 4, 5), (2048, 16, 5))
B_HEADS = D_MODEL // (2 * HEAD_DIM)
C_HEADS = D_MODEL // HEAD_DIM
C_KV_HEADS = 4
C_GROUP = C_HEADS // C_KV_HEADS
GRID_W = 64
ROPE_THETA = 10000.0
AXIS_ROPE_DIM = HEAD_DIM // 2
NUM_BUCKETS = 32
REL_MAX_DISTANCE = 1024
REL_BIAS_HEADS = A_HEADS


def rms_norm_2(x, g):
    xf = x.astype(jnp.float32)
    y = xf * lax.rsqrt(jnp.mean(xf * xf, axis=-1, keepdims=True) + EPS)
    return (y * g.astype(jnp.float32)).astype(x.dtype)

def t5_bucket(rel):
    nb = NUM_BUCKETS // 2
    max_exact = nb // 2
    side = jnp.where(rel > 0, nb, 0)
    n = jnp.abs(rel)
    nf = jnp.maximum(n, 1).astype(jnp.float32)
    large = max_exact + (jnp.log(nf / max_exact) / math.log(REL_MAX_DISTANCE / max_exact)
                         * (nb - max_exact)).astype(jnp.int32)
    large = jnp.minimum(large, nb - 1)
    return side + jnp.where(n < max_exact, n, large)

def dilated_window_attention(xn, w_qkv, w_o, rel_bias):
    B, S, _ = xn.shape
    nblk = S // BLOCK
    starts = jnp.arange(nblk, dtype=jnp.int32) * BLOCK
    qkv = xn @ w_qkv
    q, k, v = jnp.split(qkv, 3, axis=-1)
    q = q.reshape(B, S, A_HEADS, HEAD_DIM) * (HEAD_DIM ** -0.5)
    k = k.reshape(B, S, A_HEADS, HEAD_DIM)
    v = v.reshape(B, S, A_HEADS, HEAD_DIM)
    outs, glses = [], []
    h0 = 0
    for (win, dil, nh) in A_GROUPS:
        qg, kg, vg = q[:, :, h0:h0 + nh], k[:, :, h0:h0 + nh], v[:, :, h0:h0 + nh]
        n_side = win // (2 * dil)
        offs = jnp.arange(-n_side, n_side + 1, dtype=jnp.int32) * dil
        bias = rel_bias[t5_bucket(offs), h0:h0 + nh].astype(jnp.float32).T
        qb = qg.reshape(B, nblk, BLOCK, nh, HEAD_DIM).transpose(1, 0, 2, 3, 4)

        def block_fn(args, kg=kg, vg=vg, offs=offs, bias=bias):
            q_blk, start = args
            pos = start + jnp.arange(BLOCK, dtype=jnp.int32)[:, None] + offs[None, :]
            valid = (pos >= 0) & (pos < S)
            idx = jnp.clip(pos, 0, S - 1)
            k_sel = kg[:, idx]
            v_sel = vg[:, idx]
            logits = jnp.einsum('bqhd,bqkhd->bhqk', q_blk, k_sel).astype(jnp.float32)
            logits = logits + bias[None, :, None, :]
            logits = jnp.where(valid[None, None], logits, -jnp.inf)
            lse = jax.nn.logsumexp(logits, axis=-1)
            p = jnp.exp(logits - lse[..., None])
            o = jnp.einsum('bhqk,bqkhd->bqhd', p.astype(vg.dtype), v_sel)
            return o, lse

        o, lse = lax.map(block_fn, (qb, starts))
        o = o.transpose(1, 0, 2, 3, 4).reshape(B, S, nh, HEAD_DIM)
        lse = lse.transpose(1, 0, 3, 2).reshape(B, S, nh)
        outs.append(o)
        glses.append(jax.nn.logsumexp(lse, axis=-1) - math.log(nh))
        h0 += nh
    alpha = jax.nn.softmax(jnp.stack(glses, axis=-1), axis=-1)
    n_groups = len(A_GROUPS)
    o = jnp.concatenate(
        [outs[g] * (n_groups * alpha[..., g])[..., None, None].astype(outs[g].dtype)
         for g in range(n_groups)], axis=2)
    return o.reshape(B, S, A_HEADS * HEAD_DIM) @ w_o

def differential_attention(xn, w_qkv, lam, subln_g, w_o, rel_bias, lambda_init):
    B, S, _ = xn.shape
    nblk = S // BLOCK
    starts = jnp.arange(nblk, dtype=jnp.int32) * BLOCK
    qkv = xn @ w_qkv
    q, k, v = jnp.split(qkv, 3, axis=-1)
    q = q.reshape(B, S, B_HEADS, 2, HEAD_DIM) * (HEAD_DIM ** -0.5)
    k = k.reshape(B, S, B_HEADS, 2, HEAD_DIM)
    v = v.reshape(B, S, B_HEADS, 2 * HEAD_DIM)
    lamf = lam.astype(jnp.float32)
    lam_full = (jnp.exp(jnp.sum(lamf[0] * lamf[1])) - jnp.exp(jnp.sum(lamf[2] * lamf[3]))
                + lambda_init)
    keys = jnp.arange(S, dtype=jnp.int32)
    qb = q.reshape(B, nblk, BLOCK, B_HEADS, 2, HEAD_DIM).transpose(1, 0, 2, 3, 4, 5)

    def block_fn(args):
        q_blk, start = args
        rel = keys[None, :] - (start + jnp.arange(BLOCK, dtype=jnp.int32))[:, None]
        bias = rel_bias[t5_bucket(rel)].astype(jnp.float32)
        bias = bias.reshape(BLOCK, S, B_HEADS, 2).transpose(2, 3, 0, 1)
        logits = jnp.einsum('bqhjd,bkhjd->bhjqk', q_blk, k).astype(jnp.float32) + bias[None]
        p = jax.nn.softmax(logits, axis=-1)
        a = p[:, :, 0] - lam_full * p[:, :, 1]
        return jnp.einsum('bhqk,bkhe->bqhe', a.astype(v.dtype), v)

    o = lax.map(block_fn, (qb, starts))
    o = o.transpose(1, 0, 2, 3, 4).reshape(B, S, B_HEADS, 2 * HEAD_DIM)
    o = rms_norm_2(o, subln_g) * (1.0 - lambda_init)
    return o.reshape(B, S, B_HEADS * 2 * HEAD_DIM) @ w_o

def axial_rope_tables(S):
    n_rows = S // GRID_W
    row = jnp.repeat(jnp.arange(n_rows, dtype=jnp.int32), GRID_W).astype(jnp.float32)
    col = jnp.tile(jnp.arange(GRID_W, dtype=jnp.int32), n_rows).astype(jnp.float32)
    half = AXIS_ROPE_DIM // 2
    inv = ROPE_THETA ** (-jnp.arange(half, dtype=jnp.float32) / half)
    ang = jnp.concatenate([row[:, None] * inv, col[:, None] * inv], axis=-1)
    return jnp.cos(ang), jnp.sin(ang)

def apply_axial_rope(x, cos, sin):
    B, S, H, _ = x.shape
    half = AXIS_ROPE_DIM // 2
    xs = x.astype(jnp.float32).reshape(B, S, H, 2, 2, half)
    x1, x2 = xs[..., 0, :], xs[..., 1, :]
    c = cos.reshape(S, 1, 2, half)
    s = sin.reshape(S, 1, 2, half)
    out = jnp.stack([x1 * c - x2 * s, x2 * c + x1 * s], axis=-2)
    return out.reshape(B, S, H, HEAD_DIM).astype(x.dtype)

def axial_gqa_attention(xn, w_qkv, q_norm_g, k_norm_g, w_o, cos, sin):
    B, S, _ = xn.shape
    nblk = S // BLOCK
    qkv = xn @ w_qkv
    q = qkv[..., :C_HEADS * HEAD_DIM].reshape(B, S, C_HEADS, HEAD_DIM)
    k = qkv[..., C_HEADS * HEAD_DIM:(C_HEADS + C_KV_HEADS) * HEAD_DIM].reshape(B, S, C_KV_HEADS, HEAD_DIM)
    v = qkv[..., (C_HEADS + C_KV_HEADS) * HEAD_DIM:].reshape(B, S, C_KV_HEADS, HEAD_DIM)
    q = apply_axial_rope(rms_norm_2(q, q_norm_g), cos, sin) * (HEAD_DIM ** -0.5)
    k = apply_axial_rope(rms_norm_2(k, k_norm_g), cos, sin)
    qb = q.reshape(B, nblk, BLOCK, C_KV_HEADS, C_GROUP, HEAD_DIM).transpose(1, 0, 2, 3, 4, 5)

    def block_fn(q_blk):
        logits = jnp.einsum('bqkgd,bskd->bkgqs', q_blk, k).astype(jnp.float32)
        p = jax.nn.softmax(logits, axis=-1)
        return jnp.einsum('bkgqs,bskd->bqkgd', p.astype(v.dtype), v)

    o = lax.map(block_fn, qb)
    o = o.transpose(1, 0, 2, 3, 4, 5).reshape(B, S, C_HEADS * HEAD_DIM)
    return o @ w_o

def sq_relu_mlp(xn, w_in, w_out):
    h = jax.nn.relu(xn @ w_in)
    return (h * h) @ w_out

def lambda_init_fn(layer_idx):
    return 0.8 - 0.6 * math.exp(-0.3 * layer_idx)

def second_inputs(seed: int = 0) -> dict:
    key = jax.random.key(seed)
    ks = jax.random.split(key, 24)
    n_a = len(range(0, DEPTH_2, N_MIXERS))
    n_b = len(range(1, DEPTH_2, N_MIXERS))
    n_c = len(range(2, DEPTH_2, N_MIXERS))

    def nrm(k, shape, scale):
        return jax.random.normal(k, shape, jnp.float32) * scale

    d_attn = A_HEADS * HEAD_DIM
    c_qkv = (C_HEADS + 2 * C_KV_HEADS) * HEAD_DIM
    return {
        "x": nrm(ks[0], (BATCH, SEQ, D_MODEL), 1.0),
        "rel_bias": nrm(ks[1], (NUM_BUCKETS, REL_BIAS_HEADS), 0.3),
        "norm_mix_g": 1.0 + nrm(ks[2], (DEPTH_2, D_MODEL), 0.02),
        "norm_mlp_g": 1.0 + nrm(ks[3], (DEPTH_2, D_MODEL), 0.02),
        "norm_final_g": 1.0 + nrm(ks[4], (D_MODEL,), 0.02),
        "a_w_qkv": nrm(ks[5], (n_a, D_MODEL, 3 * d_attn), D_MODEL ** -0.5),
        "a_w_o": nrm(ks[6], (n_a, d_attn, D_MODEL), d_attn ** -0.5),
        "b_w_qkv": nrm(ks[7], (n_b, D_MODEL, 3 * d_attn), D_MODEL ** -0.5),
        "b_lambda": nrm(ks[8], (n_b, 4, HEAD_DIM), 0.1),
        "b_subln_g": 1.0 + nrm(ks[9], (n_b, 2 * HEAD_DIM), 0.02),
        "b_w_o": nrm(ks[10], (n_b, d_attn, D_MODEL), d_attn ** -0.5),
        "c_w_qkv": nrm(ks[11], (n_c, D_MODEL, c_qkv), D_MODEL ** -0.5),
        "c_q_norm_g": 1.0 + nrm(ks[12], (n_c, HEAD_DIM), 0.02),
        "c_k_norm_g": 1.0 + nrm(ks[13], (n_c, HEAD_DIM), 0.02),
        "c_w_o": nrm(ks[14], (n_c, C_HEADS * HEAD_DIM, D_MODEL), (C_HEADS * HEAD_DIM) ** -0.5),
        "mlp_w_in": nrm(ks[15], (DEPTH_2, D_MODEL, D_FF_2), D_MODEL ** -0.5),
        "mlp_w_out": nrm(ks[16], (DEPTH_2, D_FF_2, D_MODEL), D_FF_2 ** -0.5),
    }

def second_block(x, rel_bias, norm_mix_g, norm_mlp_g, norm_final_g, a_w_qkv, a_w_o,
              b_w_qkv, b_lambda, b_subln_g, b_w_o, c_w_qkv, c_q_norm_g, c_k_norm_g,
              c_w_o, mlp_w_in, mlp_w_out):
    S = x.shape[1]
    cos, sin = axial_rope_tables(S)
    h = x
    for i in range(DEPTH_2):
        kind, j = i % N_MIXERS, i // N_MIXERS
        hn = rms_norm_2(h, norm_mix_g[i])
        if kind == 0:
            mix = dilated_window_attention(hn, a_w_qkv[j], a_w_o[j], rel_bias)
        elif kind == 1:
            mix = differential_attention(hn, b_w_qkv[j], b_lambda[j], b_subln_g[j], b_w_o[j],
                                         rel_bias, lambda_init_fn(i))
        else:
            mix = axial_gqa_attention(hn, c_w_qkv[j], c_q_norm_g[j], c_k_norm_g[j], c_w_o[j],
                                      cos, sin)
        h = h + mix
        h = h + sq_relu_mlp(rms_norm_2(h, norm_mlp_g[i]), mlp_w_in[i], mlp_w_out[i])
    return rms_norm_2(h, norm_final_g)


def setup_inputs(seed=0):
    out = dict(first_inputs(seed))
    for name, value in second_inputs(seed + 1).items():
        if name != "x":
            out[name + "_2"] = value
    return out


def reference(
    x, mix_norm, w_in, w_alpha2, b_alpha, gla_norm, q_norm, k_norm, sinks, w_out, ffn_norm,
    w_up, conv_w, conv_b, w_down, rel_bias_2, norm_mix_g_2, norm_mlp_g_2, norm_final_g_2,
    a_w_qkv_2, a_w_o_2, b_w_qkv_2, b_lambda_2, b_subln_g_2, b_w_o_2, c_w_qkv_2, c_q_norm_g_2,
    c_k_norm_g_2, c_w_o_2, mlp_w_in_2, mlp_w_out_2,
):
    x = first_block(
        x, mix_norm, w_in, w_alpha2, b_alpha, gla_norm, q_norm, k_norm, sinks, w_out, ffn_norm,
        w_up, conv_w, conv_b, w_down,
    )
    return second_block(
        x, rel_bias_2, norm_mix_g_2, norm_mlp_g_2, norm_final_g_2, a_w_qkv_2, a_w_o_2,
        b_w_qkv_2, b_lambda_2, b_subln_g_2, b_w_o_2, c_w_qkv_2, c_q_norm_g_2, c_k_norm_g_2,
        c_w_o_2, mlp_w_in_2, mlp_w_out_2,
    )


_drawn_inputs = setup_inputs


def setup_inputs(seed=0):
    import zlib

    import numpy as np

    out = dict(_drawn_inputs(seed))
    spreads = {}
    factors = {'mix_norm': 3.506,
     'b_alpha': 3.941,
     'gla_norm': 7.061,
     'q_norm': 8.0,
     'k_norm': 8.0,
     'sinks': 17.351,
     'ffn_norm': 4.826,
     'conv_b': 4.433,
     'norm_mix_g_2': 5.208,
     'norm_final_g_2': 8.303,
     'b_lambda_2': 4.96,
     'b_subln_g_2': 64.0,
     'norm_mlp_g_2': 8.0}
    for name, (base, spread) in spreads.items():
        noise = np.random.default_rng([zlib.crc32(name.encode()), seed]).standard_normal(out[name].shape)
        drawn = base * np.exp(spread * noise) if base else spread * noise
        out[name] = __import__('jax').numpy.asarray(drawn.astype(out[name].dtype))
    for name, factor in factors.items():
        out[name] = (out[name] * factor).astype(out[name].dtype)
    return out
```

```python
import math
from contextlib import ExitStack

import numpy as np
import concourse.bass as bass
from concourse import mybir

F32 = mybir.dt.float32
F32R = mybir.dt.float32r
ALU = mybir.AluOpType
ACT = mybir.ActivationFunctionType

P = 128
S = 512
D = 1024
KD = D // P
NQ = S // P
EPS = 1e-6
NEG = -1e30

FF1 = 2816
NF1 = FF1 // P
FF2 = 4096
NF2 = FF2 // P
PAIRS = 8
CHUNK = 64
NCH = S // CHUNK
GH = 4
WIN = 128
EXT = S + 3 * P

N_IN = 18
N_OUT = KD
CHUNKS1 = [(0, 8), (8, 16), (16, 22)]
T_IN = 0
T_OUT = T_IN + N_IN
T_MLP1 = T_OUT + N_OUT
T_QKV = [0, 0]
T_WO = [0, 0]
T_MLP2 = [0, 0]
_t = T_MLP1 + 2 * NF1 + KD * len(CHUNKS1)
for _l in range(2):
    T_QKV[_l] = _t
    T_WO[_l] = _t + 3 * PAIRS
    T_MLP2[_l] = T_WO[_l] + KD
    _t = T_MLP2[_l] + 2 * NF2
N_TILES = _t
Z_GQ, Z_GK, Z_GV, Z_GR, Z_SK, Z_SV, Z_SQ = 0, 2, 4, 8, 12, 13, 14

_cols = {}
_n = 0
for _name, _w in [("mix_norm", 8), ("ffn_norm", 8), ("mix2a", 8), ("mix2b", 8), ("mlp2a", 8), ("mlp2b", 8),
                  ("final", 8), ("conv_w", 3 * 2 * NF1), ("conv_b", 2 * NF1), ("b_alpha", 2), ("gla_norm", 1),
                  ("q_norm", 1), ("k_norm", 1), ("subln", 1), ("sinks", 8), ("lam", 256), ("w_glr", 8 * 32),
                  ("w_alpha", 256), ("rel_bias", 16)]:
    _cols[_name] = (_n, _n + _w)
    _n += _w
N_PAR = _n
_ccols = {}
_n = 0
for _name, _w in [("ident", P), ("flip", P), ("mean_d", P), ("mean_128", P), ("mean_64", P), ("gla_mask", P), ("reset", S)]:
    _ccols[_name] = (_n, _n + _w)
    _n += _w
N_CON = _n
LAMBDA_INIT = 0.8 - 0.6 * math.exp(-0.3 * 1)


def program(nc, x_in, params, consts, sel, buckets, swa_table, weights, tables, out):
    with ExitStack() as ctx:
        def sb(name, shape, dt=F32):
            return ctx.enter_context(nc.sbuf_tensor(name, shape, dt))

        def sem(name):
            return ctx.enter_context(nc.semaphore(name))

        x = sb("x", [P, KD, S])
        xn_hi = sb("xn_hi", [P, KD, S], F32R)
        xn_lo = sb("xn_lo", [P, KD, S], F32R)
        ff_hi = sb("ff_hi", [P, KD, S], F32R)
        ff_lo = sb("ff_lo", [P, KD, S], F32R)
        stage = sb("stage", [P, 2, KD, P])
        w_hi = sb("w_hi", [P, 2, KD, P], F32R)
        w_lo = sb("w_lo", [P, 2, KD, P], F32R)
        z = sb("z", [P, N_IN, S])
        par = sb("par", [P, N_PAR])
        con = sb("con", [P, N_CON])
        bias = sb("bias", [P, 2, 2, EXT])
        qkv = sb("qkv", [P, 2, 3, S])
        v_tok = sb("v_tok", [P, 2, 2, NQ, P])
        prob = sb("prob", [P, 2, 2, S])
        tmp = sb("tmp", [P, 4, S])
        rstd = sb("rstd", [P, S])
        mx = sb("mx", [P, 2, 8])
        nm = sb("nm", [P, 2, 8])
        sm = sb("sm", [P, 2, 8])
        rc = sb("rc", [P, 2, 8])
        es = sb("es", [P, 2, 8])
        lse_nm = sb("lse_nm", [P, PAIRS, 8])
        lse_sm = sb("lse_sm", [P, PAIRS, 8])
        small = sb("small", [P, 128])
        glr_w = sb("glr_w", [P, 2, KD * 32], F32R)

        oT = z[:, 0:KD, :]
        pT = z[:, KD:2 * KD, :].rearrange("p (h k) s -> p h k s", h=2)

        banks = [ctx.enter_context(nc.psum_tensor(f"bank{i}", [P, S], F32)) for i in range(8)]
        G = banks[0:2]
        SC = banks[2:4]
        TR = banks[4:6]
        OB = banks[6]
        MB = banks[7]

        def pcol(name, a=0, b=None):
            s, e = _cols[name]
            return par[:, s + a:(e if b is None else s + b)]

        def ccol(name):
            s, e = _ccols[name]
            return con[:, s:e]

        ident = ccol("ident")

        loaded = sem("loaded")
        stage_full = [sem(f"stage_full{i}") for i in range(2)]
        hi_ready = sem("hi_ready")
        lo_ready = sem("lo_ready")
        hi_free = sem("hi_free")
        tile_done = sem("tile_done")
        evac = [sem(f"evac{i}") for i in range(2)]
        sq_ready, ss_done, rstd_ready = sem("sq_ready"), sem("ss_done"), sem("rstd_ready")
        sq_used = sem("sq_used")
        glr_split = sem("glr_split")
        glr_done, glr_read, gate_in = sem("glr_done"), sem("glr_read"), sem("gate_in")
        gate_abs, gate_log = sem("gate_abs"), sem("gate_log")
        decay_sum, decay_exp, decay_diff, key_exp = sem("decay_sum"), sem("decay_exp"), sem("decay_diff"), sem("key_exp")
        gla_keys = sem("gla_keys")
        turned_in, turned_out = sem("turned_in"), sem("turned_out")
        state_in, state_out = sem("state_in"), sem("state_out")
        gla_a, gla_masked, gla_o, gla_sq, gla_ss = sem("gla_a"), sem("gla_masked"), sem("gla_o"), sem("gla_sq"), sem("gla_ss")
        gla_r, swn_r, post_r = sem("gla_r"), sem("swn_r"), sem("post_r")
        gla_t, gla_hi, gla_lo = sem("gla_t"), sem("gla_hi"), sem("gla_lo")
        gates_on = sem("gates_on")
        swn_sq, swn_ss, swn_done = sem("swn_sq"), sem("swn_ss"), sem("swn_done")
        swv_t, swv_done = sem("swv_t"), sem("swv_done")
        swa_hi, swa_lo = sem("swa_hi"), sem("swa_lo")
        conv_0, conv_1, silu_done, f_made = sem("conv_0"), sem("conv_1"), sem("silu_done"), sem("f_made")
        ffh_ready, ff_ready = sem("ffh_ready"), sem("ff_ready")
        tab_mm, tab_sb, tables_saved = sem("tab_mm"), sem("tab_sb"), sem("tables_saved")
        lam_sum, lam_exp, lam_done = sem("lam_sum"), sem("lam_exp"), sem("lam_done")
        grp_d, grp_a, grp_t, grp_row = sem("grp_d"), sem("grp_a"), sem("grp_t"), sem("grp_row")
        post_sq, post_mm, post_t, post_hi, post_lo = (sem("post_sq"), sem("post_mm"), sem("post_t"),
                                                      sem("post_hi"), sem("post_lo"))
        final_ready = sem("final_ready")
        sel_in = sem("sel_in")
        squared = sem("squared")
        t_ready, xh_ready, xn_ready = sem("t_ready"), sem("xh_ready"), sem("xn_ready")
        x_ready = sem("x_ready")
        zero_done = sem("zero_done")
        chains = {"dve": sem("dve_chain"), "act": sem("act_chain"), "pe": sem("pe_chain")}
        bias_in = [sem(f"bias_in{i}") for i in range(2)]
        out_sent = sem("out_sent")

        at = {"dve": 0, "act": 0, "pe": 0}

        def link(key, eng, ins):
            at[key] += 1
            ins.then_inc(chains[key], 1)
            eng.wait_ge(chains[key], at[key])

        class Core:
            def __init__(self, n, pairs_out, ranges):
                self.n = n
                self.lse_kept = sem(f"{n}_lse")
                self.vt_done = sem(f"{n}_vt")
                self.v_ready = sem(f"{n}_v")
                self.scored = sem(f"{n}_scored")
                self.maxed = sem(f"{n}_maxed")
                self.negated = sem(f"{n}_negated")
                self.expd = sem(f"{n}_expd")
                self.summed = sem(f"{n}_summed")
                self.recd = sem(f"{n}_recd")
                self.scaled = sem(f"{n}_scaled")
                self.turned = sem(f"{n}_turned")
                self.copied = sem(f"{n}_copied")
                self.o_done = sem(f"{n}_o")
                self.o_read = swa_lo if n == "swa" else sem(f"{n}_oread")
                self.parity = (lambda q_, p: p % 2) if n == "swa" else (lambda q_, p: q_)
                self.halves_out = pairs_out
                self.ranges = ranges

        def qkv_tile(l, p, u, j):
            i = 3 * u + j
            if isinstance(p, int):
                return T_QKV[l] // 2 + (3 * p + j) // 2, i % 2
            return T_QKV[l] // 2 + 3 * p[0] + i // 2, i % 2

        full = [(0, NQ)] * NQ
        swa = Core("swa", 2, [(max(0, n - 1), n + 1) for n in range(NQ)])
        att = [Core("dil", 2, full), Core("dif", 1, full)]

        block = ctx.enter_context(nc.Block())


        flat_bias = bias[:].rearrange("p a b c -> p (a b c)")
        kd_tok = flat_bias[:, 0:2 * S].rearrange("p (j t f) -> p j t f", j=2, t=NQ)
        gv_tok = flat_bias[:, 2 * S:6 * S].rearrange("p (t h f) -> p t h f", t=NQ, h=GH)
        state = prob[:].rearrange("p a b s -> p (a b s)").rearrange("p (j c f) -> p j c f", j=2, c=NCH)
        bucket = flat_bias[0:32, 0:2 * 1024]
        table_sb = prob[0:16].rearrange("p a b s -> p a (b s)")
        swa_pT = qkv[:, 0:2, 0:2, :]
        eps_col = small[:, 96:97]
        decay = small[:, 0:16].rearrange("p (j c) -> p j c", j=2)
        lam_s, neg_lam = small[:, 16:20], small[:, 20:21]
        lh = small[:, 24:88].rearrange("p (n h) -> p n h", n=NQ)
        grp = sb("grp", [P, 6, NQ, 3])
        lhe = sb("lhe", [P, 2, NQ, 16])
        selector = z[0:3, 16:18].rearrange("p a s -> p (a s)")
        GROUPS = [(0, 6), (6, 11), (11, 16)]

        def toeplitz(table, p):
            return bass.AP(tensor=table.tensor, offset=2 * p * 1024, ap=[[1, P], [1024, 2], [1, EXT]])

        @block.sync
        def _(sp):
            def load(m, p_, first=False):
                if not first:
                    sp.wait_ge(lo_ready, 2 * m + p_ - 1)
                if isinstance(m, int):
                    src = weights[2 * m + p_]
                else:
                    src = weights[bass.ds(2 * m + p_, 1)].rearrange("o p c -> (o p) c")
                sp.dma_start(stage[:, p_].rearrange("p k c -> p (k c)"), src).then_inc(stage_full[p_], 16)

            def loads(t0, t1):
                with sp.Fori(t0 // 2, t1 // 2) as m:
                    for p_ in range(2):
                        load(m, p_)

            def bias_load(core, table, p, q_, used):
                if used is not None:
                    sp.wait_ge(core.maxed, used)
                if core is swa:
                    sp.dma_start(bias[:, q_, :, 2 * P:4 * P], table[p]).then_inc(bias_in[q_], 16)
                else:
                    sp.dma_start(bias[:, q_], toeplitz(table, p)).then_inc(bias_in[q_], 16)

            sp.dma_start(par[:], params).then_inc(loaded, 16)
            sp.dma_start(x[:], x_in).then_inc(loaded, 16)
            load(0, 0, True)
            load(0, 1, True)
            sp.dma_start(con[:], consts).then_inc(loaded, 16)
            sp.dma_start(bucket, buckets).then_inc(loaded, 16)
            loads(2, T_OUT + 2)
            sp.wait_ge(gla_lo, GH)
            for p in range(4):
                bias_load(swa, swa_table, p, p % 2, 8 * (p - 1) if p >= 2 else None)
            sp.wait_ge(swa.maxed, 8 * 4)
            sp.dma_start(selector, sel).then_inc(sel_in, 16)
            loads(T_OUT + 2, T_QKV[0])
            sp.wait_ge(tables_saved, 32)
            for l in range(2):
                core, before = att[l], (swa if l == 0 else att[0])
                sp.wait_ge(before.maxed, 8 * (4 if l == 0 else PAIRS))
                for p in range(2):
                    bias_load(core, tables[l], p, p, None)
                loads(T_QKV[l], T_QKV[l] + 6)
                with sp.Fori(1, 4) as i:
                    for u in range(2):
                        for j in range(3 * u, 3 * u + 3):
                            if j == 3 * u + 2:
                                bias_load(core, tables[l], 2 * i + u, u, 16 * i + 8 * u - 8)
                            load(T_QKV[l] // 2 + 3 * i + j // 2, j % 2)
                loads(T_WO[l], T_QKV[1] if l == 0 else N_TILES)
            sp.wait_ge(final_ready, KD)
            sp.dma_start(out, z[:, 0:KD, :]).then_inc(out_sent, 16)
            sp.wait_ge(out_sent, 16)

        @block.gpsimd
        def _(pool):
            def split_lo(m, p_, first=False):
                pool.wait_ge(hi_ready, 2 * m + p_ + 1)
                if not first:
                    pool.wait_ge(tile_done, 2 * m + p_ - 1)
                nc.gpsimd.tensor_tensor(w_lo[:, p_], stage[:, p_], w_hi[:, p_].bitcast(F32),
                                        ALU.subtract).then_inc(lo_ready, 1)
            split_lo(0, 0, True)
            split_lo(0, 1, True)
            with pool.Fori(1, N_TILES // 2) as m:
                for p_ in range(2):
                    split_lo(m, p_)

        @block.tensor
        def _(pe):
            def tile(m, p_, hi, lo, nk=KD, ready=None, late=None):
                pe.wait_ge(hi_ready, 2 * m + p_ + 1)
                if not (isinstance(m, int) and m == 0):
                    pe.wait_ge(evac[p_], m)
                if late is not None:
                    pe.wait_ge(late[0], late[1] - 1)
                for k in range(nk):
                    if ready is not None:
                        pe.wait_ge(ready[0], ready[1] + k + 1)
                    if late is not None and k == nk - 1:
                        pe.wait_ge(*late)
                    pe.matmul(G[p_][:], w_hi[:, p_, k], hi[:, k], start=(k == 0), stop=False)
                    mm = pe.matmul(G[p_][:], w_hi[:, p_, k], lo[:, k], start=False, stop=False)
                mm.then_inc(hi_free, 1)
                pe.wait_ge(lo_ready, 2 * m + p_ + 1)
                for k in range(nk):
                    mm = pe.matmul(G[p_][:], w_lo[:, p_, k], hi[:, k], start=False, stop=(k == nk - 1))
                mm.then_inc(tile_done, 1)

            def tiles(t0, t1, hi, lo, nk=KD, ready=None):
                if ready is not None:
                    tile(t0 // 2, 0, hi, lo, nk, ready)
                    tile(t0 // 2, 1, hi, lo, nk)
                    t0 += 2
                with pe.Fori(t0 // 2, t1 // 2) as m:
                    for p_ in range(2):
                        tile(m, p_, hi, lo, nk)

            def norm(n):
                for k in range(KD):
                    pe.wait_ge(sq_ready, KD * n + k + 1)
                    pe.matmul(MB[:], ccol("mean_d"), tmp[:, k % 2], start=(k == 0), stop=(k == KD - 1)).then_inc(sq_used, 1)

            def scores(c, p, q_, n, qT, kT):
                a, b = c.ranges[n]
                for h in range(2):
                    r = slice(64 * h, 64 * h + 64)
                    if not (isinstance(p, int) and p == 0 and n == 0):
                        pe.wait_ge(c.maxed, 8 * p + 2 * n + h - 1)
                    pe.matmul(SC[h][:, 0:(b - a) * P], qT[r, n * P:(n + 1) * P], kT[r, a * P:b * P],
                              start=True, stop=True).then_inc(c.scored, 1)

            def turn(c, p, n):
                a, b = c.ranges[n]
                for h in range(c.halves_out):
                    i = c.halves_out * n + h
                    pe.wait_ge(c.scaled, 4 * c.halves_out * p + i + 1)
                    if not (isinstance(p, int) and p == 0 and i < 2):
                        pe.wait_ge(c.copied, 4 * c.halves_out * p + i - 1)
                    for j in range(b - a):
                        mm = pe.transpose(TR[i % 2][:, j * P:(j + 1) * P], prob[:, n % 2, h, j * P:(j + 1) * P],
                                          ident if c is swa else ccol("flip"))
                    mm.then_inc(c.turned, 1)

            def values(c, p, v, pt):
                pe.wait_ge(c.copied, 4 * c.halves_out * (p + 1))
                if not (isinstance(p, int) and p == 0):
                    pe.wait_ge(c.o_read, p)
                hs = range(c.halves_out)
                if c is swa:
                    for n in range(NQ):
                        a, b = c.ranges[n]
                        cols = slice(n * P, (n + 1) * P)
                        for h in hs:
                            for j in range(b - a):
                                mm = pe.matmul(OB[:, cols], v[:, h, a + j], pt[:, h, j, cols],
                                               start=(h == 0 and j == 0), stop=(h == 1 and j == b - a - 1))
                else:
                    for h in hs:
                        for k in range(NQ):
                            mm = pe.matmul(OB[:], v[:, h, k], pt[:, h, k], start=(h == 0 and k == 0),
                                           stop=(h == len(hs) - 1 and k == NQ - 1))
                mm.then_inc(c.o_done, 1)

            pe.wait_ge(loaded, 64)
            norm(0)
            for b in range(2):
                mm = pe.matmul(SC[b][0:16], pcol("rel_bias")[0:32], bucket[:, b * S:(b + 1) * S], start=True, stop=True)
            mm.then_inc(tab_mm, 1)
            tiles(T_IN, T_OUT, xn_hi, xn_lo, ready=(xn_ready, 0))

            pe.wait_ge(glr_split, 2)
            n_mm = 0
            for w, mv in ((0, xn_hi), (0, xn_lo), (1, xn_hi)):
                for k in range(KD):
                    mm = pe.matmul(MB[0:32], glr_w[:, w, k * 32:(k + 1) * 32], mv[:, k], start=(n_mm == 0), stop=(n_mm == 23))
                    n_mm += 1
            mm.then_inc(glr_done, 1)
            pe.wait_ge(glr_read, 1)
            for j in range(2):
                mm = pe.matmul(TR[j][:], pcol("w_alpha")[0:16, j * P:(j + 1) * P], tmp[0:16, 0], start=True, stop=True)
            mm.then_inc(gate_in, 1)

            for h in range(GH + 2):
                bank = (OB, MB)[h % 2]
                if h >= 2:
                    pe.wait_ge(turned_out, h - 1)
                if h == GH:
                    pe.wait_ge(gla_keys, 6)
                if h < GH:
                    pe.wait_ge(evac[h % 2], (Z_GV + h) // 2 + 1)
                src = z[:, Z_GV + h] if h < GH else qkv[:, h - GH, 2]
                for t in range(NQ):
                    mm = pe.transpose(bank[:, t * P:(t + 1) * P], src[:, t * P:(t + 1) * P], ident)
                mm.then_inc(turned_in, 1)
            for j in range(2):
                for c in range(NCH - 1):
                    r = slice(64 * (c % 2), 64 * (c % 2) + 64)
                    i = (NCH - 1) * j + c
                    if i == 0:
                        pe.wait_ge(turned_out, GH + 2)
                    if j and c < 2:
                        pe.wait_ge(gla_r, c + 1)
                    if c >= 2 or j:
                        pe.wait_ge(state_out, 2 * (i - 1) if c != 0 else 2 * i)
                    pe.matmul(SC[c % 2][:, 0:256], kd_tok[r, j, c // 2], gv_tok[r, c // 2, 2 * j:2 * j + 2],
                              start=True, stop=True).then_inc(state_in, 1)
                for h in range(2):
                    r = slice(64 * h, 64 * h + 64)
                    if j:
                        pe.wait_ge(gla_masked, h + 1)
                    for t in range(NQ):
                        cols = slice(t * P, (t + 1) * P)
                        mm = pe.matmul(TR[h][:, cols], qkv[r, j, 1, cols], z[r, Z_GQ + j, cols], start=True, stop=True)
                    mm.then_inc(gla_a, 1)
                for h in range(2):
                    r = slice(64 * h, 64 * h + 64)
                    bank = (OB, MB)[h]
                    pe.wait_ge(gla_masked, 2 * j + h + 1)
                    if h == 0:
                        pe.wait_ge(state_out, 2 * (NCH - 1) * (j + 1))
                    if j:
                        pe.wait_ge(gla_t, 2 * (j - 1) + h + 1)
                    for t in range(NQ):
                        pe.matmul(bank[:, t * P:(t + 1) * P], gv_tok[:, t, 2 * j + h], tmp[:, h, t * P:(t + 1) * P],
                                  start=True, stop=False)
                        for c in (2 * t, 2 * t + 1):
                            cols = slice(c * CHUNK, (c + 1) * CHUNK)
                            mm = pe.matmul(bank[:, cols], state[r, j, c], z[r, Z_GQ + j, cols], start=False,
                                           stop=(c == 2 * t + 1))
                    mm.then_inc(gla_o, 1)
                for h in range(2):
                    pe.wait_ge(gla_sq, 2 * j + h + 1)
                    pe.matmul(SC[h][:], ccol("mean_128"), tmp[:, 2], start=True, stop=True).then_inc(gla_ss, 1)

            for i in range(5):
                pe.wait_ge(swn_sq, i + 1)
                if i >= 2:
                    pe.wait_ge(swn_done, i - 1)
                if i == 0:
                    pe.wait_ge(gla_lo, GH)
                pe.matmul(SC[i % 2][:], ccol("mean_64"), tmp[:, i % 2], start=True, stop=True).then_inc(swn_ss, 1)
            for t in range(NQ):
                mm = pe.transpose(MB[:, t * P:(t + 1) * P], z[:, Z_SV, t * P:(t + 1) * P], ident)
            mm.then_inc(swv_t, 1)
            pe.wait_ge(swn_done, 5)
            pe.wait_ge(swv_done, 1)
            for p in range(4):
                q = z[:, Z_SQ + p]
                scores(swa, p, 0, 0, q, z[:, Z_SK])
                scores(swa, p, 0, 1, q, z[:, Z_SK])
                turn(swa, p, 0)
                scores(swa, p, 0, 2, q, z[:, Z_SK])
                turn(swa, p, 1)
                scores(swa, p, 0, 3, q, z[:, Z_SK])
                turn(swa, p, 2)
                turn(swa, p, 3)
                values(swa, p, v_tok[:, 0], swa_pT)
            pe.wait_ge(swa_lo, 4)
            tiles(T_OUT, T_MLP1, ff_hi, ff_lo)

            norm(1)
            t = T_MLP1
            for n, (a, b) in enumerate(CHUNKS1):
                tiles(t, t + 2 * (b - a), xn_hi, xn_lo, ready=(xn_ready, KD) if n == 0 else None)
                t += 2 * (b - a)
                with pe.Fori(t // 2, t // 2 + KD // 2) as m:
                    for p_ in range(2):
                        tile(m, p_, ff_hi, ff_lo, b - a, late=(ff_ready, b))
                t += KD

            for l in range(2):
                c = att[l]
                norm(2 + 2 * l)
                def proj(p, u, j):
                    first = isinstance(p, int) and p == 0 and j == 0
                    tile(*qkv_tile(l, p, u, j), xn_hi, xn_lo, ready=(xn_ready, KD * (2 + 2 * l)) if first else None)

                def v_turn(p, u, at_p):
                    m, p_ = qkv_tile(l, at_p, u, 2)
                    pe.wait_ge(evac[p_], m + 1)
                    if not (isinstance(p, int) and p == 0):
                        pe.wait_ge(c.v_ready, p)
                    for t in range(NQ):
                        mm = pe.transpose(MB[:, t * P:(t + 1) * P], qkv[:, u, 2, t * P:(t + 1) * P], ident)
                    mm.then_inc(c.vt_done, 1)

                def pair(p, u, nxt):
                    q, k = qkv[:, u, 0], qkv[:, u, 1]
                    scores(c, p, u, 0, q, k)
                    if nxt is not None:
                        proj(nxt, 1 - u, 0)
                    turn(c, p, 0)
                    scores(c, p, u, 1, q, k)
                    if nxt is not None:
                        proj(nxt, 1 - u, 1)
                    turn(c, p, 1)
                    scores(c, p, u, 2, q, k)
                    scores(c, p, u, 3, q, k)
                    if nxt is not None:
                        proj(nxt, 1 - u, 2)
                    turn(c, p, 2)
                    turn(c, p, 3)
                    pe.wait_ge(c.v_ready, p + 1)
                    values(c, p, v_tok[:, u], pT)
                    if nxt is not None:
                        v_turn(p + 1, 1 - u, nxt)

                for j in range(3):
                    proj(0, 0, j)
                v_turn(0, 0, 0)
                pair(0, 0, 1)
                with pe.Fori(0, 3) as i:
                    pair(2 * i + 1, 1, (i + 1,))
                    pair(2 * i + 2, 0, (i + 1,))
                pair(7, 1, None)

                if l == 0:
                    pe.wait_ge(grp_d, 8)
                    for n in range(NQ):
                        mm = pe.transpose(MB[0:3, n * P:(n + 1) * P], grp[:, 5, n, :], ccol("flip"))
                    mm.then_inc(grp_t, 1)
                    pe.wait_ge(grp_row, 1)
                    pe.wait_ge(sel_in, 16)
                for p in range(PAIRS):
                    i = PAIRS * l + p
                    if p >= 2:
                        pe.wait_ge(post_t, i - 1)
                    if l == 0:
                        pe.matmul(SC[p % 2][:], selector[:, p * P:(p + 1) * P], tmp[0:3, 3], start=True,
                                  stop=True).then_inc(post_mm, 1)
                    else:
                        pe.wait_ge(post_sq, p + 1)
                        pe.matmul(SC[p % 2][:], ccol("mean_128"), tmp[:, 2 + p % 2], start=True,
                                  stop=True).then_inc(post_mm, 1)
                tiles(T_WO[l], T_MLP2[l], ff_hi, ff_lo, ready=(post_lo, PAIRS * l))
                norm(3 + 2 * l)
                for n in range(NF2 // KD):
                    t = T_MLP2[l] + 2 * KD * n
                    tiles(t, t + KD, xn_hi, xn_lo, ready=(xn_ready, KD * (3 + 2 * l)) if n == 0 else None)
                    with pe.Fori((t + KD) // 2, (t + 2 * KD) // 2) as m:
                        for p_ in range(2):
                            tile(m, p_, ff_hi, ff_lo, late=(ff_ready, NF1 + NF2 * l + KD * (n + 1)))
            norm(6)

        @block.scalar
        def _(act):
            def split_hi(m, p_, first=False):
                act.wait_ge(stage_full[p_], 16 * (m + 1))
                if not first:
                    act.wait_ge(hi_free, 2 * m + p_ - 1)
                act.activation(w_hi[:, p_], stage[:, p_], ACT.Copy).then_inc(hi_ready, 1)

            def splits(t0, t1):
                with act.Fori(t0 // 2, t1 // 2) as m:
                    for p_ in range(2):
                        split_hi(m + 1, p_)

            def rsqrt(bank, done):
                link("act", act, act.activation(rstd[:], bank[:], ACT.Ln, bias=eps_col))
                act.activation(rstd[:], rstd[:], ACT.Exp, scale=-0.5).then_inc(done, 1)

            def norm(n, t=None):
                if n == 0:
                    act.wait_ge(loaded, 64)
                    act.wait_ge(squared, 2)
                else:
                    for p_ in range(2):
                        act.wait_ge(evac[p_], t // 2)
                for k in range(KD):
                    if k >= 2:
                        act.wait_ge(sq_used, KD * n + k - 1)
                    act.activation(tmp[:, k % 2], x[:, k], ACT.Square).then_inc(sq_ready, 1)
                act.wait_ge(sq_used, KD * (n + 1))
                rsqrt(MB, rstd_ready)
                if n == 6:
                    return
                for k in range(KD):
                    act.wait_ge(t_ready, KD * n + k + 1)
                    act.activation(xn_hi[:, k], tmp[:, 2 + k % 2], ACT.Copy).then_inc(xh_ready, 1)

            def exps(c, p, q_, n, sink=None):
                a, b = c.ranges[n]
                for h in range(2):
                    s = 2 * n + h
                    act.wait_ge(c.negated, 8 * p + s + 1)
                    if sink is not None:
                        act.activation(es[:, q_, s:s + 1], nm[:, q_, s:s + 1], ACT.Exp, bias=sink(h))
                    pr = prob[:, n % 2, h, 0:(b - a) * P]
                    act.activation(pr, pr, ACT.Exp, bias=nm[:, q_, s:s + 1],
                                   accum_out=sm[:, q_, s:s + 1]).then_inc(c.expd, 1)

            def copies(c, p, n, pt):
                a, b = c.ranges[n]
                for h in range(c.halves_out):
                    i = c.halves_out * n + h
                    act.wait_ge(c.turned, 4 * c.halves_out * p + i + 1)
                    if i == 0 and not (isinstance(p, int) and p == 0):
                        act.wait_ge(c.o_done, p)
                    act.activation(pt[:, h, 0:b - a, n * P:(n + 1) * P],
                                   TR[i % 2][:, 0:(b - a) * P].rearrange("p (k s) -> p k s", k=b - a),
                                   ACT.Copy).then_inc(c.copied, 1)

            act.wait_ge(loaded, 16)
            split_hi(0, 0, True)
            split_hi(0, 1, True)
            norm(0)
            act.activation(glr_w[:, 0], pcol("w_glr"), ACT.Copy).then_inc(glr_split, 1)
            act.wait_ge(tab_sb, 2)
            for l in range(2):
                act.dma_start(tables[l], table_sb[:, l, :]).then_inc(tables_saved, 16)
            with act.Fori(0, N_IN // 2) as m:
                for p_ in range(2):
                    split_hi(m + 1, p_)
                    act.wait_ge(tile_done, 2 * m + p_ + 1)
                    act.activation(z[:, bass.ds(2 * m + p_, 1)].rearrange("p o s -> p (o s)"), G[p_][:],
                                   ACT.Copy).then_inc(evac[p_], 1)
            act.wait_ge(lam_sum, 1)
            act.activation(lam_s[:, 2:4], lam_s[:, 0:2], ACT.Exp).then_inc(lam_exp, 1)
            for j in range(2):
                act.wait_ge(gate_abs, j + 1)
                link("act", act, act.activation(qkv[:, j, 1], TR[j][:], ACT.Abs, bias=pcol("b_alpha", j, j + 1)))
                link("act", act, act.activation(qkv[:, j, 1], qkv[:, j, 1], ACT.Exp, scale=-1.0))
                act.activation(qkv[:, j, 1], qkv[:, j, 1], ACT.Ln, bias=1.0).then_inc(gate_log, 1)
            for j in range(2):
                act.wait_ge(decay_sum, j + 1)
                last = qkv[:, j, 0].rearrange("p (c t) -> p c t", t=CHUNK)[:, :, CHUNK - 1]
                act.activation(decay[:, j], last, ACT.Exp, scale=1.0 / 16)
                act.activation(qkv[:, j, 1], qkv[:, j, 0], ACT.Exp, scale=-1.0 / 16)
                act.activation(tmp[:, 2 + j], qkv[:, j, 0], ACT.Exp, scale=1.0 / 16).then_inc(decay_exp, 1)
                act.wait_ge(decay_diff, j + 1)
                act.activation(qkv[:, j, 2], qkv[:, j, 2], ACT.Exp, scale=1.0 / 16).then_inc(key_exp, 1)
            for h in range(GH):
                act.activation(z[:, Z_GR + h], z[:, Z_GR + h], ACT.Silu).then_inc(gates_on, 1)
            for j in range(2):
                for h in range(2):
                    act.wait_ge(gla_o, 2 * j + h + 1)
                    if h or j:
                        act.wait_ge(gla_ss, 2 * j + h)
                    act.activation(tmp[:, 2], (OB, MB)[h][:], ACT.Square).then_inc(gla_sq, 1)
                    act.wait_ge(gla_ss, 2 * j + h + 1)
                    rsqrt(SC[h], gla_r)
                    act.wait_ge(gla_t, 2 * j + h + 1)
                    act.activation(ff_hi[:, 2 * j + h], tmp[:, 3], ACT.Copy).then_inc(gla_hi, 1)
            act.wait_ge(gla_lo, GH)
            def swa_square(i):
                src = z[:, Z_SK] if i == 0 else z[:, Z_SQ + i - 1]
                act.activation(tmp[:, i % 2], src, ACT.Square).then_inc(swn_sq, 1)
            swa_square(0)
            for i in range(5):
                if i < 4:
                    if i:
                        act.wait_ge(swn_ss, i)
                    swa_square(i + 1)
                act.wait_ge(swn_ss, i + 1)
                if i:
                    act.wait_ge(swn_done, i)
                rsqrt(SC[i % 2], swn_r)
            for p in range(4):
                def sink(h, p=p):
                    return pcol("sinks", 2 * p + h, 2 * p + h + 1)
                exps(swa, p, 0, 0, sink)
                exps(swa, p, 0, 1, sink)
                copies(swa, p, 0, swa_pT)
                exps(swa, p, 0, 2, sink)
                copies(swa, p, 1, swa_pT)
                exps(swa, p, 0, 3, sink)
                copies(swa, p, 2, swa_pT)
                copies(swa, p, 3, swa_pT)
                act.wait_ge(swa.o_done, p + 1)
                act.activation(ff_hi[:, GH + p], OB[:], ACT.Copy).then_inc(swa_hi, 1)
            splits(T_OUT, T_MLP1)

            norm(1, T_MLP1)
            t = T_MLP1
            for a, b in CHUNKS1:
                with act.Fori(0, b - a) as i:
                    f, m = i + a, i + t // 2
                    for p_ in range(2):
                        split_hi(m + 1, p_)
                        act.wait_ge(tile_done, 2 * m + p_ + 1)
                        if p_ == 0:
                            act.wait_ge(ff_ready, f)
                        w2 = par[:, bass.ds(_cols["conv_w"][0] + 4 * NF1 + 2 * f + p_, 1)]
                        bc = par[:, bass.ds(_cols["conv_b"][0] + 2 * f + p_, 1)]
                        act.activation(tmp[:, p_], G[p_][:], ACT.Identity, bias=bc, scale=w2).then_inc(conv_0, 1)
                    act.wait_ge(evac[0], m + 1)
                    act.activation(tmp[:, 2], tmp[:, 0], ACT.Silu).then_inc(silu_done, 1)
                    act.wait_ge(f_made, f + 1)
                    act.activation(ff_hi[:, bass.ds(i, 1)].rearrange("p o s -> p (o s)"), tmp[:, 3],
                                   ACT.Copy).then_inc(ffh_ready, 1)
                t += 2 * (b - a)
                splits(t, t + KD)
                t += KD

            for l in range(2):
                c = att[l]
                norm(2 + 2 * l, T_QKV[l])
                def proj(p, u, j):
                    m, p_ = qkv_tile(l, p, u, j)
                    split_hi(m + 1, p_)
                    act.wait_ge(tile_done, 2 * m + p_ + 1)
                    dst = qkv[:, u, j].rearrange("p (n s) -> p n s", n=NQ)
                    if j == 0:
                        dst = dst[:, :, ::-1]
                    act.activation(dst, G[p_][:].rearrange("p (n s) -> p n s", n=NQ), ACT.Copy,
                                   scale=(0.125 if j == 0 else 1.0)).then_inc(evac[p_], 1)

                def pair(p, u, nxt):
                    exps(c, p, u, 0)
                    if nxt is not None:
                        proj(nxt, 1 - u, 0)
                    copies(c, p, 0, pT)
                    exps(c, p, u, 1)
                    if nxt is not None:
                        proj(nxt, 1 - u, 1)
                    copies(c, p, 1, pT)
                    exps(c, p, u, 2)
                    exps(c, p, u, 3)
                    if nxt is not None:
                        proj(nxt, 1 - u, 2)
                    copies(c, p, 2, pT)
                    copies(c, p, 3, pT)

                for j in range(3):
                    proj(0, 0, j)
                pair(0, 0, 1)
                with act.Fori(0, 3) as i:
                    pair(2 * i + 1, 1, (i + 1,))
                    pair(2 * i + 2, 0, (i + 1,))
                pair(7, 1, None)
                if l == 0:
                    act.wait_ge(c.lse_kept, 2 * PAIRS)
                    act.activation(lse_sm[:], lse_sm[:], ACT.Ln).then_inc(grp_a, 1)
                    act.wait_ge(grp_d, 3)
                    act.activation(lhe[:, 1], lhe[:, 1], ACT.Exp).then_inc(grp_a, 1)
                    act.wait_ge(grp_d, 4)
                    act.activation(grp[:, 1], grp[:, 1], ACT.Ln).then_inc(grp_a, 1)
                    act.wait_ge(grp_d, 6)
                    act.activation(grp[:, 2], grp[:, 2], ACT.Exp).then_inc(grp_a, 1)
                else:
                    act.wait_ge(c.o_read, PAIRS)
                for p in range(PAIRS):
                    i = PAIRS * l + p
                    if l == 1:
                        if p == 0:
                            act.activation(tmp[:, 2], oT[:, 0], ACT.Square).then_inc(post_sq, 1)
                        if p < PAIRS - 1:
                            if p >= 1:
                                act.wait_ge(post_mm, i)
                            act.activation(tmp[:, 2 + (p + 1) % 2], oT[:, p + 1], ACT.Square).then_inc(post_sq, 1)
                        act.wait_ge(post_mm, i + 1)
                        if p:
                            act.wait_ge(post_t, i)
                        rsqrt(SC[p % 2], post_r)
                    act.wait_ge(post_t, i + 1)
                    act.activation(ff_hi[:, p], tmp[:, p % 2], ACT.Copy).then_inc(post_hi, 1)
                splits(T_WO[l], T_MLP2[l])
                norm(3 + 2 * l, T_MLP2[l])
                for n in range(NF2 // KD):
                    t = T_MLP2[l] + 2 * KD * n
                    f0 = NF1 + NF2 * l + KD * n
                    with act.Fori(0, KD // 2) as i:
                        for p_ in range(2):
                            split_hi(i + t // 2 + 1, p_)
                            act.wait_ge(tile_done, 2 * i + t + p_ + 1)
                            act.wait_ge(squared, 2 * i + f0 - NF1 + p_ + 1)
                            act.activation(tmp[:, p_], G[p_][:], ACT.Relu).then_inc(evac[p_], 1)
                            act.wait_ge(evac[p_], i + t // 2 + 1)
                            act.activation(ff_hi[:, bass.ds(2 * i + p_, 1)].rearrange("p o s -> p (o s)"), tmp[:, p_],
                                           ACT.Square).then_inc(ffh_ready, 1)
                    t += KD
                    splits(t, t + KD if t + KD < N_TILES else N_TILES - 2)
            norm(6, N_TILES)

        @block.vector
        def _(dve):
            def add_tiles(t0, n):
                with dve.Fori(0, n // 2) as i:
                    for p_ in range(2):
                        dve.wait_ge(tile_done, 2 * i + t0 + p_ + 1)
                        xs = x[:, bass.ds(2 * i + p_, 1)].rearrange("p o s -> p (o s)")
                        dve.tensor_tensor(xs, xs, G[p_][:], ALU.add).then_inc(evac[p_], 1)

            def norm(n, name):
                dve.wait_ge(rstd_ready, n + 1)

                def low(k):
                    dve.wait_ge(xh_ready, KD * n + k + 1)
                    dve.tensor_tensor(xn_lo[:, k], tmp[:, 2 + k % 2], xn_hi[:, k].bitcast(F32),
                                      ALU.subtract).then_inc(xn_ready, 1)
                for k in range(KD):
                    g = pcol(name, k, k + 1)
                    if n == 6:
                        dve.scalar_tensor_tensor(out=z[:, k], in0=x[:, k], scalar=g, in1=rstd[:], op0=ALU.mult,
                                                 op1=ALU.mult).then_inc(final_ready, 1)
                        continue
                    if k >= 2:
                        dve.wait_ge(xn_ready, KD * n + k - 1)
                    dve.scalar_tensor_tensor(out=tmp[:, 2 + k % 2], in0=x[:, k], scalar=g, in1=rstd[:], op0=ALU.mult,
                                             op1=ALU.mult).then_inc(t_ready, 1)
                    if k >= 1:
                        low(k - 1)
                if n < 6:
                    low(KD - 1)

            def maxima(c, p, q_, n, sink=None):
                a, b = c.ranges[n]
                w = (b - a) * P
                off = (a - n + NQ - 1) * P
                ho = c.halves_out
                for h in range(2):
                    s = 2 * n + h
                    dve.wait_ge(c.scored, 8 * p + s + 1)
                    if not (isinstance(p, int) and p == 0 and n < 2):
                        dve.wait_ge(c.turned, ho * (4 * p + n - 2) + min(h, ho - 1) + 1)
                    dve.memset(small[:, 104 + 8 * q_ + s:105 + 8 * q_ + s], 0.0)
                    dve.tensor_tensor_reduce(out=prob[:, n % 2, h, 0:w], in0=SC[h][:, 0:w],
                                             in1=bias[:, c.parity(q_, p), h, off:off + w], scale=1.0, scalar=-3e38,
                                             op0=ALU.add, op1=ALU.max,
                                             accum_out=mx[:, q_, s:s + 1]).then_inc(c.maxed, 1)
                for h in range(2):
                    s = 2 * n + h
                    dve.wait_ge(c.maxed, 8 * p + s + 1)
                    if sink is None:
                        ins = dve.tensor_scalar(nm[:, q_, s:s + 1], mx[:, q_, s:s + 1], -1.0, None, ALU.mult)
                    else:
                        ins = dve.tensor_scalar(nm[:, q_, s:s + 1], mx[:, q_, s:s + 1], sink(h), -1.0, ALU.max, ALU.mult)
                    ins.then_inc(c.negated, 1)

            def scale(c, p, q_, n, sink=None):
                a, b = c.ranges[n]
                s = slice(2 * n, 2 * n + 2)
                per = {swa: 2, att[0]: 1, att[1]: 3}[c]
                base = per * (4 * p + n)
                dve.wait_ge(c.expd, 8 * p + 2 * n + 2)
                if sink is not None:
                    dve.tensor_tensor(sm[:, q_, s], sm[:, q_, s], es[:, q_, s], ALU.add).then_inc(c.recd, 1)
                    dve.wait_ge(c.recd, base + 1)
                dve.reciprocal(rc[:, q_, s], sm[:, q_, s]).then_inc(c.recd, 1)
                dve.wait_ge(c.recd, base + (2 if sink is not None else 1))
                pr = [prob[:, n % 2, h, 0:(b - a) * P] for h in range(2)]
                rs = [rc[:, q_, 2 * n + h:2 * n + h + 1] for h in range(2)]
                if c is att[1]:
                    dve.tensor_scalar(rs[1], rs[1], neg_lam, None, ALU.mult).then_inc(c.recd, 1)
                    dve.tensor_scalar(pr[0], pr[0], rs[0], None, ALU.mult).then_inc(c.recd, 1)
                    dve.wait_ge(c.recd, base + 3)
                    dve.scalar_tensor_tensor(out=pr[0], in0=pr[1], scalar=rs[1], in1=pr[0], op0=ALU.mult,
                                             op1=ALU.add).then_inc(c.scaled, 1)
                else:
                    for h in range(2):
                        dve.tensor_scalar(pr[h], pr[h], rs[h], None, ALU.mult).then_inc(c.scaled, 1)

            def dlink(ins):
                link("dve", dve, ins)

            dve.memset(small[:, 0:96], 0.0)
            dve.memset(small[:, 96:128], EPS).then_inc(squared, 1)
            dve.memset(v_tok[:], 0.0).then_inc(squared, 1)
            dve.wait_ge(squared, 2)
            dve.wait_ge(loaded, 64)
            norm(0, "mix_norm")
            dve.wait_ge(glr_split, 1)
            dve.tensor_tensor(glr_w[:, 1], pcol("w_glr"), glr_w[:, 0].bitcast(F32), ALU.subtract).then_inc(glr_split, 1)
            dve.wait_ge(tab_mm, 1)
            for b in range(2):
                dve.tensor_copy(table_sb[:, 1, b * S:(b + 1) * S], SC[b][0:16])
                ins = dve.tensor_tensor(table_sb[:, 0, b * S:(b + 1) * S], SC[b][0:16],
                                        bucket[0:16, 1024 + b * S:1024 + (b + 1) * S], ALU.add)
                ins.then_inc(tab_sb, 1)
            dve.tensor_scalar(pcol("q_norm"), pcol("q_norm"), 0.125, None, ALU.mult)
            dve.tensor_scalar(pcol("subln"), pcol("subln"), 1.0 - LAMBDA_INIT, None, ALU.mult)
            lam = pcol("lam").rearrange("p (i d) -> p i d", i=4)
            lam_prod = lhe[:].rearrange("p a n h -> p (a n h)").rearrange("p (i d) -> p i d", i=2)
            dlink(dve.tensor_tensor(lam_prod, lam[:, 0::2], lam[:, 1::2], ALU.mult))
            dve.tensor_reduce(lam_s[:, 0:2], lam_prod, mybir.AxisListType.X, ALU.add).then_inc(lam_sum, 1)
            dve.wait_ge(lam_exp, 1)
            dlink(dve.tensor_tensor(neg_lam, lam_s[:, 3:4], lam_s[:, 2:3], ALU.subtract))
            dlink(dve.tensor_scalar(neg_lam, neg_lam, -LAMBDA_INIT, None, ALU.add))

            dve.wait_ge(glr_done, 1)
            dve.tensor_copy(tmp[0:16, 0], MB[0:16]).then_inc(glr_read, 1)
            dve.wait_ge(gate_in, 1)
            for j in range(2):
                b = pcol("b_alpha", j, j + 1)
                dve.tensor_scalar(qkv[:, j, 0], TR[j][:], b, 0.0, ALU.add, ALU.min).then_inc(gate_abs, 1)
            for h in range(GH):
                dve.wait_ge(turned_in, h + 1)
                dve.tensor_copy(gv_tok[:, :, h], (OB, MB)[h % 2][:].rearrange("p (t f) -> p t f", t=NQ)).then_inc(turned_out, 1)
            for j in range(2):
                dve.wait_ge(gate_log, j + 1)
                dlink(dve.tensor_tensor(qkv[:, j, 1], qkv[:, j, 0], qkv[:, j, 1], ALU.subtract))
                dve.tensor_tensor_scan(qkv[:, j, 0], ccol("reset"), qkv[:, j, 1], 0.0, ALU.mult, ALU.add).then_inc(decay_sum, 1)
                dve.wait_ge(decay_sum, j + 1)
                v = qkv[:, j, 0].rearrange("p (c t) -> p c t", t=CHUNK)
                dve.tensor_tensor(qkv[:, j, 2].rearrange("p (c t) -> p c t", t=CHUNK),
                                  v[:, :, CHUNK - 1:CHUNK].broadcast_to([P, NCH, CHUNK]), v, ALU.subtract).then_inc(decay_diff, 1)
            for j in range(2):
                dve.wait_ge(decay_exp, j + 1)
                dve.scalar_tensor_tensor(out=z[:, Z_GQ + j], in0=z[:, Z_GQ + j], scalar=0.125, in1=tmp[:, 2 + j],
                                         op0=ALU.mult, op1=ALU.mult).then_inc(gla_keys, 1)
                dve.tensor_tensor(qkv[:, j, 1], z[:, Z_GK + j], qkv[:, j, 1], ALU.mult).then_inc(gla_keys, 1)
                dve.wait_ge(key_exp, j + 1)
                dve.tensor_tensor(qkv[:, j, 2], z[:, Z_GK + j], qkv[:, j, 2], ALU.mult).then_inc(gla_keys, 1)
            for j in range(2):
                dve.wait_ge(turned_in, GH + j + 1)
                dve.tensor_copy(kd_tok[:, j], (OB, MB)[j][:].rearrange("p (t f) -> p t f", t=NQ)).then_inc(turned_out, 1)
            dve.wait_ge(tables_saved, 32)
            for j in range(2):
                dlink(dve.memset(state[:, j, 0], 0.0))
                for c in range(NCH - 1):
                    i = (NCH - 1) * j + c
                    dve.wait_ge(state_in, i + 1)
                    if i:
                        dve.wait_ge(state_out, 2 * i)
                    for h in range(2):
                        r = slice(64 * h, 64 * h + 64)
                        dve.scalar_tensor_tensor(out=state[r, j, c + 1], in0=state[r, j, c], scalar=decay[r, j, c:c + 1],
                                                 in1=SC[c % 2][r, P * h:P * h + P], op0=ALU.mult,
                                                 op1=ALU.add).then_inc(state_out, 1)
                for h in range(2):
                    dve.wait_ge(gla_a, 2 * j + h + 1)
                    if j:
                        dve.wait_ge(gla_o, h + 1)
                    dve.tensor_tensor(tmp[:, h].rearrange("p (t s) -> p t s", t=NQ), TR[h][:].rearrange("p (t s) -> p t s", t=NQ),
                                      ccol("gla_mask").rearrange("p (o s) -> p o s", o=1).broadcast_to([P, NQ, P]),
                                      ALU.mult).then_inc(gla_masked, 1)
                for h in range(2):
                    i = 2 * j + h
                    o = (OB, MB)[h]
                    dve.wait_ge(gla_r, i + 1)
                    if i:
                        dve.wait_ge(gla_lo, i)
                    dlink(dve.scalar_tensor_tensor(out=tmp[:, 3], in0=o[:], scalar=pcol("gla_norm"), in1=rstd[:],
                                                   op0=ALU.mult, op1=ALU.mult))
                    dve.wait_ge(gates_on, i + 1)
                    dve.tensor_tensor(tmp[:, 3], tmp[:, 3], z[:, Z_GR + i], ALU.mult).then_inc(gla_t, 1)
                    dve.wait_ge(gla_hi, i + 1)
                    dve.tensor_tensor(ff_lo[:, i], tmp[:, 3], ff_hi[:, i].bitcast(F32), ALU.subtract).then_inc(gla_lo, 1)

            for i in range(5):
                dve.wait_ge(swn_r, i + 1)
                zi = z[:, Z_SK] if i == 0 else z[:, Z_SQ + i - 1]
                g = pcol("k_norm") if i == 0 else pcol("q_norm")
                dve.scalar_tensor_tensor(out=zi, in0=zi, scalar=g, in1=rstd[:], op0=ALU.mult, op1=ALU.mult).then_inc(swn_done, 1)
                dve.wait_ge(swn_done, i + 1)
            dve.wait_ge(swv_t, 1)
            vt = MB[:].rearrange("p (t f) -> p t f", t=NQ)
            dve.tensor_copy(v_tok[:, 0, 0, :, 0:64], vt[:, :, 0:64])
            dve.tensor_copy(v_tok[:, 0, 1, :, 64:128], vt[:, :, 64:128]).then_inc(swv_done, 1)
            for p in range(4):
                def sink(h, p=p):
                    return pcol("sinks", 2 * p + h, 2 * p + h + 1)
                dve.wait_ge(bias_in[p % 2], 16 * (p // 2 + 1))
                maxima(swa, p, 0, 0, sink)
                maxima(swa, p, 0, 1, sink)
                scale(swa, p, 0, 0, sink)
                scale(swa, p, 0, 1, sink)
                maxima(swa, p, 0, 2, sink)
                scale(swa, p, 0, 2, sink)
                maxima(swa, p, 0, 3, sink)
                scale(swa, p, 0, 3, sink)
                dve.wait_ge(swa_hi, p + 1)
                dve.tensor_tensor(ff_lo[:, GH + p], OB[:], ff_hi[:, GH + p].bitcast(F32), ALU.subtract).then_inc(swa_lo, 1)
            add_tiles(T_OUT, KD)

            norm(1, "ffn_norm")
            t = T_MLP1
            for a, b in CHUNKS1:
                with dve.Fori(0, b - a) as i:
                    f, m = i + a, i + t // 2
                    for p_ in range(2):
                        cs = [par[:, bass.ds(_cols["conv_w"][0] + 2 * NF1 * j + 2 * f + p_, 1)] for j in range(2)]
                        dve.wait_ge(conv_0, 2 * f + p_ + 1)
                        dve.scalar_tensor_tensor(out=tmp[:, p_, 1:S], in0=G[p_][:, 0:S - 1], scalar=cs[1], in1=tmp[:, p_, 1:S],
                                                 op0=ALU.mult, op1=ALU.add).then_inc(conv_1, 1)
                        dve.wait_ge(conv_1, 2 * f + p_ + 1)
                        dve.scalar_tensor_tensor(out=tmp[:, p_, 2:S], in0=G[p_][:, 0:S - 2], scalar=cs[0], in1=tmp[:, p_, 2:S],
                                                 op0=ALU.mult, op1=ALU.add).then_inc(evac[p_], 1)
                    dve.wait_ge(silu_done, f + 1)
                    dve.wait_ge(evac[1], m + 1)
                    dve.tensor_tensor(tmp[:, 3], tmp[:, 2], tmp[:, 1], ALU.mult).then_inc(f_made, 1)
                    dve.wait_ge(ffh_ready, f + 1)
                    dve.tensor_tensor(ff_lo[:, bass.ds(i, 1)].rearrange("p o s -> p (o s)"), tmp[:, 3],
                                      ff_hi[:, bass.ds(i, 1)].rearrange("p o s -> p (o s)").bitcast(F32),
                                      ALU.subtract).then_inc(ff_ready, 1)
                t += 2 * (b - a)
                add_tiles(t, KD)
                t += KD

            for l in range(2):
                c = att[l]
                norm(2 + 2 * l, ("mix2a", "mix2b")[l])

                def v_copy(p, u):
                    dve.wait_ge(c.vt_done, p + 1)
                    if not (isinstance(p, int) and p < 2):
                        dve.wait_ge(c.o_done, p - 1)
                    vt = MB[:].rearrange("p (t f) -> p t f", t=NQ)
                    if l == 0:
                        dve.tensor_copy(v_tok[:, u, 0, :, 0:64], vt[:, :, 0:64])
                        ins = dve.tensor_copy(v_tok[:, u, 1, :, 64:128], vt[:, :, 64:128])
                    else:
                        ins = dve.tensor_copy(v_tok[:, u, 0], vt)
                    ins.then_inc(c.v_ready, 1)

                def pair(p, u, nxt):
                    dve.wait_ge(bias_in[u], 16 * (2 + 4 * l) + (16 * (p // 2 + 1) if isinstance(p, int) else 16 * nxt_of(p, u)))
                    maxima(c, p, u, 0)
                    scale(c, p, u, 0)
                    maxima(c, p, u, 1)
                    scale(c, p, u, 1)
                    maxima(c, p, u, 2)
                    maxima(c, p, u, 3)
                    scale(c, p, u, 2)
                    scale(c, p, u, 3)
                    if l == 0:
                        at_p = bass.ds(p, 1)
                        dve.tensor_copy(lse_nm[:, at_p].rearrange("p o s -> p (o s)"), nm[:, u]).then_inc(c.lse_kept, 1)
                        dve.tensor_copy(lse_sm[:, at_p].rearrange("p o s -> p (o s)"), sm[:, u]).then_inc(c.lse_kept, 1)
                    dve.wait_ge(c.o_done, p + 1)
                    dve.tensor_copy(oT[:, bass.ds(p, 1)].rearrange("p o s -> p (o s)"), OB[:]).then_inc(c.o_read, 1)
                    if nxt is not None:
                        v_copy(p + 1, 1 - u)

                loop = {}

                def nxt_of(p, u):
                    return loop["i"] + (1 if u == 1 else 2)

                v_copy(0, 0)
                pair(0, 0, 1)
                with dve.Fori(0, 3) as i:
                    loop["i"] = i
                    pair(2 * i + 1, 1, True)
                    pair(2 * i + 2, 0, True)
                pair(7, 1, None)

                if l == 0:
                    dve.wait_ge(grp_a, 1)
                    dlink(dve.tensor_tensor(lse_sm[:], lse_sm[:], lse_nm[:], ALU.subtract))
                    dve.tensor_copy(lhe[:, 0].rearrange("p n (q h) -> p q n h", h=2),
                                    lse_sm[:].rearrange("p q (n h) -> p q n h", h=2)).then_inc(grp_d, 1)
                    dve.wait_ge(grp_d, 1)
                    for g, (a, b) in enumerate(GROUPS):
                        ins = dve.tensor_reduce(grp[:, 0, :, g:g + 1].rearrange("p n o -> p (n o)"), lhe[:, 0, :, a:b],
                                                mybir.AxisListType.X, ALU.max)
                    ins.then_inc(grp_d, 1)
                    dve.wait_ge(grp_d, 2)
                    for g, (a, b) in enumerate(GROUPS):
                        ins = dve.tensor_tensor(lhe[:, 1, :, a:b], lhe[:, 0, :, a:b],
                                                grp[:, 0, :, g:g + 1].broadcast_to([P, NQ, b - a]), ALU.subtract)
                    ins.then_inc(grp_d, 1)
                    dve.wait_ge(grp_a, 2)
                    for g, (a, b) in enumerate(GROUPS):
                        ins = dve.tensor_reduce(grp[:, 1, :, g:g + 1].rearrange("p n o -> p (n o)"), lhe[:, 1, :, a:b],
                                                mybir.AxisListType.X, ALU.add)
                    ins.then_inc(grp_d, 1)
                    dve.wait_ge(grp_a, 3)
                    dlink(dve.tensor_tensor(grp[:, 1], grp[:, 1], grp[:, 0], ALU.add))
                    for g, (a, b) in enumerate(GROUPS):
                        ins = dve.tensor_scalar(grp[:, 1, :, g:g + 1], grp[:, 1, :, g:g + 1], -math.log(b - a), None, ALU.add)
                    dlink(ins)
                    m3 = small[:, 88:92]
                    dve.tensor_reduce(m3, grp[:, 1], mybir.AxisListType.X, ALU.max).then_inc(grp_d, 1)
                    dve.wait_ge(grp_d, 5)
                    dve.tensor_tensor(grp[:, 2], grp[:, 1], m3.rearrange("p (n o) -> p n o", o=1).broadcast_to([P, NQ, 3]),
                                      ALU.subtract).then_inc(grp_d, 1)
                    dve.wait_ge(grp_a, 4)
                    s3 = small[:, 92:96]
                    dlink(dve.tensor_reduce(s3, grp[:, 2], mybir.AxisListType.X, ALU.add))
                    dve.reciprocal(s3, s3).then_inc(grp_d, 1)
                    dve.wait_ge(grp_d, 7)
                    dve.scalar_tensor_tensor(out=grp[:, 5], in0=grp[:, 2], scalar=3.0,
                                             in1=s3.rearrange("p (n o) -> p n o", o=1).broadcast_to([P, NQ, 3]),
                                             op0=ALU.mult, op1=ALU.mult).then_inc(grp_d, 1)
                    dve.wait_ge(grp_t, 1)
                    dve.tensor_copy(tmp[0:3, 3], MB[0:3]).then_inc(grp_row, 1)

                def low(p):
                    dve.wait_ge(post_hi, PAIRS * l + p + 1)
                    dve.tensor_tensor(ff_lo[:, p], tmp[:, p % 2], ff_hi[:, p].bitcast(F32), ALU.subtract).then_inc(post_lo, 1)

                for p in range(PAIRS):
                    i = PAIRS * l + p
                    dve.wait_ge(post_mm, i + 1)
                    if p >= 2:
                        dve.wait_ge(post_lo, i - 1)
                    if l == 0:
                        dve.tensor_tensor(tmp[:, p % 2], oT[:, p], SC[p % 2][:], ALU.mult).then_inc(post_t, 1)
                    else:
                        dve.wait_ge(post_r, p + 1)
                        dve.scalar_tensor_tensor(out=tmp[:, p % 2], in0=oT[:, p], scalar=pcol("subln"), in1=rstd[:],
                                                 op0=ALU.mult, op1=ALU.mult).then_inc(post_t, 1)
                    if p >= 1:
                        low(p - 1)
                low(PAIRS - 1)
                add_tiles(T_WO[l], KD)
                norm(3 + 2 * l, ("mlp2a", "mlp2b")[l])
                for n in range(NF2 // KD):
                    t = T_MLP2[l] + 2 * KD * n
                    f0 = NF1 + NF2 * l + KD * n

                    def low2(i, p_):
                        dve.wait_ge(ffh_ready, 2 * i + f0 + p_ + 1)
                        at_f = bass.ds(2 * i + p_, 1)
                        dve.tensor_tensor(ff_lo[:, at_f].rearrange("p o s -> p (o s)"), tmp[:, 2 + p_],
                                          ff_hi[:, at_f].rearrange("p o s -> p (o s)").bitcast(F32),
                                          ALU.subtract).then_inc(ff_ready, 1)
                    with dve.Fori(0, KD // 2) as i:
                        for p_ in range(2):
                            dve.wait_ge(evac[p_], i + t // 2 + 1)
                            dve.tensor_tensor(tmp[:, 2 + p_], tmp[:, p_], tmp[:, p_], ALU.mult).then_inc(squared, 1)
                            dve.wait_ge(squared, 2 * i + f0 - NF1 + p_ + 3)
                            low2(i, p_)
                    add_tiles(t + KD, KD)
            norm(6, "final")


_BLOCKED = {}


def _toeplitz_index():
    return np.arange(1024) - (S - 1)


def _buckets():
    rel = _toeplitz_index()
    nb, me = 16, 8
    n = np.abs(rel)
    nf = np.maximum(n, 1).astype(np.float32)
    large = me + (np.log(nf / np.float32(me)) / np.float32(math.log(1024 / me)) * np.float32(nb - me)).astype(np.int32)
    bucket = np.where(rel > 0, nb, 0) + np.where(n < me, n, np.minimum(large, nb - 1))
    both = np.zeros((32, 2048), np.float32)
    both[bucket, np.arange(1024)] = 1.0
    h = 0
    for win, dil, nh in ((128, 1, 6), (512, 4, 5), (2048, 16, 5)):
        ok = (n % dil == 0) & (n <= dil * (win // (2 * dil)))
        both[h:h + nh, 1024:] = np.where(ok, 0.0, NEG)
        h += nh
    return both


def _swa_table():
    dist = (WIN + np.arange(P)[:, None] - np.arange(2 * P)[None]).astype(np.float32)
    rows = []
    for h in (0, 4, 1, 5, 2, 6, 3, 7):
        slope = np.float32(2.0 ** (-(h + 1)))
        rows.append(np.where((dist >= 0) & (dist < WIN), -slope * dist, np.float32(NEG)))
    return np.ascontiguousarray(np.stack(rows).reshape(4, 2, P, 2 * P).transpose(0, 2, 1, 3).astype(np.float32))


def _constants():
    c = np.zeros((P, N_CON), np.float32)

    def put(name, a):
        s, e = _ccols[name]
        c[:a.shape[0], s:e] = a
    put("ident", np.eye(P))
    put("flip", np.eye(P)[::-1])
    put("mean_d", np.full((P, P), 1.0 / D))
    put("mean_128", np.full((P, P), 1.0 / 128))
    put("mean_64", np.kron(np.eye(2), np.full((64, 64), 1.0 / 64)))
    i = np.arange(P)
    put("gla_mask", (i[:, None] <= i[None, :]) & (i[:, None] // CHUNK == i[None, :] // CHUNK))
    put("reset", np.tile((np.arange(S) % CHUNK != 0)[None], (P, 1)))
    return c


def _tiles(w):
    k, n = w.shape
    return w.reshape(k // P, P, n // P, P).transpose(2, 1, 0, 3).reshape(n // P, P, (k // P) * P)


def _weights(i):
    w = i["w_in"][0]
    parts = np.split(w, np.cumsum([256, 256, 512, 512, 16, 512, 128])[:7], axis=1)
    gq, gk, gv, gr, _, sq, sk, sv = parts
    heads = sq.reshape(D, 8, 64)[:, [0, 4, 1, 5, 2, 6, 3, 7]].reshape(D, 512)
    seq = [_tiles(np.concatenate([gq, gk, gv, gr, sk, sv, heads], axis=1))]
    wo = i["w_out"][0]
    low = wo[512:].reshape(8, 64, D)[[0, 4, 1, 5, 2, 6, 3, 7]].reshape(512, D)
    seq.append(_tiles(np.concatenate([wo[:512], low])))
    up = i["w_up"][0].reshape(D, 2, NF1, P).transpose(0, 2, 1, 3).reshape(D, 2 * FF1)
    up, down = _tiles(up), i["w_down"][0]
    for a, b in CHUNKS1:
        seq.append(up[2 * a:2 * b])
        t = _tiles(down[a * P:b * P])
        seq.append(np.pad(t, ((0, 0), (0, 0), (0, D - t.shape[2]))))
    for l, (qkv, wo) in enumerate((("a_w_qkv_2", "a_w_o_2"), ("b_w_qkv_2", "b_w_o_2"))):
        w = i[qkv][0].reshape(D, 3, PAIRS, P).transpose(0, 2, 1, 3).reshape(D, 3 * D)
        seq += [_tiles(w), _tiles(i[wo][0])]
        up, down = _tiles(i["mlp_w_in_2"][l]), i["mlp_w_out_2"][l]
        for n in range(NF2 // KD):
            seq += [up[KD * n:KD * n + KD], _tiles(down[D * n:D * n + D])]
    return np.concatenate(seq)


def _params(i):
    p = np.zeros((P, N_PAR), np.float32)

    def put(name, a):
        s, e = _cols[name]
        p[:a.shape[0], s:e] = a

    def cols(v):
        return v.reshape(-1, P).T
    put("mix_norm", cols(i["mix_norm"][0]))
    put("ffn_norm", cols(i["ffn_norm"][0]))
    for l in range(2):
        put(("mix2a", "mix2b")[l], cols(i["norm_mix_g_2"][l]))
        put(("mlp2a", "mlp2b")[l], cols(i["norm_mlp_g_2"][l]))
    put("final", cols(i["norm_final_g_2"]))
    cw = i["conv_w"][0].reshape(3, 2, NF1, P)
    put("conv_w", cw.transpose(3, 0, 2, 1).reshape(P, -1))
    put("conv_b", i["conv_b"][0].reshape(2, NF1, P).transpose(2, 1, 0).reshape(P, -1))
    put("b_alpha", cols(i["b_alpha"][0]))
    put("gla_norm", i["gla_norm"][0][:, None])
    put("q_norm", np.tile(i["q_norm"][0], 2)[:, None])
    put("k_norm", np.tile(i["k_norm"][0], 2)[:, None])
    put("subln", i["b_subln_g_2"][0][:, None])
    put("sinks", np.tile(i["sinks"][0][[0, 4, 1, 5, 2, 6, 3, 7]][None], (P, 1)))
    put("lam", np.tile(i["b_lambda_2"][0].reshape(1, 256), (P, 1)))
    glr = np.zeros((KD, P, 32), np.float32)
    glr[:, :, :16] = i["w_in"][0][:, 1536:1552].reshape(KD, P, 16)
    put("w_glr", glr.transpose(1, 0, 2).reshape(P, -1))
    put("w_alpha", i["w_alpha2"][0])
    put("rel_bias", i["rel_bias_2"])
    return p


def kernel(**inputs):
    import concourse.bacc as bacc
    from concourse.bass_utils import run_bass_kernel_spmd

    i = {k: np.asarray(v) for k, v in inputs.items()}
    arrays = {
        "x_in": np.ascontiguousarray(i["x"][0].reshape(S, KD, P).transpose(2, 1, 0)),
        "params": _params(i),
        "consts": _constants(),
        "sel": (np.repeat([0] * 6 + [1] * 5 + [2] * 5, 64)[None] == np.arange(3)[:, None]).astype(np.float32),
        "buckets": _buckets(),
        "swa_table": _swa_table(),
        "weights": _weights(i),
    }
    nc = bacc.Bacc("TRN2", target_bir_lowering=False, num_devices=1)
    args = [nc.dram_tensor(n, a.shape, F32, kind="ExternalInput").ap() for n, a in arrays.items()]
    tables = [nc.dram_tensor(f"table{l}", (16, 1024), F32, kind="Internal").ap() for l in range(2)]
    out = nc.dram_tensor("out", (P, KD, S), F32, kind="ExternalOutput").ap()
    program(nc, *args, tables, out)
    r = run_bass_kernel_spmd(nc, [arrays], core_ids=[0])
    return r.results[0]["out"].transpose(2, 1, 0).reshape(1, S, D)
```

```python
import math
from contextlib import ExitStack

import numpy as np
import concourse.bass as bass
from concourse import mybir

F32 = mybir.dt.float32
F32R = mybir.dt.float32r
ALU = mybir.AluOpType
ACT = mybir.ActivationFunctionType

P = 128
S = 512
D = 1024
KD = D // P
NQ = S // P
EPS = 1e-6
NEG = -1e30

FF1 = 2816
NF1 = FF1 // P
FF2 = 4096
NF2 = FF2 // P
PAIRS = 8
NEAR = 3
DIL = 4
CHUNK = 64
NCH = S // CHUNK
GH = 4
WIN = 128
EXT = S + 3 * P

N_IN = 18
N_OUT = KD
CHUNKS1 = [(0, 8), (8, 16), (16, 22)]
T_IN = 0
T_OUT = T_IN + N_IN
T_MLP1 = T_OUT + N_OUT
T_QKV = [0, 0]
T_WO = [0, 0]
T_MLP2 = [0, 0]
_t = T_MLP1 + 2 * NF1 + KD * len(CHUNKS1)
for _l in range(2):
    T_QKV[_l] = _t
    T_WO[_l] = _t + 3 * PAIRS
    T_MLP2[_l] = T_WO[_l] + KD
    _t = T_MLP2[_l] + 2 * NF2
N_TILES = _t
Z_SK, Z_SV, Z_SQ, Z_GQ, Z_GK, Z_GV, Z_GR = 0, 1, 2, 6, 8, 10, 14
SWA_TILES = [(8, 11), (11, 14), (14, 16), (16, 18)]

_cols = {}
_n = 0
for _name, _w in [("mix_norm", 8), ("ffn_norm", 8), ("mix2a", 8), ("mix2b", 8), ("mlp2a", 8), ("mlp2b", 8),
                  ("final", 8), ("conv_w", 3 * 2 * NF1), ("conv_b", 2 * NF1), ("b_alpha", 2), ("gla_norm", 1),
                  ("q_norm", 1), ("k_norm", 1), ("subln", 1), ("sinks", 8), ("lam", 256), ("w_glr", 8 * 32),
                  ("w_alpha", 256), ("rel_bias", 16)]:
    _cols[_name] = (_n, _n + _w)
    _n += _w
N_PAR = _n
_ccols = {}
_n = 0
for _name, _w in [("ident", P), ("flip", P), ("mean_d", P), ("mean_128", P), ("mean_64", P), ("gla_mask", P), ("reset", S)]:
    _ccols[_name] = (_n, _n + _w)
    _n += _w
N_CON = _n
LAMBDA_INIT = 0.8 - 0.6 * math.exp(-0.3 * 1)


def program(nc, x_in, params, consts, sel, buckets, swa_table, weights, tables, out):
    with ExitStack() as ctx:
        def sb(name, shape, dt=F32):
            return ctx.enter_context(nc.sbuf_tensor(name, shape, dt))

        def sem(name):
            return ctx.enter_context(nc.semaphore(name))

        x = sb("x", [P, KD, S])
        xn_hi = sb("xn_hi", [P, KD, S], F32R)
        xn_lo = sb("xn_lo", [P, KD, S], F32R)
        ff_hi = sb("ff_hi", [P, KD, S], F32R)
        ff_lo = sb("ff_lo", [P, KD, S], F32R)
        stage = sb("stage", [P, 2, KD, P])
        w_hi = sb("w_hi", [P, 2, KD, P], F32R)
        w_lo = sb("w_lo", [P, 2, KD, P], F32R)
        z = sb("z", [P, N_IN, S])
        par = sb("par", [P, N_PAR])
        con = sb("con", [P, N_CON])
        bias = sb("bias", [P, 2, 2, EXT])
        qkv = sb("qkv", [P, 2, 3, S])
        v_tok = sb("v_tok", [P, 2, 2, NQ, P])
        prob = sb("prob", [P, 2, 2, S])
        tmp = sb("tmp", [P, 4, S])
        rstd = sb("rstd", [P, S])
        rstd_h = sb("rstd_h", [P, S])
        mx = sb("mx", [P, 2, 8])
        nm = sb("nm", [P, 2, 8])
        sm = sb("sm", [P, 2, 8])
        rc = sb("rc", [P, 2, 8])
        es = sb("es", [P, 2, 8])
        lse_nm = sb("lse_nm", [P, PAIRS, 8])
        lse_sm = sb("lse_sm", [P, PAIRS, 8])
        small = sb("small", [P, 128])
        glr_w = sb("glr_w", [P, 2, KD * 32], F32R)

        oT = z[:, 0:KD, :]
        pT = z[:, KD:2 * KD, :].rearrange("p (h k) s -> p h k s", h=2)

        banks = [ctx.enter_context(nc.psum_tensor(f"bank{i}", [P, S], F32)) for i in range(8)]
        G = banks[0:2]
        SC = banks[2:4]
        TR = banks[4:6]
        OB = banks[6]
        MB = banks[7]

        def pcol(name, a=0, b=None):
            s, e = _cols[name]
            return par[:, s + a:(e if b is None else s + b)]

        def ccol(name):
            s, e = _ccols[name]
            return con[:, s:e]

        ident = ccol("ident")

        loaded = sem("loaded")
        stage_full = [sem(f"stage_full{i}") for i in range(2)]
        hi_ready = sem("hi_ready")
        lo_ready = sem("lo_ready")
        hi_free = sem("hi_free")
        tile_done = sem("tile_done")
        evac = [sem(f"evac{i}") for i in range(2)]
        x_in_done = [sem(f"x_in{i}") for i in range(2)]
        const_ready, acc_zero = sem("const_ready"), sem("acc_zero")
        sq_ready, acc_done, ss_done = sem("sq_ready"), sem("acc_done"), sem("ss_done")
        eps_added, inv_ready, rstd_ready = sem("eps_added"), sem("inv_ready"), sem("rstd_ready")
        glr_split = sem("glr_split")
        glr_done, glr_read, gate_in = sem("glr_done"), sem("glr_read"), sem("gate_in")
        gate_abs, gate_log = sem("gate_abs"), sem("gate_log")
        decay_sum, decay_exp, decay_diff, key_exp = sem("decay_sum"), sem("decay_exp"), sem("decay_diff"), sem("key_exp")
        gla_keys = sem("gla_keys")
        turned_in, turned_out = sem("turned_in"), sem("turned_out")
        state_in, state_out = sem("state_in"), sem("state_out")
        gla_a, gla_masked, gla_o, gla_sq, gla_ss = sem("gla_a"), sem("gla_masked"), sem("gla_o"), sem("gla_sq"), sem("gla_ss")
        gla_r, swn_r, post_r = sem("gla_r"), sem("swn_r"), sem("post_r")
        gla_t, gla_hi, gla_lo = sem("gla_t"), sem("gla_hi"), sem("gla_lo")
        gates_on = sem("gates_on")
        swn_sq, swn_ss, swn_done = sem("swn_sq"), sem("swn_ss"), sem("swn_done")
        swv_t, swv_done = sem("swv_t"), sem("swv_done")
        swa_hi, swa_lo = sem("swa_hi"), sem("swa_lo")
        conv_0, conv_1, conv_2, silu_done, f_made = sem("conv_0"), sem("conv_1"), sem("conv_2"), sem("silu_done"), sem("f_made")
        ffh_ready, ff_ready = sem("ffh_ready"), sem("ff_ready")
        tab_mm, tab_sb, tables_saved = sem("tab_mm"), sem("tab_sb"), sem("tables_saved")
        lam_sum, lam_exp, lam_done = sem("lam_sum"), sem("lam_exp"), sem("lam_done")
        grp_d, grp_a, grp_t, grp_row = sem("grp_d"), sem("grp_a"), sem("grp_t"), sem("grp_row")
        gate_mm, gated, gate_hi, post_ln = sem("gate_mm"), sem("gated"), sem("gate_hi"), sem("post_ln")
        post_sq, post_mm, post_t, post_hi, post_lo = (sem("post_sq"), sem("post_mm"), sem("post_t"),
                                                      sem("post_hi"), sem("post_lo"))
        final_ready = sem("final_ready")
        sel_in = sem("sel_in")
        squared = sem("squared")
        xh_ready, xn_ready = sem("xh_ready"), sem("xn_ready")
        u_ready = sem("u_ready")
        chains = {"dve": sem("dve_chain"), "act": sem("act_chain"), "pe": sem("pe_chain")}
        bias_in = [sem(f"bias_in{i}") for i in range(2)]
        out_sent = sem("out_sent")

        at = {"dve": 0, "act": 0, "pe": 0}

        def link(key, eng, ins):
            at[key] += 1
            ins.then_inc(chains[key], 1)
            eng.wait_ge(chains[key], at[key])

        class Core:
            def __init__(self, n, pairs_out, ranges):
                self.n = n
                self.lse_kept = sem(f"{n}_lse")
                self.vt_done = sem(f"{n}_vt")
                self.v_ready = sem(f"{n}_v")
                self.scored = sem(f"{n}_scored")
                self.maxed = sem(f"{n}_maxed")
                self.negated = sem(f"{n}_negated")
                self.expd = sem(f"{n}_expd")
                self.summed = sem(f"{n}_summed")
                self.recd = sem(f"{n}_recd")
                self.scaled = sem(f"{n}_scaled")
                self.turned = sem(f"{n}_turned")
                self.copied = sem(f"{n}_copied")
                self.o_done = sem(f"{n}_o")
                self.pv_done = sem(f"{n}_pv") if n == "swa" else None
                self.o_read = {"swa": swa_lo, "dif": post_t}.get(n) or sem(f"{n}_oread")
                self.parity = (lambda q_, p: p % 2) if n == "swa" else (lambda q_, p: q_)
                self.halves_out = pairs_out
                self.ranges = ranges

        def qkv_tile(l, p, u, j):
            i = 3 * u + j
            if isinstance(p, int):
                return T_QKV[l] // 2 + (3 * p + j) // 2, i % 2
            return T_QKV[l] // 2 + 3 * p[0] + i // 2, i % 2

        def near(p):
            return isinstance(p, int) and p < NEAR

        swa = Core("swa", 2, lambda p, n: (max(0, n - 1), n + 1))
        att = [Core("dil", 2, lambda p, n: (max(0, n - 1), min(NQ, n + 2)) if near(p) else (n, n + 1)),
               Core("dif", 1, lambda p, n: (0, NQ))]

        block = ctx.enter_context(nc.Block())


        flat_bias = bias[:].rearrange("p a b c -> p (a b c)")
        kd_tok = flat_bias[:, 0:2 * S].rearrange("p (j t f) -> p j t f", j=2, t=NQ)
        gv_tok = flat_bias[:, 2 * S:6 * S].rearrange("p (t h f) -> p t h f", t=NQ, h=GH)
        state = prob[:].rearrange("p a b s -> p (a b s)").rearrange("p (j c f) -> p j c f", j=2, c=NCH)
        bucket = flat_bias[0:32, 0:2560]
        table_sb = prob[0:16].rearrange("p a b s -> p a (b s)")
        swa_pT = v_tok[:, 1]
        acc = tmp[:, 2]
        eps_col = small[:, 96:97]
        decay = small[:, 0:16].rearrange("p (j c) -> p j c", j=2)
        lam_s, neg_lam = small[:, 16:20], small[:, 20:21]
        lh = small[:, 24:88].rearrange("p (n h) -> p n h", n=NQ)
        grp = sb("grp", [P, 6, NQ, 3])
        lhe = sb("lhe", [P, 2, NQ, 16])
        selector = z[0:3, 16:18].rearrange("p a s -> p (a s)")
        near_row = tmp[0:1, 3]
        class_sb = tmp[0:16, 3, 0:256]
        GROUPS = [(0, 6), (6, 11), (11, 16)]

        def toeplitz(table, p):
            w = table.shape[1]
            return bass.AP(tensor=table.tensor, offset=2 * p * w, ap=[[1, P], [w, 2], [1, EXT if w > EXT else P]])

        @block.sync
        def _(sp):
            def load(m, p_, first=False):
                if not first:
                    sp.wait_ge(lo_ready, 2 * m + p_ - 1)
                if isinstance(m, int):
                    src = weights[2 * m + p_]
                else:
                    src = weights[bass.ds(2 * m + p_, 1)].rearrange("o p c -> (o p) c")
                sp.dma_start(stage[:, p_].rearrange("p k c -> p (k c)"), src).then_inc(stage_full[p_], 16)

            def loads(t0, t1):
                with sp.Fori(t0 // 2, t1 // 2) as m:
                    for p_ in range(2):
                        load(m, p_)

            def bias_load(core, table, p, q_, used):
                if used is not None:
                    sp.wait_ge(core.maxed, used)
                if core is swa:
                    sp.dma_start(bias[:, q_, :, 2 * P:4 * P], table[p]).then_inc(bias_in[q_], 16)
                elif core is att[0] and not near(p):
                    sp.dma_start(bias[:, q_, :, 3 * P:4 * P], toeplitz(tables[2], p)).then_inc(bias_in[q_], 16)
                else:
                    sp.dma_start(bias[:, q_], toeplitz(table, p)).then_inc(bias_in[q_], 16)

            sp.dma_start(par[:], params).then_inc(loaded, 16)
            for i in range(2):
                sp.dma_start(x[:, 4 * i:4 * i + 4], x_in[:, 4 * i:4 * i + 4]).then_inc(x_in_done[i], 16)
            load(0, 0, True)
            load(0, 1, True)
            sp.dma_start(con[:], consts).then_inc(loaded, 16)
            sp.dma_start(bucket, buckets).then_inc(loaded, 16)
            loads(2, 6)
            sp.wait_ge(tab_sb, 3)
            for p in range(4):
                loads(6 + 2 * p, 8 + 2 * p)
                if p < 2:
                    bias_load(swa, swa_table, p, p, None)
            loads(14, 18)
            bias_load(swa, swa_table, 2, 0, 8)
            bias_load(swa, swa_table, 3, 1, 16)
            loads(T_OUT, T_OUT + 2)
            sp.wait_ge(gla_lo, GH)
            sp.dma_start(selector, sel).then_inc(sel_in, 16)
            loads(T_OUT + 2, T_QKV[0])
            sp.wait_ge(tables_saved, 48)
            for l in range(2):
                core, before = att[l], (swa if l == 0 else att[0])
                sp.wait_ge(before.maxed, 8 * (4 if l == 0 else PAIRS))
                for p in range(2):
                    bias_load(core, tables[l], p, p, None)
                loads(T_QKV[l], T_QKV[l] + 6)

                def pair_loads(i):
                    for u in range(2):
                        for j in range(3 * u, 3 * u + 3):
                            if j == 3 * u + 2:
                                bias_load(core, tables[l], 2 * i + u, u, 16 * i + 8 * u - 8)
                            load(T_QKV[l] // 2 + 3 * i + j // 2, j % 2)
                if l == 0:
                    pair_loads(1)
                with sp.Fori(2 - l, 4) as i:
                    pair_loads(i)
                loads(T_WO[l], T_QKV[1] if l == 0 else N_TILES)
            for k in range(KD):
                sp.wait_ge(final_ready, k + 1)
                sp.dma_start(out[:, k], z[:, k]).then_inc(out_sent, 16)
            sp.wait_ge(out_sent, 16 * KD)

        @block.gpsimd
        def _(pool):
            def split_lo(m, p_, first=False):
                pool.wait_ge(hi_ready, 2 * m + p_ + 1)
                if not first:
                    pool.wait_ge(tile_done, 2 * m + p_ - 1)
                nc.gpsimd.tensor_tensor(w_lo[:, p_], stage[:, p_], w_hi[:, p_].bitcast(F32),
                                        ALU.subtract).then_inc(lo_ready, 1)
            split_lo(0, 0, True)
            split_lo(0, 1, True)
            with pool.Fori(1, N_TILES // 2) as m:
                for p_ in range(2):
                    split_lo(m, p_)

        @block.tensor
        def _(pe):
            def tile(m, p_, hi, lo, nk=KD, ready=None, late=None, order=None):
                pe.wait_ge(hi_ready, 2 * m + p_ + 1)
                if not (isinstance(m, int) and m == 0):
                    pe.wait_ge(evac[p_], m)
                if late is not None:
                    pe.wait_ge(late[0], late[1] - 1)
                ks = order or list(range(nk))

                def highs(ks, first):
                    for k in ks:
                        if ready is not None and k < ready[2]:
                            pe.wait_ge(ready[0], ready[1] + k + 1)
                        if late is not None and k == nk - 1:
                            pe.wait_ge(*late)
                        pe.matmul(G[p_][:], w_hi[:, p_, k], hi[:, k], start=(first and k == ks[0]), stop=False)
                        mm = pe.matmul(G[p_][:], w_hi[:, p_, k], lo[:, k], start=False, stop=False)
                    return mm

                def lows(ks, last):
                    for k in ks:
                        mm = pe.matmul(G[p_][:], w_lo[:, p_, k], hi[:, k], start=False, stop=(last and k == ks[-1]))
                    return mm

                if ready is None and late is None:
                    highs(ks, True).then_inc(hi_free, 1)
                    pe.wait_ge(lo_ready, 2 * m + p_ + 1)
                    lows(ks, True).then_inc(tile_done, 1)
                else:
                    highs(ks[:-1], True)
                    pe.wait_ge(lo_ready, 2 * m + p_ + 1)
                    lows(ks[:-1], False)
                    highs(ks[-1:], False).then_inc(hi_free, 1)
                    lows(ks[-1:], True).then_inc(tile_done, 1)

            def tiles(t0, t1, hi, lo, nk=KD, ready=None, n=None):
                if ready is not None:
                    tile(t0 // 2, 0, hi, lo, nk, ready)
                    if n is not None:
                        norm(n)
                    tile(t0 // 2, 1, hi, lo, nk)
                    t0 += 2
                with pe.Fori(t0 // 2, t1 // 2) as m:
                    for p_ in range(2):
                        tile(m, p_, hi, lo, nk)

            def norm(n):
                pe.wait_ge(acc_done, KD * (n + 1))
                pe.matmul(MB[:], ccol("mean_d"), acc, start=True, stop=True).then_inc(ss_done, 1)

            def scores(c, p, q_, n, qT, kT):
                a, b = c.ranges(p, n)
                for h in range(2):
                    r = slice(64 * h, 64 * h + 64)
                    if not (isinstance(p, int) and p == 0 and n == 0):
                        pe.wait_ge(c.maxed, 8 * p + 2 * n + h - 1)
                    pe.matmul(SC[h][:, 0:(b - a) * P], qT[r, n * P:(n + 1) * P], kT[r, a * P:b * P],
                              start=True, stop=True).then_inc(c.scored, 1)

            def turn(c, p, n):
                a, b = c.ranges(p, n)
                for h in range(c.halves_out):
                    i = c.halves_out * n + h
                    pe.wait_ge(c.scaled, 4 * c.halves_out * p + i + 1)
                    if not (isinstance(p, int) and p == 0 and i < 2):
                        pe.wait_ge(c.copied, 4 * c.halves_out * p + i - 1)
                    for j in range(b - a):
                        mm = pe.transpose(TR[i % 2][:, j * P:(j + 1) * P], prob[:, n % 2, h, j * P:(j + 1) * P],
                                          ident if c is swa else ccol("flip"))
                    mm.then_inc(c.turned, 1)

            def values(c, p, v, pt):
                pe.wait_ge(c.copied, 4 * c.halves_out * (p + 1))
                if not (isinstance(p, int) and p == 0):
                    pe.wait_ge(c.o_read, p)
                if c is att[0]:
                    for n in range(NQ):
                        a, b = c.ranges(p, n)
                        cols = slice(n * P, (n + 1) * P)
                        for h in range(2):
                            for j in range(b - a):
                                mm = pe.matmul(OB[:, cols], v[:, h, a + j], pt[:, h, j, cols], start=(h == 0 and j == 0),
                                               stop=(h == 1 and j == b - a - 1))
                else:
                    for k in range(NQ):
                        mm = pe.matmul(OB[:], v[:, 0, k], pt[:, 0, k], start=(k == 0), stop=(k == NQ - 1))
                mm.then_inc(c.o_done, 1)

            def swa_values(p, n):
                a, b = swa.ranges(p, n)
                pe.wait_ge(swa.copied, 8 * p + 2 * n + 2)
                if n == 0 and p:
                    pe.wait_ge(swa_lo, p)
                for h in range(2):
                    for j in range(b - a):
                        mm = pe.matmul(OB[:, n * P:(n + 1) * P], v_tok[:, 0, h, a + j], swa_pT[:, n % 2, 2 * h + j],
                                       start=(h == 0 and j == 0), stop=(h == 1 and j == b - a - 1))
                mm.then_inc(swa.pv_done, 1)

            def swa_norm(i):
                pe.wait_ge(swn_sq, i + 1)
                if i >= 2:
                    pe.wait_ge(swn_r, i - 1)
                pe.matmul(SC[i % 2][:], ccol("mean_64"), tmp[:, i % 2], start=True, stop=True).then_inc(swn_ss, 1)

            pe.wait_ge(loaded, 48)
            for b in range(2):
                pe.matmul(SC[b][0:16], pcol("rel_bias")[0:32], bucket[:, b * S:(b + 1) * S], start=True, stop=True)
            mm = pe.matmul(OB[0:16, 0:256], pcol("rel_bias")[0:32], bucket[:, 2048:2304], start=True, stop=True)
            mm.then_inc(tab_mm, 1)

            tile(0, 0, xn_hi, xn_lo, ready=(xn_ready, 0, KD))
            norm(0)
            tile(0, 1, xn_hi, xn_lo)
            pe.wait_ge(glr_split, 2)
            pe.wait_ge(inv_ready, 1)
            n_mm = 0
            for w, mv in ((0, xn_hi), (0, xn_lo), (1, xn_hi)):
                for k in range(KD):
                    mm = pe.matmul(MB[0:32], glr_w[:, w, k * 32:(k + 1) * 32], mv[:, k], start=(n_mm == 0), stop=(n_mm == 23))
                    n_mm += 1
            mm.then_inc(glr_done, 1)
            tile(1, 0, xn_hi, xn_lo)
            pe.wait_ge(glr_read, 1)
            for j in range(2):
                mm = pe.matmul(TR[j][:], pcol("w_alpha")[0:16, j * P:(j + 1) * P], qkv[0:16, 0, 2], start=True, stop=True)
            mm.then_inc(gate_in, 1)
            pe.wait_ge(tab_sb, 3)
            for t in range(3, 8):
                tile(t // 2, t % 2, xn_hi, xn_lo)
                swa_norm(t - 3)
            pe.wait_ge(evac[1], 1)
            for t in range(NQ):
                mm = pe.transpose(MB[:, t * P:(t + 1) * P], z[:, Z_SV, t * P:(t + 1) * P], ident)
            mm.then_inc(swv_t, 1)
            pe.wait_ge(gate_log, 2)
            pe.wait_ge(swn_done, 5)
            for p in range(4):
                a, b = SWA_TILES[p]
                q = z[:, Z_SQ + p]
                scores(swa, p, 0, 0, q, z[:, Z_SK])
                tile(a // 2, a % 2, xn_hi, xn_lo)
                turn(swa, p, 0)
                scores(swa, p, 0, 1, q, z[:, Z_SK])
                if p == 0:
                    pe.wait_ge(swv_done, 1)
                tile((a + 1) // 2, (a + 1) % 2, xn_hi, xn_lo)
                swa_values(p, 0)
                turn(swa, p, 1)
                scores(swa, p, 0, 2, q, z[:, Z_SK])
                if b - a == 3:
                    tile((a + 2) // 2, (a + 2) % 2, xn_hi, xn_lo)
                swa_values(p, 1)
                turn(swa, p, 2)
                scores(swa, p, 0, 3, q, z[:, Z_SK])
                swa_values(p, 2)
                turn(swa, p, 3)
                swa_values(p, 3)

            for h in range(GH + 2):
                bank = (OB, MB)[h % 2]
                if h >= 2:
                    pe.wait_ge(turned_out, h - 1)
                if h == 0:
                    pe.wait_ge(swa_lo, 4)
                if h == GH:
                    pe.wait_ge(gla_keys, 6)
                src = z[:, Z_GV + h] if h < GH else qkv[:, h - GH, 2]
                for t in range(NQ):
                    mm = pe.transpose(bank[:, t * P:(t + 1) * P], src[:, t * P:(t + 1) * P], ident)
                mm.then_inc(turned_in, 1)
            for j in range(2):
                for c in range(NCH - 1):
                    r = slice(64 * (c % 2), 64 * (c % 2) + 64)
                    i = (NCH - 1) * j + c
                    if i == 0:
                        pe.wait_ge(turned_out, GH + 2)
                    if j and c < 2:
                        pe.wait_ge(gla_r, c + 1)
                    if c >= 2 or j:
                        pe.wait_ge(state_out, 2 * (i - 1) if c != 0 else 2 * i)
                    pe.matmul(SC[c % 2][:, 0:256], kd_tok[r, j, c // 2], gv_tok[r, c // 2, 2 * j:2 * j + 2],
                              start=True, stop=True).then_inc(state_in, 1)
                for h in range(2):
                    r = slice(64 * h, 64 * h + 64)
                    if j:
                        pe.wait_ge(gla_masked, h + 1)
                    for t in range(NQ):
                        cols = slice(t * P, (t + 1) * P)
                        mm = pe.matmul(TR[h][:, cols], qkv[r, j, 1, cols], z[r, Z_GQ + j, cols], start=True, stop=True)
                    mm.then_inc(gla_a, 1)
                for h in range(2):
                    r = slice(64 * h, 64 * h + 64)
                    bank = (OB, MB)[h]
                    pe.wait_ge(gla_masked, 2 * j + h + 1)
                    if h == 0:
                        pe.wait_ge(state_out, 2 * (NCH - 1) * (j + 1))
                    if j:
                        pe.wait_ge(gla_t, 2 * (j - 1) + h + 1)
                    for t in range(NQ):
                        pe.matmul(bank[:, t * P:(t + 1) * P], gv_tok[:, t, 2 * j + h], tmp[:, h, t * P:(t + 1) * P],
                                  start=True, stop=False)
                        for c in (2 * t, 2 * t + 1):
                            cols = slice(c * CHUNK, (c + 1) * CHUNK)
                            mm = pe.matmul(bank[:, cols], state[r, j, c], z[r, Z_GQ + j, cols], start=False,
                                           stop=(c == 2 * t + 1))
                    mm.then_inc(gla_o, 1)
                for h in range(2):
                    pe.wait_ge(gla_sq, 2 * j + h + 1)
                    pe.matmul(SC[h][:], ccol("mean_128"), tmp[:, 2], start=True, stop=True).then_inc(gla_ss, 1)

            tile(T_OUT // 2, 0, ff_hi, ff_lo, ready=(gla_lo, 0, GH), order=[4, 5, 6, 7, 0, 1, 2, 3])
            tile(T_OUT // 2, 1, ff_hi, ff_lo)
            tiles(T_OUT + 2, T_MLP1, ff_hi, ff_lo)

            t = T_MLP1
            for n, (a, b) in enumerate(CHUNKS1):
                if n == 0:
                    tiles(t, t + 2 * (b - a), xn_hi, xn_lo, ready=(xn_ready, KD, KD), n=1)
                else:
                    tiles(t, t + 2 * (b - a), xn_hi, xn_lo)
                t += 2 * (b - a)
                with pe.Fori(t // 2, t // 2 + KD // 2) as m:
                    for p_ in range(2):
                        tile(m, p_, ff_hi, ff_lo, b - a, late=(ff_ready, b))
                t += KD

            for l in range(2):
                c = att[l]

                def proj(p, u, j):
                    first = isinstance(p, int) and p == 0 and j == 0
                    tile(*qkv_tile(l, p, u, j), xn_hi, xn_lo, ready=(xn_ready, KD * (2 + 2 * l), KD) if first else None)
                    if first:
                        norm(2 + 2 * l)

                def head_norm(p):
                    pe.wait_ge(post_sq, p + 1)
                    pe.matmul(TR[0][:], ccol("mean_128"), tmp[:, 2], start=True, stop=True).then_inc(post_mm, 1)

                def v_turn(p, u, at_p):
                    m, p_ = qkv_tile(l, at_p, u, 2)
                    pe.wait_ge(evac[p_], m + 1)
                    if not (isinstance(p, int) and p == 0):
                        pe.wait_ge(c.v_ready, p)
                    for t in range(NQ):
                        mm = pe.transpose(MB[:, t * P:(t + 1) * P], qkv[:, u, 2, t * P:(t + 1) * P], ident)
                    mm.then_inc(c.vt_done, 1)

                def pair(p, u, nxt):
                    q, k = qkv[:, u, 0], qkv[:, u, 1]
                    after = l == 1 and not (isinstance(p, int) and p == 0)
                    scores(c, p, u, 0, q, k)
                    if after:
                        head_norm(p - 1)
                    if nxt is not None:
                        proj(nxt, 1 - u, 0)
                    if after:
                        pe.wait_ge(post_r, p)
                    turn(c, p, 0)
                    scores(c, p, u, 1, q, k)
                    if nxt is not None:
                        proj(nxt, 1 - u, 1)
                    turn(c, p, 1)
                    scores(c, p, u, 2, q, k)
                    scores(c, p, u, 3, q, k)
                    if nxt is not None:
                        proj(nxt, 1 - u, 2)
                    turn(c, p, 2)
                    turn(c, p, 3)
                    last_near = l == 0 and isinstance(p, int) and p == NEAR - 1
                    if last_near:
                        pe.wait_ge(grp_d, 5)
                        pe.wait_ge(c.maxed, 8 * NEAR)
                        for n in range(NQ):
                            mm = pe.transpose(SC[1][0:1, n * P:(n + 1) * P], grp[:, 1, n, 0:1], ccol("flip"))
                        mm.then_inc(grp_t, 1)
                    pe.wait_ge(c.v_ready, p + 1)
                    values(c, p, v_tok[:, u], pT)
                    if last_near:
                        pe.wait_ge(grp_row, 1)
                        for n in range(NQ):
                            mm = pe.matmul(SC[0][:, n:n + 1], near_row[:, n * P:(n + 1) * P], ident[0:1, 0:1], start=True,
                                           stop=True)
                        mm.then_inc(grp_t, 1)
                    if nxt is not None:
                        v_turn(p + 1, 1 - u, nxt)

                for j in range(3):
                    proj(0, 0, j)
                v_turn(0, 0, 0)
                pair(0, 0, 1)
                if l == 0:
                    pair(1, 1, 2)
                    pair(2, 0, 3)
                    pe.wait_ge(grp_d, 6)
                with pe.Fori(1 - l, 3) as i:
                    pair(2 * i + 1, 1, (i + 1,))
                    pair(2 * i + 2, 0, (i + 1,))
                pair(7, 1, None)

                if l == 0:
                    pe.wait_ge(grp_d, 14)
                    for n in range(NQ):
                        mm = pe.transpose(MB[0:3, n * P:(n + 1) * P], grp[:, 5, n, :], ccol("flip"))
                    mm.then_inc(grp_t, 1)
                    pe.wait_ge(grp_row, 2)
                    pe.wait_ge(sel_in, 16)
                    for p in range(PAIRS):
                        if p >= 2:
                            pe.wait_ge(gated, p - 1)
                        pe.matmul(SC[p % 2][:], selector[:, p * P:(p + 1) * P], tmp[0:3, 3], start=True,
                                  stop=True).then_inc(gate_mm, 1)
                else:
                    head_norm(PAIRS - 1)
                tiles(T_WO[l], T_MLP2[l], ff_hi, ff_lo, ready=(post_lo, PAIRS * l, KD))
                for n in range(NF2 // KD):
                    t = T_MLP2[l] + 2 * KD * n
                    if n == 0:
                        tiles(t, t + KD, xn_hi, xn_lo, ready=(xn_ready, KD * (3 + 2 * l), KD), n=3 + 2 * l)
                    else:
                        tiles(t, t + KD, xn_hi, xn_lo)
                    with pe.Fori((t + KD) // 2, (t + 2 * KD) // 2) as m:
                        for p_ in range(2):
                            tile(m, p_, ff_hi, ff_lo, late=(ff_ready, NF1 + NF2 * l + KD * (n + 1)))
            norm(6)

        @block.scalar
        def _(act):
            def split_hi(m, p_, first=False):
                act.wait_ge(stage_full[p_], 16 * (m + 1))
                if not first:
                    act.wait_ge(hi_free, 2 * m + p_ - 1)
                act.activation(w_hi[:, p_], stage[:, p_], ACT.Copy).then_inc(hi_ready, 1)

            def split_x(i, k, t0, g0):
                act.wait_ge(evac[k], i + t0 // 2 + 1)
                at_k = bass.ds(2 * i + k, 1)
                xk = x[:, at_k].rearrange("p o s -> p (o s)")
                if g0 is not None:
                    act.activation(xn_hi[:, at_k].rearrange("p o s -> p (o s)"), xk, ACT.Copy,
                                   scale=par[:, bass.ds(2 * i + g0 + k, 1)]).then_inc(xh_ready, 1)
                act.activation(tmp[:, k], xk, ACT.Square).then_inc(sq_ready, 1)

            def splits_x(t0, name):
                if name == "final":
                    with act.Fori(0, KD // 2 - 1) as i:
                        for p_ in range(2):
                            split_hi(i + t0 // 2 + 1, p_)
                            split_x(i, p_, t0, None)
                    for p_ in range(2):
                        split_x(KD // 2 - 1, p_, t0, None)
                    return
                with act.Fori(0, KD // 2) as i:
                    for p_ in range(2):
                        split_hi(i + t0 // 2 + 1, p_)
                        split_x(i, p_, t0, _cols[name][0])

            def splits(t0, t1):
                with act.Fori(t0 // 2, t1 // 2) as m:
                    for p_ in range(2):
                        split_hi(m + 1, p_)

            def rsqrt(bank, done):
                link("act", act, act.activation(rstd_h[:], bank[:], ACT.Ln, bias=eps_col))
                act.activation(rstd_h[:], rstd_h[:], ACT.Exp, scale=-0.5).then_inc(done, 1)

            def root(n):
                act.wait_ge(inv_ready, n + 1)
                act.activation(rstd[:], rstd[:], ACT.Sqrt).then_inc(rstd_ready, 1)

            def exps(c, p, q_, n, sink=None):
                a, b = c.ranges(p, n)
                for h in range(2):
                    s = 2 * n + h
                    act.wait_ge(c.negated, 8 * p + s + 1)
                    if sink is not None:
                        act.activation(es[:, q_, s:s + 1], nm[:, q_, s:s + 1], ACT.Exp, bias=sink(h))
                    pr = prob[:, n % 2, h, 0:(b - a) * P]
                    act.activation(pr, pr, ACT.Exp, bias=nm[:, q_, s:s + 1],
                                   accum_out=sm[:, q_, s:s + 1]).then_inc(c.expd, 1)

            def copies(c, p, n, pt):
                a, b = c.ranges(p, n)
                for h in range(c.halves_out):
                    i = c.halves_out * n + h
                    act.wait_ge(c.turned, 4 * c.halves_out * p + i + 1)
                    if c is swa:
                        if h == 0 and 4 * p + n >= 2:
                            act.wait_ge(c.pv_done, 4 * p + n - 1)
                        dst = swa_pT[:, n % 2, 2 * h:2 * h + b - a]
                    else:
                        if i == 0 and not (isinstance(p, int) and p == 0):
                            act.wait_ge(c.o_done, p)
                        dst = pt[:, h, 0:b - a, n * P:(n + 1) * P]
                    act.activation(dst,
                                   TR[i % 2][:, 0:(b - a) * P].rearrange("p (k s) -> p k s", k=b - a),
                                   ACT.Copy).then_inc(c.copied, 1)

            def swa_square(i):
                t = i + 1 if i else 0
                act.wait_ge(evac[t % 2], t // 2 + 1)
                act.activation(tmp[:, i % 2], z[:, t], ACT.Square).then_inc(swn_sq, 1)

            act.wait_ge(loaded, 48)
            act.wait_ge(const_ready, 2)
            for k in range(KD):
                if k % 4 == 0:
                    act.wait_ge(x_in_done[k // 4], 16)
                act.activation(xn_hi[:, k], x[:, k], ACT.Copy, scale=pcol("mix_norm", k, k + 1)).then_inc(xh_ready, 1)
                if k >= 2:
                    act.wait_ge(acc_done, k - 1)
                act.activation(tmp[:, k % 2], x[:, k], ACT.Square).then_inc(sq_ready, 1)
                if k < 2:
                    split_hi(0, k, True)
            act.activation(glr_w[:, 0], pcol("w_glr"), ACT.Copy).then_inc(glr_split, 1)
            act.wait_ge(tab_sb, 3)
            for l in range(2):
                act.dma_start(tables[l], table_sb[:, l, :]).then_inc(tables_saved, 16)
            act.dma_start(tables[2], class_sb).then_inc(tables_saved, 16)
            root(0)
            for t in range(3):
                split_hi(t // 2 + 1, t % 2)
            act.wait_ge(gate_in, 1)
            for j in range(2):
                act.wait_ge(gate_abs, j + 1)
                link("act", act, act.activation(qkv[:, j, 1], TR[j][:], ACT.Abs, bias=pcol("b_alpha", j, j + 1)))
                link("act", act, act.activation(qkv[:, j, 1], qkv[:, j, 1], ACT.Exp, scale=-1.0))
                act.activation(qkv[:, j, 1], qkv[:, j, 1], ACT.Ln, bias=1.0).then_inc(gate_log, 1)
            for i in range(5):
                split_hi((i + 3) // 2 + 1, (i + 3) % 2)
                swa_square(i)
                act.wait_ge(swn_ss, i + 1)
                if i:
                    act.wait_ge(swn_done, i)
                rsqrt(SC[i % 2], swn_r)
            act.wait_ge(tables_saved, 48)
            act.wait_ge(lam_sum, 1)
            act.activation(lam_s[:, 2:4], lam_s[:, 0:2], ACT.Exp).then_inc(lam_exp, 1)
            for j in range(2):
                act.wait_ge(decay_sum, j + 1)
                last = qkv[:, j, 0].rearrange("p (c t) -> p c t", t=CHUNK)[:, :, CHUNK - 1]
                act.activation(decay[:, j], last, ACT.Exp, scale=1.0 / 16)
                act.activation(qkv[:, j, 1], qkv[:, j, 0], ACT.Exp, scale=-1.0 / 16)
                act.activation(tmp[:, 2 + j], qkv[:, j, 0], ACT.Exp, scale=1.0 / 16).then_inc(decay_exp, 1)
                act.wait_ge(decay_diff, j + 1)
                act.activation(qkv[:, j, 2], qkv[:, j, 2], ACT.Exp, scale=1.0 / 16).then_inc(key_exp, 1)
            for p in range(4):
                a, b = SWA_TILES[p]

                def sink(h, p=p):
                    return pcol("sinks", 2 * p + h, 2 * p + h + 1)
                exps(swa, p, 0, 0, sink)
                split_hi(a // 2 + 1, a % 2)
                copies(swa, p, 0, None)
                exps(swa, p, 0, 1, sink)
                split_hi((a + 1) // 2 + 1, (a + 1) % 2)
                copies(swa, p, 1, None)
                exps(swa, p, 0, 2, sink)
                if b - a == 3:
                    split_hi((a + 2) // 2 + 1, (a + 2) % 2)
                copies(swa, p, 2, None)
                exps(swa, p, 0, 3, sink)
                copies(swa, p, 3, None)
                act.wait_ge(swa.pv_done, 4 * p + 4)
                act.activation(ff_hi[:, GH + p], OB[:], ACT.Copy).then_inc(swa_hi, 1)
            for p_ in range(2):
                act.wait_ge(evac[p_], T_OUT // 2)
            for h in range(GH):
                act.activation(z[:, Z_GR + h], z[:, Z_GR + h], ACT.Silu).then_inc(gates_on, 1)
            for j in range(2):
                for h in range(2):
                    act.wait_ge(gla_o, 2 * j + h + 1)
                    if h or j:
                        act.wait_ge(gla_ss, 2 * j + h)
                    act.activation(tmp[:, 2], (OB, MB)[h][:], ACT.Square).then_inc(gla_sq, 1)
                    act.wait_ge(gla_ss, 2 * j + h + 1)
                    rsqrt(SC[h], gla_r)
                    act.wait_ge(gla_t, 2 * j + h + 1)
                    act.activation(ff_hi[:, 2 * j + h], tmp[:, 3], ACT.Copy).then_inc(gla_hi, 1)
            act.wait_ge(gla_lo, GH)
            splits_x(T_OUT, "ffn_norm")
            root(1)
            t = T_MLP1
            for a, b in CHUNKS1:
                with act.Fori(0, b - a) as i:
                    f, m = i + a, i + t // 2
                    for p_ in range(2):
                        split_hi(m + 1, p_)
                        act.wait_ge(evac[p_], m + 1)
                        if p_ == 0:
                            act.wait_ge(ff_ready, f)
                        w2 = par[:, bass.ds(_cols["conv_w"][0] + 4 * NF1 + 2 * f + p_, 1)]
                        bc = par[:, bass.ds(_cols["conv_b"][0] + 2 * f + p_, 1)]
                        act.activation(tmp[:, p_], tmp[:, 2 + p_], ACT.Identity, bias=bc, scale=w2).then_inc(conv_0, 1)
                    act.wait_ge(conv_2, 2 * f + 1)
                    act.activation(tmp[:, 0], tmp[:, 0], ACT.Silu).then_inc(silu_done, 1)
                    act.wait_ge(f_made, f + 1)
                    act.activation(ff_hi[:, bass.ds(i, 1)].rearrange("p o s -> p (o s)"), tmp[:, 1],
                                   ACT.Copy).then_inc(ffh_ready, 1)
                t += 2 * (b - a)
                if b < NF1:
                    splits(t, t + KD)
                else:
                    splits_x(t, "mix2a")
                t += KD

            for l in range(2):
                c = att[l]
                root(2 + 2 * l)

                def proj(p, u, j):
                    m, p_ = qkv_tile(l, p, u, j)
                    split_hi(m + 1, p_)

                def square(p):
                    act.wait_ge(c.o_done, p + 1)
                    act.activation(tmp[:, 2], OB[:], ACT.Square).then_inc(post_sq, 1)

                def head_norm(p):
                    act.wait_ge(post_mm, p + 1)
                    if not (isinstance(p, int) and p == 0):
                        act.wait_ge(post_t, p)
                    act.activation(rstd_h[:], TR[0][:], ACT.Ln, bias=eps_col).then_inc(post_ln, 1)
                    act.wait_ge(post_ln, p + 1)
                    act.activation(rstd_h[:], rstd_h[:], ACT.Exp, scale=-0.5).then_inc(post_r, 1)

                def high(p):
                    act.wait_ge(post_t, p + 1)
                    act.activation(ff_hi[:, bass.ds(p, 1)].rearrange("p o s -> p (o s)"), tmp[:, 0],
                                   ACT.Copy).then_inc(post_hi, 1)

                def group_sums(g0, g1, d0):
                    a, b = GROUPS[g0][0], GROUPS[g1 - 1][1]
                    act.wait_ge(c.lse_kept, b)
                    act.activation(lse_sm[:, a // 2:b // 2], lse_sm[:, a // 2:b // 2], ACT.Ln).then_inc(grp_a, 1)
                    act.wait_ge(grp_d, d0 + 3)
                    act.activation(lhe[:, 1, :, a:b], lhe[:, 1, :, a:b], ACT.Exp).then_inc(grp_a, 1)
                    act.wait_ge(grp_d, d0 + 4)
                    act.activation(grp[:, 1, :, g0:g1], grp[:, 1, :, g0:g1], ACT.Ln).then_inc(grp_a, 1)

                def pair(p, u, nxt):
                    exps(c, p, u, 0)
                    after = l == 1 and not (isinstance(p, int) and p == 0)
                    if after:
                        head_norm(p - 1)
                    if nxt is not None:
                        proj(nxt, 1 - u, 0)
                    copies(c, p, 0, pT)
                    exps(c, p, u, 1)
                    if after:
                        high(p - 1)
                    if nxt is not None:
                        proj(nxt, 1 - u, 1)
                    copies(c, p, 1, pT)
                    exps(c, p, u, 2)
                    exps(c, p, u, 3)
                    if nxt is not None:
                        proj(nxt, 1 - u, 2)
                    if l == 0 and isinstance(p, int) and p == NEAR - 1:
                        group_sums(0, 1, 0)
                    copies(c, p, 2, pT)
                    copies(c, p, 3, pT)
                    if l == 1:
                        square(p)

                for j in range(3):
                    proj(0, 0, j)
                pair(0, 0, 1)
                if l == 0:
                    pair(1, 1, 2)
                    pair(2, 0, 3)
                with act.Fori(1 - l, 3) as i:
                    pair(2 * i + 1, 1, (i + 1,))
                    pair(2 * i + 2, 0, (i + 1,))
                pair(7, 1, None)
                if l == 0:
                    group_sums(1, 3, 6)
                    act.wait_ge(grp_d, 12)
                    act.activation(grp[:, 2], grp[:, 2], ACT.Exp).then_inc(grp_a, 1)
                    for p in range(PAIRS):
                        act.wait_ge(gated, p + 1)
                        act.activation(ff_hi[:, p], tmp[:, p % 2], ACT.Copy).then_inc(gate_hi, 1)
                else:
                    head_norm(PAIRS - 1)
                    high(PAIRS - 1)
                splits_x(T_WO[l], ("mlp2a", "mlp2b")[l])
                root(3 + 2 * l)
                for n in range(NF2 // KD):
                    t = T_MLP2[l] + 2 * KD * n
                    f0 = NF2 * l + KD * n
                    with act.Fori(0, KD // 2) as i:
                        for p_ in range(2):
                            split_hi(i + t // 2 + 1, p_)
                            act.wait_ge(tile_done, 2 * i + t + p_ + 1)
                            act.wait_ge(ff_ready, 2 * i + f0 + NF1 + p_ - 1)
                            act.activation(tmp[:, p_], G[p_][:], ACT.Relu).then_inc(evac[p_], 1)
                            act.wait_ge(u_ready, 2 * i + f0 + p_ + 1)
                            act.activation(ff_hi[:, bass.ds(2 * i + p_, 1)].rearrange("p o s -> p (o s)"), tmp[:, 2 + p_],
                                           ACT.Square).then_inc(ffh_ready, 1)
                    t += KD
                    if n < NF2 // KD - 1:
                        splits(t, t + KD)
                    else:
                        splits_x(t, ("mix2b", "final")[l])
            root(6)

        @block.vector
        def _(dve):
            def add_tiles(t0):
                with dve.Fori(0, KD // 2) as i:
                    for p_ in range(2):
                        dve.wait_ge(tile_done, 2 * i + t0 + p_ + 1)
                        xs = x[:, bass.ds(2 * i + p_, 1)].rearrange("p o s -> p (o s)")
                        dve.tensor_tensor(xs, xs, G[p_][:], ALU.add).then_inc(evac[p_], 1)

            def low_x(i, k, n, g0):
                at_k = bass.ds(2 * i + k, 1)
                if g0 is not None:
                    dve.wait_ge(xh_ready, 2 * i + KD * n + k + 1)
                    dve.scalar_tensor_tensor(out=xn_lo[:, at_k].rearrange("p o s -> p (o s)"),
                                             in0=x[:, at_k].rearrange("p o s -> p (o s)"),
                                             scalar=par[:, bass.ds(2 * i + g0 + k, 1)],
                                             in1=xn_hi[:, at_k].rearrange("p o s -> p (o s)").bitcast(F32),
                                             op0=ALU.mult, op1=ALU.subtract).then_inc(xn_ready, 1)
                dve.wait_ge(sq_ready, 2 * i + KD * n + k + 1)
                if not (isinstance(i, int) and n == 0 and i == 0 and k == 0):
                    dve.wait_ge(acc_done, 2 * i + KD * n + k)
                dve.tensor_tensor(acc, acc, tmp[:, k], ALU.add).then_inc(acc_done, 1)

            def add_tiles_x(t0, n, name):
                dve.memset(acc, 0.0).then_inc(acc_zero, 1)
                dve.wait_ge(acc_zero, n + 1)
                with dve.Fori(0, KD // 2) as i:
                    for p_ in range(2):
                        dve.wait_ge(tile_done, 2 * i + t0 + p_ + 1)
                        xs = x[:, bass.ds(2 * i + p_, 1)].rearrange("p o s -> p (o s)")
                        dve.tensor_tensor(xs, xs, G[p_][:], ALU.add).then_inc(evac[p_], 1)
                        low_x(i, p_, n, None if name == "final" else _cols[name][0])
                inverse(n)

            def inverse(n):
                dve.wait_ge(ss_done, n + 1)
                dve.tensor_scalar(rstd[:], MB[:], EPS, None, ALU.add).then_inc(eps_added, 1)
                dve.wait_ge(eps_added, n + 1)
                dve.reciprocal(rstd[:], rstd[:]).then_inc(inv_ready, 1)

            def maxima(c, p, q_, n, sink=None):
                a, b = c.ranges(p, n)
                w = (b - a) * P
                off = (a - n + NQ - 1) * P
                ho = c.halves_out
                for h in range(2):
                    s = 2 * n + h
                    dve.wait_ge(c.scored, 8 * p + s + 1)
                    if not (isinstance(p, int) and p == 0 and n < 2):
                        dve.wait_ge(c.turned, ho * (4 * p + n - 2) + min(h, ho - 1) + 1)
                    dve.memset(small[:, 104 + 8 * q_ + s:105 + 8 * q_ + s], 0.0)
                    dve.tensor_tensor_reduce(out=prob[:, n % 2, h, 0:w], in0=SC[h][:, 0:w],
                                             in1=bias[:, c.parity(q_, p), h, off:off + w], scale=1.0, scalar=-3e38,
                                             op0=ALU.add, op1=ALU.max,
                                             accum_out=mx[:, q_, s:s + 1]).then_inc(c.maxed, 1)
                for h in range(2):
                    s = 2 * n + h
                    dve.wait_ge(c.maxed, 8 * p + s + 1)
                    if sink is None:
                        ins = dve.tensor_scalar(nm[:, q_, s:s + 1], mx[:, q_, s:s + 1], -1.0, None, ALU.mult)
                    else:
                        ins = dve.tensor_scalar(nm[:, q_, s:s + 1], mx[:, q_, s:s + 1], sink(h), -1.0, ALU.max, ALU.mult)
                    ins.then_inc(c.negated, 1)

            def scale(c, p, q_, n, sink=None):
                a, b = c.ranges(p, n)
                s = slice(2 * n, 2 * n + 2)
                per = {swa: 2, att[0]: 1, att[1]: 3}[c]
                base = per * (4 * p + n)
                dve.wait_ge(c.expd, 8 * p + 2 * n + 2)
                if sink is not None:
                    dve.tensor_tensor(sm[:, q_, s], sm[:, q_, s], es[:, q_, s], ALU.add).then_inc(c.recd, 1)
                    dve.wait_ge(c.recd, base + 1)
                dve.reciprocal(rc[:, q_, s], sm[:, q_, s]).then_inc(c.recd, 1)
                dve.wait_ge(c.recd, base + (2 if sink is not None else 1))
                pr = [prob[:, n % 2, h, 0:(b - a) * P] for h in range(2)]
                rs = [rc[:, q_, 2 * n + h:2 * n + h + 1] for h in range(2)]
                if c is att[1]:
                    dve.tensor_scalar(rs[1], rs[1], neg_lam, None, ALU.mult).then_inc(c.recd, 1)
                    dve.tensor_scalar(pr[0], pr[0], rs[0], None, ALU.mult).then_inc(c.recd, 1)
                    dve.wait_ge(c.recd, base + 3)
                    dve.scalar_tensor_tensor(out=pr[0], in0=pr[1], scalar=rs[1], in1=pr[0], op0=ALU.mult,
                                             op1=ALU.add).then_inc(c.scaled, 1)
                else:
                    for h in range(2):
                        dve.tensor_scalar(pr[h], pr[h], rs[h], None, ALU.mult).then_inc(c.scaled, 1)

            def dlink(ins):
                link("dve", dve, ins)

            dve.memset(small[:, 0:96], 0.0)
            dve.memset(small[:, 96:128], EPS).then_inc(const_ready, 1)
            dve.memset(v_tok[:], 0.0).then_inc(const_ready, 1)
            dve.memset(acc, 0.0).then_inc(acc_zero, 1)
            dve.wait_ge(const_ready, 2)
            dve.wait_ge(acc_zero, 1)
            dve.wait_ge(loaded, 48)
            for k in range(KD):
                if k % 4 == 0:
                    dve.wait_ge(x_in_done[k // 4], 16)
                low_x(k // 2, k % 2, 0, _cols["mix_norm"][0])
            dve.wait_ge(glr_split, 1)
            dve.tensor_tensor(glr_w[:, 1], pcol("w_glr"), glr_w[:, 0].bitcast(F32), ALU.subtract).then_inc(glr_split, 1)
            dve.wait_ge(tab_mm, 1)
            for b in range(2):
                dve.tensor_copy(table_sb[:, 1, b * S:(b + 1) * S], SC[b][0:16])
                ins = dve.tensor_tensor(table_sb[:, 0, b * S:(b + 1) * S], SC[b][0:16],
                                        bucket[0:16, 1024 + b * S:1024 + (b + 1) * S], ALU.add)
                ins.then_inc(tab_sb, 1)
            dve.tensor_tensor(class_sb, OB[0:16, 0:256], bucket[0:16, 2304:2560], ALU.add).then_inc(tab_sb, 1)
            inverse(0)
            dve.tensor_scalar(pcol("q_norm"), pcol("q_norm"), 0.125, None, ALU.mult)
            dve.tensor_scalar(pcol("subln"), pcol("subln"), 1.0 - LAMBDA_INIT, None, ALU.mult)
            lam = pcol("lam").rearrange("p (i d) -> p i d", i=4)
            lam_prod = lhe[:].rearrange("p a n h -> p (a n h)").rearrange("p (i d) -> p i d", i=2)
            dlink(dve.tensor_tensor(lam_prod, lam[:, 0::2], lam[:, 1::2], ALU.mult))
            dve.tensor_reduce(lam_s[:, 0:2], lam_prod, mybir.AxisListType.X, ALU.add).then_inc(lam_sum, 1)

            def project(t):
                dve.wait_ge(tile_done, t + 1)
                dve.tensor_tensor(z[:, t], G[t % 2][:], rstd[:], ALU.mult).then_inc(evac[t % 2], 1)

            def swa_norm(i):
                dve.wait_ge(swn_r, i + 1)
                zi = z[:, i + 1 if i else 0]
                g = pcol("k_norm") if i == 0 else pcol("q_norm")
                dve.scalar_tensor_tensor(out=zi, in0=zi, scalar=g, in1=rstd_h[:], op0=ALU.mult, op1=ALU.mult).then_inc(swn_done, 1)

            dve.wait_ge(rstd_ready, 1)
            project(0)
            project(1)
            dve.wait_ge(glr_done, 1)
            dve.tensor_tensor(qkv[0:16, 0, 2], MB[0:16], rstd[0:16], ALU.mult).then_inc(glr_read, 1)
            project(2)
            dve.wait_ge(gate_in, 1)
            for j in range(2):
                b = pcol("b_alpha", j, j + 1)
                dve.tensor_scalar(qkv[:, j, 0], TR[j][:], b, 0.0, ALU.add, ALU.min).then_inc(gate_abs, 1)
            project(3)
            for j in range(2):
                dve.wait_ge(gate_log, j + 1)
                dlink(dve.tensor_tensor(qkv[:, j, 1], qkv[:, j, 0], qkv[:, j, 1], ALU.subtract))
                dve.tensor_tensor_scan(qkv[:, j, 0], ccol("reset"), qkv[:, j, 1], 0.0, ALU.mult, ALU.add).then_inc(decay_sum, 1)
                dve.wait_ge(decay_sum, j + 1)
                v = qkv[:, j, 0].rearrange("p (c t) -> p c t", t=CHUNK)
                dve.tensor_tensor(qkv[:, j, 2].rearrange("p (c t) -> p c t", t=CHUNK),
                                  v[:, :, CHUNK - 1:CHUNK].broadcast_to([P, NCH, CHUNK]), v, ALU.subtract).then_inc(decay_diff, 1)
            for t in range(4, 8):
                swa_norm(t - 4)
                project(t)
            swa_norm(4)
            dve.wait_ge(swv_t, 1)
            vt = MB[:].rearrange("p (t f) -> p t f", t=NQ)
            dve.tensor_copy(v_tok[:, 0, 0, :, 0:64], vt[:, :, 0:64])
            dve.tensor_copy(v_tok[:, 0, 1, :, 64:128], vt[:, :, 64:128]).then_inc(swv_done, 1)
            dve.wait_ge(tables_saved, 48)
            for p in range(4):
                a, b = SWA_TILES[p]

                def sink(h, p=p):
                    return pcol("sinks", 2 * p + h, 2 * p + h + 1)
                dve.wait_ge(bias_in[p % 2], 16 * (p // 2 + 1))
                maxima(swa, p, 0, 0, sink)
                scale(swa, p, 0, 0, sink)
                project(a)
                maxima(swa, p, 0, 1, sink)
                scale(swa, p, 0, 1, sink)
                project(a + 1)
                maxima(swa, p, 0, 2, sink)
                scale(swa, p, 0, 2, sink)
                if b - a == 3:
                    project(a + 2)
                maxima(swa, p, 0, 3, sink)
                scale(swa, p, 0, 3, sink)
                dve.wait_ge(swa_hi, p + 1)
                dve.tensor_tensor(ff_lo[:, GH + p], OB[:], ff_hi[:, GH + p].bitcast(F32), ALU.subtract).then_inc(swa_lo, 1)
            dve.wait_ge(lam_exp, 1)
            dlink(dve.tensor_tensor(neg_lam, lam_s[:, 3:4], lam_s[:, 2:3], ALU.subtract))
            dlink(dve.tensor_scalar(neg_lam, neg_lam, -LAMBDA_INIT, None, ALU.add))
            for h in range(GH):
                dve.wait_ge(turned_in, h + 1)
                dve.tensor_copy(gv_tok[:, :, h], (OB, MB)[h % 2][:].rearrange("p (t f) -> p t f", t=NQ)).then_inc(turned_out, 1)
            for j in range(2):
                dve.wait_ge(decay_exp, j + 1)
                dve.scalar_tensor_tensor(out=z[:, Z_GQ + j], in0=z[:, Z_GQ + j], scalar=0.125, in1=tmp[:, 2 + j],
                                         op0=ALU.mult, op1=ALU.mult).then_inc(gla_keys, 1)
                dve.tensor_tensor(qkv[:, j, 1], z[:, Z_GK + j], qkv[:, j, 1], ALU.mult).then_inc(gla_keys, 1)
                dve.wait_ge(key_exp, j + 1)
                dve.tensor_tensor(qkv[:, j, 2], z[:, Z_GK + j], qkv[:, j, 2], ALU.mult).then_inc(gla_keys, 1)
            for j in range(2):
                dve.wait_ge(turned_in, GH + j + 1)
                dve.tensor_copy(kd_tok[:, j], (OB, MB)[j][:].rearrange("p (t f) -> p t f", t=NQ)).then_inc(turned_out, 1)
            for j in range(2):
                dlink(dve.memset(state[:, j, 0], 0.0))
                for c in range(NCH - 1):
                    i = (NCH - 1) * j + c
                    dve.wait_ge(state_in, i + 1)
                    if i:
                        dve.wait_ge(state_out, 2 * i)
                    for h in range(2):
                        r = slice(64 * h, 64 * h + 64)
                        dve.scalar_tensor_tensor(out=state[r, j, c + 1], in0=state[r, j, c], scalar=decay[r, j, c:c + 1],
                                                 in1=SC[c % 2][r, P * h:P * h + P], op0=ALU.mult,
                                                 op1=ALU.add).then_inc(state_out, 1)
                for h in range(2):
                    dve.wait_ge(gla_a, 2 * j + h + 1)
                    if j:
                        dve.wait_ge(gla_o, h + 1)
                    dve.tensor_tensor(tmp[:, h].rearrange("p (t s) -> p t s", t=NQ), TR[h][:].rearrange("p (t s) -> p t s", t=NQ),
                                      ccol("gla_mask").rearrange("p (o s) -> p o s", o=1).broadcast_to([P, NQ, P]),
                                      ALU.mult).then_inc(gla_masked, 1)
                for h in range(2):
                    i = 2 * j + h
                    o = (OB, MB)[h]
                    dve.wait_ge(gla_r, i + 1)
                    if i:
                        dve.wait_ge(gla_lo, i)
                    dlink(dve.scalar_tensor_tensor(out=tmp[:, 3], in0=o[:], scalar=pcol("gla_norm"), in1=rstd_h[:],
                                                   op0=ALU.mult, op1=ALU.mult))
                    dve.wait_ge(gates_on, i + 1)
                    dve.tensor_tensor(tmp[:, 3], tmp[:, 3], z[:, Z_GR + i], ALU.mult).then_inc(gla_t, 1)
                    dve.wait_ge(gla_hi, i + 1)
                    dve.tensor_tensor(ff_lo[:, i], tmp[:, 3], ff_hi[:, i].bitcast(F32), ALU.subtract).then_inc(gla_lo, 1)

            dve.memset(v_tok[:, 1], 0.0)
            add_tiles_x(T_OUT, 1, "ffn_norm")
            dve.wait_ge(rstd_ready, 2)
            t = T_MLP1
            for a, b in CHUNKS1:
                with dve.Fori(0, b - a) as i:
                    f, m = i + a, i + t // 2
                    for p_ in range(2):
                        cs = [par[:, bass.ds(_cols["conv_w"][0] + 2 * NF1 * j + 2 * f + p_, 1)] for j in range(2)]
                        u = tmp[:, 2 + p_]
                        dve.wait_ge(tile_done, 2 * m + p_ + 1)
                        dve.tensor_tensor(u, G[p_][:], rstd[:], ALU.mult).then_inc(evac[p_], 1)
                        dve.wait_ge(conv_0, 2 * f + p_ + 1)
                        dve.scalar_tensor_tensor(out=tmp[:, p_, 1:S], in0=u[:, 0:S - 1], scalar=cs[1], in1=tmp[:, p_, 1:S],
                                                 op0=ALU.mult, op1=ALU.add).then_inc(conv_1, 1)
                        dve.wait_ge(conv_1, 2 * f + p_ + 1)
                        dve.scalar_tensor_tensor(out=tmp[:, p_, 2:S], in0=u[:, 0:S - 2], scalar=cs[0], in1=tmp[:, p_, 2:S],
                                                 op0=ALU.mult, op1=ALU.add).then_inc(conv_2, 1)
                    dve.wait_ge(silu_done, f + 1)
                    dve.wait_ge(conv_2, 2 * f + 2)
                    dve.tensor_tensor(tmp[:, 1], tmp[:, 0], tmp[:, 1], ALU.mult).then_inc(f_made, 1)
                    dve.wait_ge(ffh_ready, f + 1)
                    dve.tensor_tensor(ff_lo[:, bass.ds(i, 1)].rearrange("p o s -> p (o s)"), tmp[:, 1],
                                      ff_hi[:, bass.ds(i, 1)].rearrange("p o s -> p (o s)").bitcast(F32),
                                      ALU.subtract).then_inc(ff_ready, 1)
                t += 2 * (b - a)
                if b < NF1:
                    add_tiles(t)
                else:
                    add_tiles_x(t, 2, "mix2a")
                t += KD

            for l in range(2):
                c = att[l]
                dve.wait_ge(rstd_ready, 3 + 2 * l)

                def project(p, u, j):
                    m, p_ = qkv_tile(l, p, u, j)
                    dve.wait_ge(tile_done, 2 * m + p_ + 1)
                    dst = qkv[:, u, j].rearrange("p (n s) -> p n s", n=NQ)
                    order = "p (n s) -> p n s" if l == 1 or near(p) else "p (s n) -> p n s"
                    src, rs = G[p_][:].rearrange(order, n=NQ), rstd[:].rearrange(order, n=NQ)
                    if j == 0:
                        dst = dst[:, :, ::-1]
                    dve.scalar_tensor_tensor(out=dst, in0=src, scalar=(0.125 if j == 0 else 1.0), in1=rs, op0=ALU.mult,
                                             op1=ALU.mult).then_inc(evac[p_], 1)

                def head_out(p):
                    dve.wait_ge(post_r, p + 1)
                    if not (isinstance(p, int) and p == 0):
                        dve.wait_ge(post_lo, p + PAIRS)
                    dve.scalar_tensor_tensor(out=tmp[:, 0], in0=OB[:], scalar=pcol("subln"), in1=rstd_h[:],
                                             op0=ALU.mult, op1=ALU.mult).then_inc(post_t, 1)

                def head_low(p):
                    dve.wait_ge(post_hi, p + 1)
                    at_p = bass.ds(p, 1)
                    dve.tensor_tensor(ff_lo[:, at_p].rearrange("p o s -> p (o s)"), tmp[:, 0],
                                      ff_hi[:, at_p].rearrange("p o s -> p (o s)").bitcast(F32),
                                      ALU.subtract).then_inc(post_lo, 1)

                def v_copy(p, u):
                    dve.wait_ge(c.vt_done, p + 1)
                    if not (isinstance(p, int) and p < 2):
                        dve.wait_ge(c.o_done, p - 1)
                    vt = MB[:].rearrange("p (t f) -> p t f", t=NQ)
                    if l == 0:
                        dve.tensor_copy(v_tok[:, u, 0, :, 0:64], vt[:, :, 0:64])
                        ins = dve.tensor_copy(v_tok[:, u, 1, :, 64:128], vt[:, :, 64:128])
                    else:
                        ins = dve.tensor_copy(v_tok[:, u, 0], vt)
                    ins.then_inc(c.v_ready, 1)

                def group_sums(g0, g1, a0):
                    ha, hb = GROUPS[g0][0], GROUPS[g1 - 1][1]
                    pa, pb = ha // 2, hb // 2
                    gs = list(enumerate(GROUPS))[g0:g1]
                    dve.wait_ge(grp_a, a0 + 1)
                    dlink(dve.tensor_tensor(lse_sm[:, pa:pb], lse_sm[:, pa:pb], lse_nm[:, pa:pb], ALU.subtract))
                    dve.tensor_copy(lhe[:, 0, :, ha:hb].rearrange("p n (q h) -> p q n h", h=2),
                                    lse_sm[:, pa:pb].rearrange("p q (n h) -> p q n h", h=2)).then_inc(grp_d, 1)
                    dve.wait_ge(grp_d, 2 * a0 + 1)
                    for g, (a, b) in gs:
                        ins = dve.tensor_reduce(grp[:, 0, :, g:g + 1].rearrange("p n o -> p (n o)"), lhe[:, 0, :, a:b],
                                                mybir.AxisListType.X, ALU.max)
                    ins.then_inc(grp_d, 1)
                    dve.wait_ge(grp_d, 2 * a0 + 2)
                    for g, (a, b) in gs:
                        ins = dve.tensor_tensor(lhe[:, 1, :, a:b], lhe[:, 0, :, a:b],
                                                grp[:, 0, :, g:g + 1].broadcast_to([P, NQ, b - a]), ALU.subtract)
                    ins.then_inc(grp_d, 1)
                    dve.wait_ge(grp_a, a0 + 2)
                    for g, (a, b) in gs:
                        ins = dve.tensor_reduce(grp[:, 1, :, g:g + 1].rearrange("p n o -> p (n o)"), lhe[:, 1, :, a:b],
                                                mybir.AxisListType.X, ALU.add)
                    ins.then_inc(grp_d, 1)
                    dve.wait_ge(grp_a, a0 + 3)
                    dlink(dve.tensor_tensor(grp[:, 1, :, g0:g1], grp[:, 1, :, g0:g1], grp[:, 0, :, g0:g1], ALU.add))
                    for g, (a, b) in gs:
                        ins = dve.tensor_scalar(grp[:, 1, :, g:g + 1], grp[:, 1, :, g:g + 1], -math.log(b - a), None, ALU.add)
                    return ins

                def pair(p, u, nxt):
                    dve.wait_ge(bias_in[u], 16 * (2 + 4 * l) + (16 * (p // 2 + 1) if isinstance(p, int) else 16 * nxt_of(p, u)))
                    after = l == 1 and not (isinstance(p, int) and p == 0)
                    maxima(c, p, u, 0)
                    scale(c, p, u, 0)
                    if after:
                        head_out(p - 1)
                    if nxt is not None:
                        project(nxt, 1 - u, 0)
                    maxima(c, p, u, 1)
                    scale(c, p, u, 1)
                    if after:
                        head_low(p - 1)
                    if nxt is not None:
                        project(nxt, 1 - u, 1)
                    maxima(c, p, u, 2)
                    maxima(c, p, u, 3)
                    scale(c, p, u, 2)
                    scale(c, p, u, 3)
                    last_near = l == 0 and isinstance(p, int) and p == NEAR - 1
                    if l == 0:
                        at_p = bass.ds(p, 1)
                        dve.tensor_copy(lse_nm[:, at_p].rearrange("p o s -> p (o s)"), nm[:, u]).then_inc(c.lse_kept, 1)
                        dve.tensor_copy(lse_sm[:, at_p].rearrange("p o s -> p (o s)"), sm[:, u]).then_inc(c.lse_kept, 1)
                    if last_near:
                        group_sums(0, 1, 0).then_inc(grp_d, 1)
                    if nxt is not None:
                        project(nxt, 1 - u, 2)
                    if last_near:
                        dve.wait_ge(grp_t, 1)
                        dve.tensor_copy(near_row.rearrange("p (n s) -> p n s", n=NQ)[:, :, ::-1],
                                        SC[1][0:1].rearrange("p (s n) -> p n s", n=NQ)).then_inc(grp_row, 1)
                    if l == 0:
                        dve.wait_ge(c.o_done, p + 1)
                        o = oT[:, at_p].rearrange("p o s -> p (o s)")
                        if near(p):
                            dve.tensor_copy(o, OB[:]).then_inc(c.o_read, 1)
                        else:
                            dve.tensor_copy(o.rearrange("p (s n) -> p n s", n=NQ),
                                            OB[:].rearrange("p (n s) -> p n s", n=NQ)).then_inc(c.o_read, 1)
                    if last_near:
                        dve.wait_ge(grp_t, 2)
                        dve.tensor_copy(grp[:, 1, :, 0:1].rearrange("p n o -> p (n o)"), SC[0][:, 0:NQ]).then_inc(grp_d, 1)
                    if nxt is not None:
                        v_copy(p + 1, 1 - u)

                loop = {}

                def nxt_of(p, u):
                    return loop["i"] + (1 if u == 1 else 2)

                for j in range(3):
                    project(0, 0, j)
                v_copy(0, 0)
                pair(0, 0, 1)
                if l == 0:
                    pair(1, 1, 2)
                    pair(2, 0, 3)
                with dve.Fori(1 - l, 3) as i:
                    loop["i"] = i
                    pair(2 * i + 1, 1, (i + 1,))
                    pair(2 * i + 2, 0, (i + 1,))
                pair(7, 1, None)

                if l == 0:
                    dlink(group_sums(1, 3, 3))
                    m3 = small[:, 88:92]
                    dve.tensor_reduce(m3, grp[:, 1], mybir.AxisListType.X, ALU.max).then_inc(grp_d, 1)
                    dve.wait_ge(grp_d, 11)
                    dve.tensor_tensor(grp[:, 2], grp[:, 1], m3.rearrange("p (n o) -> p n o", o=1).broadcast_to([P, NQ, 3]),
                                      ALU.subtract).then_inc(grp_d, 1)
                    dve.wait_ge(grp_a, 7)
                    s3 = small[:, 92:96]
                    dlink(dve.tensor_reduce(s3, grp[:, 2], mybir.AxisListType.X, ALU.add))
                    dve.reciprocal(s3, s3).then_inc(grp_d, 1)
                    dve.wait_ge(grp_d, 13)
                    dve.scalar_tensor_tensor(out=grp[:, 5], in0=grp[:, 2], scalar=3.0,
                                             in1=s3.rearrange("p (n o) -> p n o", o=1).broadcast_to([P, NQ, 3]),
                                             op0=ALU.mult, op1=ALU.mult).then_inc(grp_d, 1)
                    dve.wait_ge(grp_t, 3)
                    dve.tensor_copy(tmp[0:3, 3].rearrange("p (s n) -> p n s", n=NQ),
                                    MB[0:3].rearrange("p (n s) -> p n s", n=NQ)).then_inc(grp_row, 1)

                    def low(p):
                        dve.wait_ge(gate_hi, p + 1)
                        dve.tensor_tensor(ff_lo[:, p], tmp[:, p % 2], ff_hi[:, p].bitcast(F32), ALU.subtract).then_inc(post_lo, 1)

                    for p in range(PAIRS):
                        dve.wait_ge(gate_mm, p + 1)
                        if p >= 2:
                            dve.wait_ge(post_lo, p - 1)
                        dve.tensor_tensor(tmp[:, p % 2], oT[:, p], SC[p % 2][:], ALU.mult).then_inc(gated, 1)
                        if p >= 1:
                            low(p - 1)
                    low(PAIRS - 1)
                else:
                    head_out(PAIRS - 1)
                    head_low(PAIRS - 1)
                add_tiles_x(T_WO[l], 3 + 2 * l, ("mlp2a", "mlp2b")[l])
                dve.wait_ge(rstd_ready, 4 + 2 * l)
                for n in range(NF2 // KD):
                    t = T_MLP2[l] + 2 * KD * n
                    f0 = NF2 * l + KD * n

                    def low2(i, p_):
                        dve.wait_ge(ffh_ready, 2 * i + f0 + NF1 + p_ + 1)
                        at_f = bass.ds(2 * i + p_, 1)
                        dve.tensor_tensor(ff_lo[:, at_f].rearrange("p o s -> p (o s)"), tmp[:, p_],
                                          ff_hi[:, at_f].rearrange("p o s -> p (o s)").bitcast(F32),
                                          ALU.subtract).then_inc(ff_ready, 1)
                    with dve.Fori(0, KD // 2) as i:
                        for p_ in range(2):
                            dve.wait_ge(evac[p_], i + t // 2 + 1)
                            dve.tensor_tensor(tmp[:, 2 + p_], tmp[:, p_], rstd[:], ALU.mult).then_inc(u_ready, 1)
                            dve.wait_ge(u_ready, 2 * i + f0 + p_ + 1)
                            dve.tensor_tensor(tmp[:, p_], tmp[:, 2 + p_], tmp[:, 2 + p_], ALU.mult).then_inc(squared, 1)
                            dve.wait_ge(squared, 2 * i + f0 + p_ + 1)
                            low2(i, p_)
                    if n < NF2 // KD - 1:
                        add_tiles(t + KD)
                    else:
                        add_tiles_x(t + KD, 4 + 2 * l, ("mix2b", "final")[l])
            dve.wait_ge(rstd_ready, 7)
            for k in range(KD):
                dve.scalar_tensor_tensor(out=z[:, k], in0=x[:, k], scalar=pcol("final", k, k + 1), in1=rstd[:],
                                         op0=ALU.mult, op1=ALU.mult).then_inc(final_ready, 1)


_BLOCKED = {}


def _toeplitz_index():
    return np.arange(1024) - (S - 1)


def _buckets():
    nb, me = 16, 8

    def one_hot(rel):
        n = np.abs(rel)
        nf = np.maximum(n, 1).astype(np.float32)
        large = me + (np.log(nf / np.float32(me)) / np.float32(math.log(1024 / me)) * np.float32(nb - me)).astype(np.int32)
        bucket = np.where(rel > 0, nb, 0) + np.where(n < me, n, np.minimum(large, nb - 1))
        return (bucket[None] == np.arange(32)[:, None]).astype(np.float32)

    def masks(rel):
        n = np.abs(rel)
        rows = [np.where((n % dil == 0) & (n <= win // 2), 0.0, NEG) for win, dil, nh in
                ((128, 1, 6), (512, 4, 5), (2048, 16, 5)) for _ in range(nh)]
        return np.pad(np.stack(rows), ((0, 16), (0, 0)))
    every = np.arange(1024) - (S - 1)
    own = DIL * (np.arange(256) - (P - 1))
    return np.concatenate([one_hot(every), masks(every), one_hot(own), masks(own)], axis=1).astype(np.float32)


def _swa_table():
    dist = (WIN + np.arange(P)[:, None] - np.arange(2 * P)[None]).astype(np.float32)
    rows = []
    for h in (0, 4, 1, 5, 2, 6, 3, 7):
        slope = np.float32(2.0 ** (-(h + 1)))
        rows.append(np.where((dist >= 0) & (dist < WIN), -slope * dist, np.float32(NEG)))
    return np.ascontiguousarray(np.stack(rows).reshape(4, 2, P, 2 * P).transpose(0, 2, 1, 3).astype(np.float32))


def _constants():
    c = np.zeros((P, N_CON), np.float32)

    def put(name, a):
        s, e = _ccols[name]
        c[:a.shape[0], s:e] = a
    put("ident", np.eye(P))
    put("flip", np.eye(P)[::-1])
    put("mean_d", np.full((P, P), 1.0 / D))
    put("mean_128", np.full((P, P), 1.0 / 128))
    put("mean_64", np.kron(np.eye(2), np.full((64, 64), 1.0 / 64)))
    i = np.arange(P)
    put("gla_mask", (i[:, None] <= i[None, :]) & (i[:, None] // CHUNK == i[None, :] // CHUNK))
    put("reset", np.tile((np.arange(S) % CHUNK != 0)[None], (P, 1)))
    return c


def _tiles(w):
    k, n = w.shape
    return w.reshape(k // P, P, n // P, P).transpose(2, 1, 0, 3).reshape(n // P, P, (k // P) * P)


def _weights(i):
    w = i["w_in"][0]
    parts = np.split(w, np.cumsum([256, 256, 512, 512, 16, 512, 128])[:7], axis=1)
    gq, gk, gv, gr, _, sq, sk, sv = parts
    heads = sq.reshape(D, 8, 64)[:, [0, 4, 1, 5, 2, 6, 3, 7]].reshape(D, 512)
    seq = [_tiles(np.concatenate([sk, sv, heads, gq, gk, gv, gr], axis=1))]
    wo = i["w_out"][0]
    low = wo[512:].reshape(8, 64, D)[[0, 4, 1, 5, 2, 6, 3, 7]].reshape(512, D)
    seq.append(_tiles(np.concatenate([wo[:512], low])))
    up = i["w_up"][0].reshape(D, 2, NF1, P).transpose(0, 2, 1, 3).reshape(D, 2 * FF1)
    up, down = _tiles(up), i["w_down"][0]
    for a, b in CHUNKS1:
        seq.append(up[2 * a:2 * b])
        t = _tiles(down[a * P:b * P])
        seq.append(np.pad(t, ((0, 0), (0, 0), (0, D - t.shape[2]))))
    for l, (qkv, wo) in enumerate((("a_w_qkv_2", "a_w_o_2"), ("b_w_qkv_2", "b_w_o_2"))):
        w = i[qkv][0].reshape(D, 3, PAIRS, P).transpose(0, 2, 1, 3).reshape(D, 3 * D)
        seq += [_tiles(w), _tiles(i[wo][0])]
        up, down = _tiles(i["mlp_w_in_2"][l]), i["mlp_w_out_2"][l]
        for n in range(NF2 // KD):
            seq += [up[KD * n:KD * n + KD], _tiles(down[D * n:D * n + D])]
    return np.concatenate(seq)


def _params(i):
    p = np.zeros((P, N_PAR), np.float32)

    def put(name, a):
        s, e = _cols[name]
        p[:a.shape[0], s:e] = a

    def cols(v):
        return v.reshape(-1, P).T
    put("mix_norm", cols(i["mix_norm"][0]))
    put("ffn_norm", cols(i["ffn_norm"][0]))
    for l in range(2):
        put(("mix2a", "mix2b")[l], cols(i["norm_mix_g_2"][l]))
        put(("mlp2a", "mlp2b")[l], cols(i["norm_mlp_g_2"][l]))
    put("final", cols(i["norm_final_g_2"]))
    cw = i["conv_w"][0].reshape(3, 2, NF1, P)
    put("conv_w", cw.transpose(3, 0, 2, 1).reshape(P, -1))
    put("conv_b", i["conv_b"][0].reshape(2, NF1, P).transpose(2, 1, 0).reshape(P, -1))
    put("b_alpha", cols(i["b_alpha"][0]))
    put("gla_norm", i["gla_norm"][0][:, None])
    put("q_norm", np.tile(i["q_norm"][0], 2)[:, None])
    put("k_norm", np.tile(i["k_norm"][0], 2)[:, None])
    put("subln", i["b_subln_g_2"][0][:, None])
    put("sinks", np.tile(i["sinks"][0][[0, 4, 1, 5, 2, 6, 3, 7]][None], (P, 1)))
    put("lam", np.tile(i["b_lambda_2"][0].reshape(1, 256), (P, 1)))
    glr = np.zeros((KD, P, 32), np.float32)
    glr[:, :, :16] = i["w_in"][0][:, 1536:1552].reshape(KD, P, 16)
    put("w_glr", glr.transpose(1, 0, 2).reshape(P, -1))
    put("w_alpha", i["w_alpha2"][0])
    put("rel_bias", i["rel_bias_2"])
    return p


def kernel(**inputs):
    import concourse.bacc as bacc
    from concourse.bass_utils import run_bass_kernel_spmd

    i = {k: np.asarray(v) for k, v in inputs.items()}
    arrays = {
        "x_in": np.ascontiguousarray(i["x"][0].reshape(S, KD, P).transpose(2, 1, 0)),
        "params": _params(i),
        "consts": _constants(),
        "sel": (np.repeat([0] * 6 + [1] * 5 + [2] * 5, 64)[None] == np.arange(3)[:, None]).astype(np.float32),
        "buckets": _buckets(),
        "swa_table": _swa_table(),
        "weights": _weights(i),
    }
    nc = bacc.Bacc("TRN2", target_bir_lowering=False, num_devices=1)
    args = [nc.dram_tensor(n, a.shape, F32, kind="ExternalInput").ap() for n, a in arrays.items()]
    tables = [nc.dram_tensor(f"table{l}", (16, w), F32, kind="Internal").ap() for l, w in enumerate((1024, 1024, 256))]
    out = nc.dram_tensor("out", (P, KD, S), F32, kind="ExternalOutput").ap()
    program(nc, *args, tables, out)
    r = run_bass_kernel_spmd(nc, [arrays], core_ids=[0])
    return r.results[0]["out"].transpose(2, 1, 0).reshape(1, S, D)
```

```python
import math
from contextlib import ExitStack

import numpy as np
import concourse.bass as bass
from concourse import mybir

F32 = mybir.dt.float32
F32R = mybir.dt.float32r
ALU = mybir.AluOpType
ACT = mybir.ActivationFunctionType

P = 128
S = 512
D = 1024
KD = D // P
NQ = S // P
EPS = 1e-6
NEG = -1e30

FF1 = 2816
NF1 = FF1 // P
FF2 = 4096
NF2 = FF2 // P
PAIRS = 8
NEAR = 3
DIL = 4
CHUNK = 64
NCH = S // CHUNK
GH = 4
WIN = 128
EXT = S + 3 * P

OUT_DVE = 5
X_PARTS = [(0, 1), (1, 2), (2, 4), (4, 8)]

N_IN = 18
N_OUT = KD
CHUNKS1 = [(0, 8), (8, 16), (16, 22)]
T_IN = 0
T_OUT = T_IN + N_IN
T_MLP1 = T_OUT + N_OUT
T_QKV = [0, 0]
T_WO = [0, 0]
T_MLP2 = [0, 0]
_t = T_MLP1 + 2 * NF1 + KD * len(CHUNKS1)
for _l in range(2):
    T_QKV[_l] = _t
    T_WO[_l] = _t + 3 * PAIRS
    T_MLP2[_l] = T_WO[_l] + KD
    _t = T_MLP2[_l] + 2 * NF2
N_TILES = _t
Z_SK, Z_SV, Z_SQ, Z_GQ, Z_GK, Z_GV, Z_GR = 0, 1, 2, 6, 8, 10, 14
SWA_TILES = [(8, 11), (11, 14), (14, 16), (16, 18)]

_cols = {}
_n = 0
for _name, _w in [("mix_norm", 8), ("ffn_norm", 8), ("mix2a", 8), ("mix2b", 8), ("mlp2a", 8), ("mlp2b", 8),
                  ("final", 8), ("conv_w", 3 * 2 * NF1), ("conv_b", 2 * NF1), ("b_alpha", 2), ("gla_norm", 1),
                  ("q_norm", 1), ("k_norm", 1), ("subln", 1), ("sinks", 8), ("lam", 256), ("w_glr", 8 * 32),
                  ("w_alpha", 256), ("rel_bias", 16)]:
    _cols[_name] = (_n, _n + _w)
    _n += _w
N_PAR = _n
_ccols = {}
_n = 0
for _name, _w in [("ident", P), ("flip", P), ("mean_d", P), ("mean_128", P), ("mean_64", P), ("gla_mask", P), ("reset", S)]:
    _ccols[_name] = (_n, _n + _w)
    _n += _w
N_CON = _n
LAMBDA_INIT = 0.8 - 0.6 * math.exp(-0.3 * 1)


def program(nc, x_in, params, consts, sel, buckets, swa_table, weights, tables, out):
    with ExitStack() as ctx:
        def sb(name, shape, dt=F32):
            return ctx.enter_context(nc.sbuf_tensor(name, shape, dt))

        def sem(name):
            return ctx.enter_context(nc.semaphore(name))

        x = sb("x", [P, KD, S])
        xn_hi = sb("xn_hi", [P, KD, S], F32R)
        xn_lo = sb("xn_lo", [P, KD, S], F32R)
        ff_hi = sb("ff_hi", [P, KD, S], F32R)
        ff_lo = sb("ff_lo", [P, KD, S], F32R)
        stage = sb("stage", [P, 2, KD, P])
        w_hi = sb("w_hi", [P, 2, KD, P], F32R)
        w_lo = sb("w_lo", [P, 2, KD, P], F32R)
        par = sb("par", [P, N_PAR])
        con = sb("con", [P, N_CON])
        bias = sb("bias", [P, 2, 2, EXT])
        qkv = sb("qkv", [P, 2, 3, S])
        prob = sb("prob", [P, 2, 2, S])
        tmp = sb("tmp", [P, 4, S])
        rstd = sb("rstd", [P, S])
        rstd_h = sb("rstd_h", [P, S])
        mx = sb("mx", [P, 2, 8])
        nm = sb("nm", [P, 2, 8])
        sm = sb("sm", [P, 2, 8])
        rc = sb("rc", [P, 2, 8])
        es = sb("es", [P, 2, 8])
        lse_nm = sb("lse_nm", [P, PAIRS, 8])
        lse_sm = sb("lse_sm", [P, PAIRS, 8])
        small = sb("small", [P, 128])
        glr_w = sb("glr_w", [P, 2, KD * 32], F32R)

        grp = sb("grp", [P, 6, NQ, 3])
        lhe = sb("lhe", [P, 2, NQ, 16])

        with nc.sbuf_tensor("z", [P, N_IN, S], F32) as z:
            with nc.sbuf_tensor("v_tok", [P, 2, 2, NQ, P], F32) as v_tok:
                pass
        zr = sb("zr", [P, N_IN, S], F32R)
        v_split = sb("v_split", [P, 2, 2, NQ, P], F32R)
        pT_split = zr[:, 8:16].rearrange("p (a k) s -> p a k s", a=2)
        qk_split = zr[:, 0:8].rearrange("p (u j a) s -> p u j a s", u=2, j=2)

        oT = z[:, 0:KD, :]
        pT = z[:, KD:2 * KD, :].rearrange("p (h k) s -> p h k s", h=2)

        banks = [ctx.enter_context(nc.psum_tensor(f"bank{i}", [P, S], F32)) for i in range(8)]
        G = banks[0:2]
        SC = banks[2:4]
        TR = banks[4:6]
        OB = banks[6]
        MB = banks[7]

        def pcol(name, a=0, b=None):
            s, e = _cols[name]
            return par[:, s + a:(e if b is None else s + b)]

        def ccol(name):
            s, e = _ccols[name]
            return con[:, s:e]

        ident = ccol("ident")

        par_in = sem("par_in")
        loaded = sem("loaded")
        stage_full = [sem(f"stage_full{i}") for i in range(2)]
        hi_ready = sem("hi_ready")
        lo_ready = sem("lo_ready")
        hi_free = sem("hi_free")
        tile_done = sem("tile_done")
        evac = [sem(f"evac{i}") for i in range(2)]
        x_in_done = [sem(f"x_in{i}") for i in range(len(X_PARTS))]
        const_ready, acc_zero = sem("const_ready"), sem("acc_zero")
        sq_ready, acc_done, ss_done = sem("sq_ready"), sem("acc_done"), sem("ss_done")
        inv_spread = sem("inv_spread")
        eps_added, inv_ready, rstd_ready = sem("eps_added"), sem("inv_ready"), sem("rstd_ready")
        glr_split = sem("glr_split")
        glr_done, glr_read, gate_in = sem("glr_done"), sem("glr_read"), sem("gate_in")
        gate_abs, gate_log = sem("gate_abs"), sem("gate_log")
        decay_sum, decay_exp, decay_diff, key_exp = sem("decay_sum"), sem("decay_exp"), sem("decay_diff"), sem("key_exp")
        gla_keys = sem("gla_keys")
        turned_in, turned_out = sem("turned_in"), sem("turned_out")
        state_in, state_out = sem("state_in"), sem("state_out")
        gla_a, gla_masked, gla_o, gla_sq, gla_ss = sem("gla_a"), sem("gla_masked"), sem("gla_o"), sem("gla_sq"), sem("gla_ss")
        gla_r, swn_r, post_r = sem("gla_r"), sem("swn_r"), sem("post_r")
        gla_t, gla_hi, gla_lo = sem("gla_t"), sem("gla_hi"), sem("gla_lo")
        gates_on = sem("gates_on")
        swn_sq, swn_ss, swn_done = sem("swn_sq"), sem("swn_ss"), sem("swn_done")
        swv_t, swv_done = sem("swv_t"), sem("swv_done")
        swa_hi, swa_lo = sem("swa_hi"), sem("swa_lo")
        conv_0, conv_1, conv_2, silu_done, f_made = sem("conv_0"), sem("conv_1"), sem("conv_2"), sem("silu_done"), sem("f_made")
        ffh_ready, ff_ready = sem("ffh_ready"), sem("ff_ready")
        tab_mm, tab_sb, tables_saved = sem("tab_mm"), sem("tab_sb"), sem("tables_saved")
        lam_sum, lam_exp = sem("lam_sum"), sem("lam_exp")
        grp_d, grp_a, grp_t, grp_row = sem("grp_d"), sem("grp_a"), sem("grp_t"), sem("grp_row")
        gate_mm, gated, gate_hi, post_ln = sem("gate_mm"), sem("gated"), sem("gate_hi"), sem("post_ln")
        post_sq, post_mm, post_t, post_hi, post_lo = (sem("post_sq"), sem("post_mm"), sem("post_t"),
                                                      sem("post_hi"), sem("post_lo"))
        scaled_out, final_ready, final_pool = sem("scaled_out"), sem("final_ready"), sem("final_pool")
        sel_in = sem("sel_in")
        squared = sem("squared")
        xh_ready, xn_ready = sem("xh_ready"), sem("xn_ready")
        u_ready = sem("u_ready")
        qk_high, qk_low = sem("qk_high"), sem("qk_low")
        pt_low, v_high = sem("pt_low"), sem("v_high")
        chains = {"dve": sem("dve_chain"), "act": sem("act_chain"), "pe": sem("pe_chain")}
        bias_in = [sem(f"bias_in{i}") for i in range(2)]
        out_sent = sem("out_sent")

        at = {"dve": 0, "act": 0, "pe": 0}

        def link(key, eng, ins):
            at[key] += 1
            ins.then_inc(chains[key], 1)
            eng.wait_ge(chains[key], at[key])

        class Core:
            def __init__(self, n, pairs_out, ranges):
                self.n = n
                self.lse_kept = sem(f"{n}_lse")
                self.vt_done = sem(f"{n}_vt")
                self.v_ready = sem(f"{n}_v")
                self.scored = sem(f"{n}_scored")
                self.maxed = sem(f"{n}_maxed")
                self.negated = sem(f"{n}_negated")
                self.expd = sem(f"{n}_expd")
                self.recd = sem(f"{n}_recd")
                self.scaled = sem(f"{n}_scaled")
                self.turned = sem(f"{n}_turned")
                self.copied = sem(f"{n}_copied")
                self.o_done = sem(f"{n}_o")
                self.pv_done = sem(f"{n}_pv") if n == "swa" else None
                self.o_read = {"swa": swa_lo, "dif": post_t}.get(n) or sem(f"{n}_oread")
                self.halves_out = pairs_out
                self.ranges = ranges

        def qkv_tile(l, p, u, j):
            i = 3 * u + j
            if isinstance(p, int):
                return T_QKV[l] // 2 + (3 * p + j) // 2, i % 2
            return T_QKV[l] // 2 + 3 * p[0] + i // 2, i % 2

        def near(p):
            return isinstance(p, int) and p < NEAR

        swa = Core("swa", 2, lambda p, n: (max(0, n - 1), n + 1))
        att = [Core("dil", 2, lambda p, n: (max(0, n - 1), min(NQ, n + 2)) if near(p) else (n, n + 1)),
               Core("dif", 1, lambda p, n: (0, NQ))]

        block = ctx.enter_context(nc.Block())


        flat_bias = bias[:].rearrange("p a b c -> p (a b c)")
        kd_tok = [v.rearrange("p (t f) -> p t f", t=NQ) for v in (flat_bias[:, 6 * S:7 * S], z[:, Z_SV])]
        gv_tok = flat_bias[:, 2 * S:6 * S].rearrange("p (h t f) -> p h t f", h=GH, t=NQ)
        swa_bias = flat_bias[:, 0:2 * S].rearrange("p (a h s) -> p a h s", a=2, h=2)
        state = prob[:].rearrange("p a b s -> p (a b s)").rearrange("p (j c f) -> p j c f", j=2, c=NCH)
        gla_bank = [OB, MB, TR[0], TR[1]]
        gla_rstd = [qkv[:, i // 2, 2 * (i % 2)] for i in range(GH)]
        bucket = flat_bias[0:32, 0:2560]
        table_sb = prob[0:16].rearrange("p a b s -> p a (b s)")
        swa_pT = v_tok[:, 1]
        acc = tmp[:, 2]
        eps_col = small[:, 96:97]
        inv_tok = small[:, 97:101]
        decay = small[:, 0:16].rearrange("p (j c) -> p j c", j=2)
        lam_s, neg_lam = small[:, 16:20], small[:, 20:21]
        selector = z[0:3, 16:18].rearrange("p a s -> p (a s)")
        near_row = tmp[0:1, 3]
        class_sb = tmp[0:16, 3, 0:256]
        GROUPS = [(0, 6), (6, 11), (11, 16)]
        GATES = [0, 3, 5, 6]
        gate_bank = [SC[0], SC[1], TR[0], TR[1]]

        def toeplitz(table, p):
            w = table.shape[1]
            return bass.AP(tensor=table.tensor, offset=2 * p * w, ap=[[1, P], [w, 2], [1, EXT if w > EXT else P]])

        @block.sync
        def _(sp):
            def load(m, p_, first=False):
                if not first:
                    sp.wait_ge(lo_ready, 2 * m + p_ - 1)
                if isinstance(m, int):
                    src = weights[2 * m + p_]
                else:
                    src = weights[bass.ds(2 * m + p_, 1)].rearrange("o p c -> (o p) c")
                sp.dma_start(stage[:, p_].rearrange("p k c -> p (k c)"), src).then_inc(stage_full[p_], 16)

            def loads(t0, t1):
                with sp.Fori(t0 // 2, t1 // 2) as m:
                    for p_ in range(2):
                        load(m, p_)

            def bias_load(core, table, p, q_, used):
                if used is not None:
                    sp.wait_ge(core.maxed, used)
                if core is swa:
                    sp.dma_start(swa_bias[:, q_], table[p]).then_inc(bias_in[q_], 16)
                elif core is att[0] and not near(p):
                    sp.dma_start(bias[:, q_, :, 3 * P:4 * P], toeplitz(tables[2], p)).then_inc(bias_in[q_], 16)
                else:
                    sp.dma_start(bias[:, q_], toeplitz(table, p)).then_inc(bias_in[q_], 16)

            sp.dma_start(par[:], params).then_inc(par_in, 16)
            for i, (a, b) in enumerate(X_PARTS):
                sp.dma_start(x[:, a:b], x_in[:, a:b]).then_inc(x_in_done[i], 16)
                if i == 1:
                    load(0, 0, True)
            load(0, 1, True)
            sp.dma_start(con[:], consts).then_inc(loaded, 16)
            sp.dma_start(bucket, buckets).then_inc(loaded, 16)
            loads(2, 6)
            sp.wait_ge(tab_sb, 3)
            for p in range(4):
                loads(6 + 2 * p, 8 + 2 * p)
                if p < 2:
                    bias_load(swa, swa_table, p, p, None)
            loads(14, 18)
            bias_load(swa, swa_table, 2, 0, 8)
            bias_load(swa, swa_table, 3, 1, 16)
            loads(T_OUT, T_OUT + 2)
            sp.wait_ge(gla_lo, GH)
            sp.dma_start(selector, sel).then_inc(sel_in, 16)
            loads(T_OUT + 2, T_QKV[0])
            sp.wait_ge(tables_saved, 48)
            for l in range(2):
                core, before = att[l], (swa if l == 0 else att[0])
                sp.wait_ge(before.maxed, 8 * (4 if l == 0 else PAIRS))
                for p in range(2):
                    bias_load(core, tables[l], p, p, None)
                loads(T_QKV[l], T_QKV[l] + 6)

                def pair_loads(i):
                    for u in range(2):
                        for j in range(3 * u, 3 * u + 3):
                            if j == 3 * u + 2:
                                bias_load(core, tables[l], 2 * i + u, u, 16 * i + 8 * u - 8)
                            load(T_QKV[l] // 2 + 3 * i + j // 2, j % 2)
                if l == 0:
                    pair_loads(1)
                with sp.Fori(2 - l, 4) as i:
                    pair_loads(i)
                loads(T_WO[l], T_QKV[1] if l == 0 else N_TILES)
            for k in (0, 5, 1, 2, 6, 3, 4, 7):
                sp.wait_ge(*((final_ready, k + 1) if k < OUT_DVE else (final_pool, k - OUT_DVE + 1)))
                sp.dma_start(out[:, k], z[:, k]).then_inc(out_sent, 16)
            sp.wait_ge(out_sent, 16 * KD)

        @block.gpsimd
        def _(pool):
            def split_lo(m, p_, first=False):
                pool.wait_ge(hi_ready, 2 * m + p_ + 1)
                if not first:
                    pool.wait_ge(tile_done, 2 * m + p_ - 1)
                nc.gpsimd.tensor_tensor(w_lo[:, p_], stage[:, p_], w_hi[:, p_].bitcast(F32),
                                        ALU.subtract).then_inc(lo_ready, 1)
            split_lo(0, 0, True)
            split_lo(0, 1, True)
            with pool.Fori(1, N_TILES // 2) as m:
                for p_ in range(2):
                    split_lo(m, p_)
            pool.wait_ge(rstd_ready, 7)
            pool.wait_ge(scaled_out, KD)
            for k in range(OUT_DVE, KD):
                nc.gpsimd.tensor_tensor(z[:, k], z[:, k], rstd[:], ALU.mult).then_inc(final_pool, 1)

        @block.tensor
        def _(pe):
            def tile(m, p_, hi, lo, nk=KD, ready=None, late=None, between=None):
                pe.wait_ge(hi_ready, 2 * m + p_ + 1)
                if not (isinstance(m, int) and m == 0):
                    pe.wait_ge(evac[p_], m)
                if late is not None:
                    pe.wait_ge(late[0], late[1] - 1)
                ks = list(range(nk))

                def highs(ks, first):
                    for k in ks:
                        if ready is not None and k < ready[2]:
                            pe.wait_ge(ready[0], ready[1] + k + 1)
                        if late is not None and k == nk - 1:
                            pe.wait_ge(*late)
                        pe.matmul(G[p_][:], w_hi[:, p_, k], hi[:, k], start=(first and k == ks[0]), stop=False)
                        mm = pe.matmul(G[p_][:], w_hi[:, p_, k], lo[:, k], start=False, stop=False)
                    return mm

                def lows(ks, last):
                    for k in ks:
                        mm = pe.matmul(G[p_][:], w_lo[:, p_, k], hi[:, k], start=False, stop=(last and k == ks[-1]))
                    return mm

                if ready is None and late is None:
                    highs(ks, True).then_inc(hi_free, 1)
                    if between is not None:
                        spread(between)
                    pe.wait_ge(lo_ready, 2 * m + p_ + 1)
                    lows(ks, True).then_inc(tile_done, 1)
                else:
                    highs(ks[:-1], True)
                    pe.wait_ge(lo_ready, 2 * m + p_ + 1)
                    lows(ks[:-1], False)
                    highs(ks[-1:], False).then_inc(hi_free, 1)
                    lows(ks[-1:], True).then_inc(tile_done, 1)

            def part(t, hi, lo, ks, first=False, last=False):
                m, p_ = t // 2, t % 2
                if first:
                    pe.wait_ge(hi_ready, t + 1)
                    pe.wait_ge(lo_ready, t + 1)
                    pe.wait_ge(evac[p_], m)
                for k in ks:
                    pe.matmul(G[p_][:], w_hi[:, p_, k], hi[:, k], start=(first and k == ks[0]), stop=False)
                    mm = pe.matmul(G[p_][:], w_hi[:, p_, k], lo[:, k], start=False, stop=False)
                if last:
                    mm.then_inc(hi_free, 1)
                for k in ks:
                    mm = pe.matmul(G[p_][:], w_lo[:, p_, k], hi[:, k], start=False, stop=(last and k == ks[-1]))
                if last:
                    mm.then_inc(tile_done, 1)

            def tiles(t0, t1, hi, lo, nk=KD, ready=None, n=None):
                if ready is not None:
                    tile(t0 // 2, 0, hi, lo, nk, ready)
                    if n is not None:
                        norm(n)
                    tile(t0 // 2, 1, hi, lo, nk, between=n)
                    t0 += 2
                with pe.Fori(t0 // 2, t1 // 2) as m:
                    for p_ in range(2):
                        tile(m, p_, hi, lo, nk)

            def norm(n):
                pe.wait_ge(acc_done, KD * (n + 1))
                for t in range(NQ):
                    mm = pe.matmul(MB[:, t:t + 1], acc[:, t * P:(t + 1) * P], ccol("mean_d")[:, 0:1], start=True, stop=True)
                mm.then_inc(ss_done, 1)

            def spread(n):
                pe.wait_ge(inv_ready, n + 1)
                for t in range(NQ):
                    mm = pe.matmul(MB[:, t * P:(t + 1) * P], inv_tok[:, t:t + 1].broadcast_to([P, P]), ident, start=True,
                                   stop=True)
                mm.then_inc(inv_spread, 1)

            def scores(c, p, q_, n, qT, kT):
                a, b = c.ranges(p, n)
                for h in range(2):
                    r = slice(64 * h, 64 * h + 64)
                    if not (isinstance(p, int) and p == 0 and n == 0):
                        pe.wait_ge(c.maxed, 8 * p + 2 * n + h - 1)
                    if c is att[1]:
                        if n == 0 and h == 0:
                            pe.wait_ge(qk_low, 2 * p + 2)
                        for i, (qa, ka) in enumerate(((0, 0), (1, 0), (0, 1))):
                            mm = pe.matmul(SC[h][:], qk_split[r, q_, 0, qa, n * P:(n + 1) * P], qk_split[r, q_, 1, ka],
                                           start=(i == 0), stop=(i == 2))
                        mm.then_inc(c.scored, 1)
                    else:
                        pe.matmul(SC[h][:, 0:(b - a) * P], qT[r, n * P:(n + 1) * P], kT[r, a * P:b * P],
                                  start=True, stop=True).then_inc(c.scored, 1)

            def turn(c, p, n):
                a, b = c.ranges(p, n)
                for h in range(c.halves_out):
                    i = c.halves_out * n + h
                    pe.wait_ge(c.scaled, 4 * c.halves_out * p + i + 1)
                    if not (isinstance(p, int) and p == 0 and i < 2):
                        pe.wait_ge(c.copied, 4 * c.halves_out * p + i - 1)
                        if c is att[1]:
                            pe.wait_ge(pt_low, 4 * p + i - 1)
                    for j in range(b - a):
                        mm = pe.transpose(TR[i % 2][:, j * P:(j + 1) * P], prob[:, n % 2, h, j * P:(j + 1) * P],
                                          ident if c is swa else ccol("flip"))
                    mm.then_inc(c.turned, 1)

            def values(c, p, v, pt):
                pe.wait_ge(c.copied, 4 * c.halves_out * (p + 1))
                if not (isinstance(p, int) and p == 0):
                    pe.wait_ge(c.o_read, p)
                if c is att[0]:
                    for n in range(NQ):
                        a, b = c.ranges(p, n)
                        cols = slice(n * P, (n + 1) * P)
                        for h in range(2):
                            for j in range(b - a):
                                mm = pe.matmul(OB[:, cols], v[:, h, a + j], pt[:, h, j, cols], start=(h == 0 and j == 0),
                                               stop=(h == 1 and j == b - a - 1))
                else:
                    pe.wait_ge(pt_low, 4 * p + 4)
                    for i, (va, pa) in enumerate(((0, 0), (1, 0), (0, 1))):
                        for k in range(NQ):
                            mm = pe.matmul(OB[:], v[:, va, k], pT_split[:, pa, k], start=(i == 0 and k == 0),
                                           stop=(i == 2 and k == NQ - 1))
                mm.then_inc(c.o_done, 1)

            def swa_values(p, n):
                a, b = swa.ranges(p, n)
                pe.wait_ge(swa.copied, 8 * p + 2 * n + 2)
                if n == 0 and p:
                    pe.wait_ge(swa_lo, p)
                for h in range(2):
                    for j in range(b - a):
                        mm = pe.matmul(OB[:, n * P:(n + 1) * P], v_tok[:, 0, h, a + j], swa_pT[:, n % 2, 2 * h + j],
                                       start=(h == 0 and j == 0), stop=(h == 1 and j == b - a - 1))
                mm.then_inc(swa.pv_done, 1)

            def token_major(p, n):
                h = 4 * (p - 2) + n
                if 0 <= h < GH + 2:
                    if h < GH:
                        t = Z_GV + h
                        pe.wait_ge(evac[t % 2], t // 2 + 1)
                        src = z[:, t]
                    else:
                        pe.wait_ge(gla_keys, 6)
                        src = qkv[:, h - GH, 2]
                    if h:
                        pe.wait_ge(turned_out, h)
                    for t in range(NQ):
                        mm = pe.transpose(MB[:, t * P:(t + 1) * P], src[:, t * P:(t + 1) * P], ident)
                    mm.then_inc(turned_in, 1)

            def swa_norm(i):
                pe.wait_ge(swn_sq, i + 1)
                if i >= 2:
                    pe.wait_ge(swn_r, i - 1)
                pe.matmul(SC[i % 2][:], ccol("mean_64"), tmp[:, i % 2], start=True, stop=True).then_inc(swn_ss, 1)

            tile(0, 0, xn_hi, xn_lo, ready=(xn_ready, 0, KD))
            pe.wait_ge(loaded, 32)
            norm(0)
            for b in range(2):
                pe.matmul(SC[b][0:16], pcol("rel_bias")[0:32], bucket[:, b * S:(b + 1) * S], start=True, stop=True)
            mm = pe.matmul(OB[0:16, 0:256], pcol("rel_bias")[0:32], bucket[:, 2048:2304], start=True, stop=True)
            mm.then_inc(tab_mm, 1)

            tile(0, 1, xn_hi, xn_lo, between=0)
            pe.wait_ge(glr_split, 2)
            pe.wait_ge(rstd_ready, 1)
            n_mm = 0
            for w, mv in ((0, xn_hi), (0, xn_lo), (1, xn_hi)):
                for k in range(KD):
                    mm = pe.matmul(MB[0:32], glr_w[:, w, k * 32:(k + 1) * 32], mv[:, k], start=(n_mm == 0), stop=(n_mm == 23))
                    n_mm += 1
            mm.then_inc(glr_done, 1)
            tile(1, 0, xn_hi, xn_lo)
            pe.wait_ge(glr_read, 1)
            for j in range(2):
                mm = pe.matmul(TR[j][:], pcol("w_alpha")[0:16, j * P:(j + 1) * P], qkv[0:16, 0, 2], start=True, stop=True)
            mm.then_inc(gate_in, 1)
            pe.wait_ge(tab_sb, 3)
            for t in range(3, 8):
                tile(t // 2, t % 2, xn_hi, xn_lo)
                swa_norm(t - 3)
            pe.wait_ge(evac[1], 1)
            for t in range(NQ):
                mm = pe.transpose(MB[:, t * P:(t + 1) * P], z[:, Z_SV, t * P:(t + 1) * P], ident)
            mm.then_inc(swv_t, 1)
            pe.wait_ge(gate_log, 2)
            pe.wait_ge(swn_r, 5)
            for p in range(4):
                a, b = SWA_TILES[p]
                q = z[:, Z_SQ + p]
                pe.wait_ge(swn_done, p + 2)
                scores(swa, p, 0, 0, q, z[:, Z_SK])
                tile(a // 2, a % 2, xn_hi, xn_lo)
                turn(swa, p, 0)
                scores(swa, p, 0, 1, q, z[:, Z_SK])
                if p == 0:
                    pe.wait_ge(swv_done, 1)
                tile((a + 1) // 2, (a + 1) % 2, xn_hi, xn_lo)
                swa_values(p, 0)
                token_major(p, 0)
                turn(swa, p, 1)
                scores(swa, p, 0, 2, q, z[:, Z_SK])
                if b - a == 3:
                    tile((a + 2) // 2, (a + 2) % 2, xn_hi, xn_lo)
                swa_values(p, 1)
                token_major(p, 1)
                turn(swa, p, 2)
                scores(swa, p, 0, 3, q, z[:, Z_SK])
                swa_values(p, 2)
                token_major(p, 2)
                turn(swa, p, 3)
                swa_values(p, 3)
                token_major(p, 3)

            pe.wait_ge(swa_lo, 4)
            pe.wait_ge(turned_out, GH + 2)
            for i in range(GH):
                j, bank = i // 2, (TR[0], TR[1], OB, MB)[i]
                r = slice(64 * (i % 2), 64 * (i % 2) + 64)
                for t in range(NQ):
                    cols = slice(t * P, (t + 1) * P)
                    mm = pe.matmul(bank[:, cols], qkv[r, j, 1, cols], z[r, Z_GQ + j, cols], start=True, stop=True)
                mm.then_inc(gla_a, 1)
            part(T_OUT, ff_hi, ff_lo, [4, 5, 6, 7], first=True)
            pe.wait_ge(gla_masked, 2)
            for c in range(NCH - 1):
                r = slice(64 * (c % 2), 64 * (c % 2) + 64)
                for j in range(2):
                    if c >= 2:
                        pe.wait_ge(state_out, 2 * (2 * (c - 2) + j + 1))
                    pe.matmul((SC, TR)[j][c % 2][:, 0:256], kd_tok[j][r, c // 2], gv_tok[r, 2 * j:2 * j + 2, c // 2],
                              start=True, stop=True).then_inc(state_in, 1)

            def output(i):
                j, bank = i // 2, gla_bank[i]
                r = slice(64 * (i % 2), 64 * (i % 2) + 64)
                for t in range(NQ):
                    pe.matmul(bank[:, t * P:(t + 1) * P], gv_tok[:, i, t], tmp[:, i, t * P:(t + 1) * P],
                              start=True, stop=False)
                    for c in (2 * t, 2 * t + 1):
                        cols = slice(c * CHUNK, (c + 1) * CHUNK)
                        mm = pe.matmul(bank[:, cols], state[r, j, c], z[r, Z_GQ + j, cols], start=False,
                                       stop=(c == 2 * t + 1))
                mm.then_inc(gla_o, 1)

            def mean_square(i):
                pe.wait_ge(gla_sq, i + 1)
                if i >= 2:
                    pe.wait_ge(gla_r, i - 1)
                pe.matmul(SC[i % 2][:], ccol("mean_128"), tmp[:, i], start=True, stop=True).then_inc(gla_ss, 1)

            pe.wait_ge(gla_masked, GH)
            pe.wait_ge(state_out, 4 * (NCH - 1))
            output(0)
            output(1)
            mean_square(0)
            output(2)
            mean_square(1)
            output(3)
            mean_square(2)
            mean_square(3)
            part(T_OUT + 1, ff_hi, ff_lo, [4, 5, 6, 7], first=True)
            for i in range(GH):
                pe.wait_ge(gla_lo, i + 1)
                for t in (T_OUT, T_OUT + 1):
                    part(t, ff_hi, ff_lo, [i], last=(i == GH - 1))
            tiles(T_OUT + 2, T_MLP1, ff_hi, ff_lo)

            t = T_MLP1
            for n, (a, b) in enumerate(CHUNKS1):
                if n == 0:
                    tiles(t, t + 2 * (b - a), xn_hi, xn_lo, ready=(xn_ready, KD, KD), n=1)
                else:
                    tiles(t, t + 2 * (b - a), xn_hi, xn_lo)
                t += 2 * (b - a)
                with pe.Fori(t // 2, t // 2 + KD // 2) as m:
                    for p_ in range(2):
                        tile(m, p_, ff_hi, ff_lo, b - a, late=(ff_ready, b))
                t += KD

            for l in range(2):
                c = att[l]

                def proj(p, u, j):
                    first = isinstance(p, int) and p == 0 and j == 0
                    tile(*qkv_tile(l, p, u, j), xn_hi, xn_lo, ready=(xn_ready, KD * (2 + 2 * l), KD) if first else None,
                         between=2 + 2 * l if isinstance(p, int) and p == 0 and j == 1 else None)
                    if first:
                        norm(2 + 2 * l)

                def head_norm(p):
                    pe.wait_ge(post_sq, p + 1)
                    pe.matmul(TR[0][:], ccol("mean_128"), tmp[:, 2], start=True, stop=True).then_inc(post_mm, 1)

                def v_turn(p, u, at_p):
                    m, p_ = qkv_tile(l, at_p, u, 2)
                    pe.wait_ge(evac[p_], m + 1)
                    if not (isinstance(p, int) and p == 0):
                        pe.wait_ge(c.v_ready, p)
                    for t in range(NQ):
                        mm = pe.transpose(MB[:, t * P:(t + 1) * P], qkv[:, u, 2, t * P:(t + 1) * P], ident)
                    mm.then_inc(c.vt_done, 1)

                def pair(p, u, nxt):
                    q, k = qkv[:, u, 0], qkv[:, u, 1]
                    after = l == 1 and not (isinstance(p, int) and p == 0)
                    scores(c, p, u, 0, q, k)
                    if after:
                        head_norm(p - 1)
                    if nxt is not None:
                        proj(nxt, 1 - u, 0)
                    fill = l == 1 and nxt is None
                    if fill:
                        pe.wait_ge(post_lo, 2 * PAIRS - 2)
                        part(T_WO[1], ff_hi, ff_lo, list(range(PAIRS - 2)), first=True)
                    if after:
                        pe.wait_ge(post_r, p)
                    turn(c, p, 0)
                    scores(c, p, u, 1, q, k)
                    if nxt is not None:
                        proj(nxt, 1 - u, 1)
                    turn(c, p, 1)
                    scores(c, p, u, 2, q, k)
                    scores(c, p, u, 3, q, k)
                    if nxt is not None:
                        proj(nxt, 1 - u, 2)
                    turn(c, p, 2)
                    turn(c, p, 3)
                    last_near = l == 0 and isinstance(p, int) and p == NEAR - 1
                    if last_near:
                        pe.wait_ge(grp_d, 5)
                        pe.wait_ge(c.maxed, 8 * NEAR)
                        for n in range(NQ):
                            mm = pe.transpose(SC[1][0:1, n * P:(n + 1) * P], grp[:, 1, n, 0:1], ccol("flip"))
                        mm.then_inc(grp_t, 1)
                    if l == 1 and nxt is not None:
                        v_turn(p + 1, 1 - u, nxt)
                    pe.wait_ge(c.v_ready, p + 1)
                    values(c, p, (v_tok, v_split)[l][:, u], pT)
                    if last_near:
                        pe.wait_ge(grp_row, 1)
                        for n in range(NQ):
                            mm = pe.matmul(SC[0][:, n:n + 1], near_row[:, n * P:(n + 1) * P], ident[0:1, 0:1], start=True,
                                           stop=True)
                        mm.then_inc(grp_t, 1)
                    if l == 0 and nxt is not None:
                        v_turn(p + 1, 1 - u, nxt)

                for j in range(3):
                    proj(0, 0, j)
                v_turn(0, 0, 0)
                pair(0, 0, 1)
                if l == 0:
                    pair(1, 1, 2)
                    pair(2, 0, 3)
                    pe.wait_ge(grp_d, 6)
                with pe.Fori(1 - l, 3) as i:
                    pair(2 * i + 1, 1, (i + 1,))
                    pair(2 * i + 2, 0, (i + 1,))
                pair(7, 1, None)

                if l == 0:
                    pe.wait_ge(grp_d, 14)
                    for n in range(NQ):
                        mm = pe.transpose(MB[0:3, n * P:(n + 1) * P], grp[:, 5, n, :], ccol("flip"))
                    mm.then_inc(grp_t, 1)
                    pe.wait_ge(grp_row, 2)
                    pe.wait_ge(sel_in, 16)
                    for i, p in enumerate(GATES):
                        pe.matmul(gate_bank[i][:], selector[:, p * P:(p + 1) * P], tmp[0:3, 3], start=True,
                                  stop=True).then_inc(gate_mm, 1)
                    for k in range(PAIRS):
                        pe.wait_ge(post_lo, k + 1)
                        for t in (T_WO[0], T_WO[0] + 1):
                            part(t, ff_hi, ff_lo, [k], first=(k == 0), last=(k == PAIRS - 1))
                else:
                    part(T_WO[1] + 1, ff_hi, ff_lo, [0], first=True)
                    head_norm(PAIRS - 1)
                    part(T_WO[1] + 1, ff_hi, ff_lo, list(range(1, PAIRS - 2)))
                    for k in (PAIRS - 2, PAIRS - 1):
                        pe.wait_ge(post_lo, PAIRS + k + 1)
                        for t in (T_WO[1], T_WO[1] + 1):
                            part(t, ff_hi, ff_lo, [k], last=(k == PAIRS - 1))
                tiles(T_WO[l] + 2, T_MLP2[l], ff_hi, ff_lo)
                for n in range(NF2 // KD):
                    t = T_MLP2[l] + 2 * KD * n
                    if n == 0:
                        tiles(t, t + KD, xn_hi, xn_lo, ready=(xn_ready, KD * (3 + 2 * l), KD), n=3 + 2 * l)
                    else:
                        tiles(t, t + KD, xn_hi, xn_lo)
                    with pe.Fori((t + KD) // 2, (t + 2 * KD) // 2) as m:
                        for p_ in range(2):
                            tile(m, p_, ff_hi, ff_lo, late=(ff_ready, NF1 + NF2 * l + KD * (n + 1)))
            norm(6)
            spread(6)

        @block.scalar
        def _(act):
            def split_hi(m, p_, first=False):
                act.wait_ge(stage_full[p_], 16 * (m + 1))
                if not first:
                    act.wait_ge(hi_free, 2 * m + p_ - 1)
                act.activation(w_hi[:, p_], stage[:, p_], ACT.Copy).then_inc(hi_ready, 1)

            def split_x(i, k, t0, g0):
                act.wait_ge(evac[k], i + t0 // 2 + 1)
                at_k = bass.ds(2 * i + k, 1)
                xk = x[:, at_k].rearrange("p o s -> p (o s)")
                if g0 is not None:
                    act.activation(xn_hi[:, at_k].rearrange("p o s -> p (o s)"), xk, ACT.Copy,
                                   scale=par[:, bass.ds(2 * i + g0 + k, 1)]).then_inc(xh_ready, 1)
                act.activation(tmp[:, k], xk, ACT.Square).then_inc(sq_ready, 1)
                if g0 is None:
                    act.activation(z[:, at_k].rearrange("p o s -> p (o s)"), xk, ACT.Copy,
                                   scale=par[:, bass.ds(2 * i + _cols["final"][0] + k, 1)]).then_inc(scaled_out, 1)

            def splits_x(t0, name):
                if name == "final":
                    with act.Fori(0, KD // 2 - 1) as i:
                        for p_ in range(2):
                            split_hi(i + t0 // 2 + 1, p_)
                            split_x(i, p_, t0, None)
                    for p_ in range(2):
                        split_x(KD // 2 - 1, p_, t0, None)
                    return
                with act.Fori(0, KD // 2) as i:
                    for p_ in range(2):
                        split_hi(i + t0 // 2 + 1, p_)
                        split_x(i, p_, t0, _cols[name][0])

            def splits(t0, t1):
                with act.Fori(t0 // 2, t1 // 2) as m:
                    for p_ in range(2):
                        split_hi(m + 1, p_)

            def root(n):
                act.wait_ge(inv_spread, n + 1)
                act.activation(rstd[:], MB[:], ACT.Sqrt).then_inc(rstd_ready, 1)

            def load_exp_and_ln():
                act.add_instruction(mybir.InstLoadActFuncSet(name=nc.get_next_instruction_name(), ins=[], outs=[],
                                                             act_func_set_id=6))

            def exps(c, p, q_, n, sink=None):
                a, b = c.ranges(p, n)
                for h in range(2):
                    s = 2 * n + h
                    act.wait_ge(c.negated, 8 * p + s + 1)
                    if sink is not None:
                        act.activation(es[:, q_, s:s + 1], nm[:, q_, s:s + 1], ACT.Exp, bias=sink(h))
                    pr = prob[:, n % 2, h, 0:(b - a) * P]
                    act.activation(pr, pr, ACT.Exp, bias=nm[:, q_, s:s + 1],
                                   accum_out=sm[:, q_, s:s + 1]).then_inc(c.expd, 1)

            def copies(c, p, n, pt):
                a, b = c.ranges(p, n)
                for h in range(c.halves_out):
                    i = c.halves_out * n + h
                    act.wait_ge(c.turned, 4 * c.halves_out * p + i + 1)
                    if c is swa:
                        if h == 0 and 4 * p + n >= 2:
                            act.wait_ge(c.pv_done, 4 * p + n - 1)
                        dst = swa_pT[:, n % 2, 2 * h:2 * h + b - a]
                    else:
                        if i == 0 and not (isinstance(p, int) and p == 0):
                            act.wait_ge(c.o_done, p)
                        dst = (pt if c is att[0] else pT_split)[:, h, 0:b - a, n * P:(n + 1) * P]
                    act.activation(dst,
                                   TR[i % 2][:, 0:(b - a) * P].rearrange("p (k s) -> p k s", k=b - a),
                                   ACT.Copy).then_inc(c.copied, 1)

            def swa_square(i):
                t = i + 1 if i else 0
                act.wait_ge(evac[t % 2], t // 2 + 1)
                act.activation(tmp[:, i % 2], z[:, t], ACT.Square).then_inc(swn_sq, 1)

            act.wait_ge(par_in, 16)
            act.wait_ge(const_ready, 2)
            for k in range(KD):
                for i, (a, b) in enumerate(X_PARTS):
                    if k == a:
                        act.wait_ge(x_in_done[i], 16)
                act.activation(xn_hi[:, k], x[:, k], ACT.Copy, scale=pcol("mix_norm", k, k + 1)).then_inc(xh_ready, 1)
                if k >= 2:
                    act.wait_ge(acc_done, k - 1)
                act.activation(tmp[:, k % 2], x[:, k], ACT.Square).then_inc(sq_ready, 1)
                if k in (1, 7):
                    split_hi(0, k // 7, True)
            act.activation(glr_w[:, 0], pcol("w_glr"), ACT.Copy).then_inc(glr_split, 1)
            root(0)
            for t in range(3):
                split_hi(t // 2 + 1, t % 2)
            act.wait_ge(tab_sb, 3)
            for l in range(2):
                act.dma_start(tables[l], table_sb[:, l, :]).then_inc(tables_saved, 16)
            act.dma_start(tables[2], class_sb).then_inc(tables_saved, 16)
            act.wait_ge(gate_in, 1)
            for j in range(2):
                act.wait_ge(gate_abs, j + 1)
                link("act", act, act.activation(qkv[:, j, 1], TR[j][:], ACT.Abs, bias=pcol("b_alpha", j, j + 1)))
                link("act", act, act.activation(qkv[:, j, 1], qkv[:, j, 1], ACT.Exp, scale=-1.0))
            for j in range(2):
                act.activation(qkv[:, j, 1], qkv[:, j, 1], ACT.Ln, bias=1.0).then_inc(gate_log, 1)
            for i in range(5):
                split_hi((i + 3) // 2 + 1, (i + 3) % 2)
                swa_square(i)
                act.wait_ge(swn_ss, i + 1)
                if i:
                    act.wait_ge(swn_done, i)
                act.activation(rstd_h[:], SC[i % 2][:], ACT.Sqrt, bias=eps_col).then_inc(swn_r, 1)
            act.wait_ge(tables_saved, 48)
            act.wait_ge(lam_sum, 1)
            act.activation(lam_s[:, 2:4], lam_s[:, 0:2], ACT.Exp).then_inc(lam_exp, 1)
            for j in range(2):
                act.wait_ge(decay_sum, j + 1)
                last = qkv[:, j, 0].rearrange("p (c t) -> p c t", t=CHUNK)[:, :, CHUNK - 1]
                act.activation(decay[:, j], last, ACT.Exp, scale=1.0 / 16)
                act.activation(qkv[:, j, 1], qkv[:, j, 0], ACT.Exp, scale=-1.0 / 16)
                act.activation(tmp[:, 2 + j], qkv[:, j, 0], ACT.Exp, scale=1.0 / 16).then_inc(decay_exp, 1)
                act.wait_ge(decay_diff, j + 1)
                act.activation(qkv[:, j, 2], qkv[:, j, 2], ACT.Exp, scale=1.0 / 16).then_inc(key_exp, 1)
            for p in range(4):
                a, b = SWA_TILES[p]

                def sink(h, p=p):
                    return pcol("sinks", 2 * p + h, 2 * p + h + 1)
                exps(swa, p, 0, 0, sink)
                split_hi(a // 2 + 1, a % 2)
                copies(swa, p, 0, None)
                exps(swa, p, 0, 1, sink)
                split_hi((a + 1) // 2 + 1, (a + 1) % 2)
                copies(swa, p, 1, None)
                exps(swa, p, 0, 2, sink)
                if b - a == 3:
                    split_hi((a + 2) // 2 + 1, (a + 2) % 2)
                copies(swa, p, 2, None)
                exps(swa, p, 0, 3, sink)
                copies(swa, p, 3, None)
                act.wait_ge(swa.pv_done, 4 * p + 4)
                act.activation(ff_hi[:, GH + p], OB[:], ACT.Copy).then_inc(swa_hi, 1)
            for p_ in range(2):
                act.wait_ge(evac[p_], T_OUT // 2)
            for h in range(GH):
                act.activation(z[:, Z_GR + h], z[:, Z_GR + h], ACT.Silu).then_inc(gates_on, 1)

            def gla_square(i):
                act.wait_ge(gla_o, i + 1)
                act.activation(tmp[:, i], gla_bank[i][:], ACT.Square).then_inc(gla_sq, 1)

            def gla_root(i):
                act.wait_ge(gla_ss, i + 1)
                link("act", act, act.activation(gla_rstd[i], SC[i % 2][:], ACT.Ln, bias=eps_col))
                act.activation(gla_rstd[i], gla_rstd[i], ACT.Exp, scale=-0.5).then_inc(gla_r, 1)

            def gla_high(i):
                act.wait_ge(gla_t, i + 1)
                act.activation(ff_hi[:, i], tmp[:, i], ACT.Copy).then_inc(gla_hi, 1)

            load_exp_and_ln()
            gla_square(0)
            for i in range(GH):
                if i + 1 < GH:
                    gla_square(i + 1)
                gla_root(i)
                if i >= 2:
                    gla_high(i - 2)
            gla_high(GH - 2)
            gla_high(GH - 1)
            act.wait_ge(gla_lo, GH)
            splits_x(T_OUT, "ffn_norm")
            root(1)
            t = T_MLP1
            for a, b in CHUNKS1:
                with act.Fori(0, b - a) as i:
                    f, m = i + a, i + t // 2
                    for p_ in range(2):
                        split_hi(m + 1, p_)
                        act.wait_ge(evac[p_], m + 1)
                        if p_ == 0:
                            act.wait_ge(ff_ready, f)
                        w2 = par[:, bass.ds(_cols["conv_w"][0] + 4 * NF1 + 2 * f + p_, 1)]
                        bc = par[:, bass.ds(_cols["conv_b"][0] + 2 * f + p_, 1)]
                        act.activation(tmp[:, p_], tmp[:, 2 + p_], ACT.Identity, bias=bc, scale=w2).then_inc(conv_0, 1)
                    act.wait_ge(conv_2, 2 * f + 1)
                    act.activation(tmp[:, 0], tmp[:, 0], ACT.Silu).then_inc(silu_done, 1)
                    act.wait_ge(f_made, f + 1)
                    act.activation(ff_hi[:, bass.ds(i, 1)].rearrange("p o s -> p (o s)"), tmp[:, 1],
                                   ACT.Copy).then_inc(ffh_ready, 1)
                t += 2 * (b - a)
                if b < NF1:
                    splits(t, t + KD)
                else:
                    splits_x(t, "mix2a")
                t += KD

            for l in range(2):
                c = att[l]
                root(2 + 2 * l)
                load_exp_and_ln()

                def proj(p, u, j):
                    m, p_ = qkv_tile(l, p, u, j)
                    split_hi(m + 1, p_)

                def split_qk(p, u, j, at_p):
                    if l == 1:
                        m, p_ = qkv_tile(l, at_p, u, j)
                        act.wait_ge(evac[p_], m + 1)
                        act.activation(qk_split[:, u, j, 0], qkv[:, u, j], ACT.Copy).then_inc(qk_high, 1)

                def v_split_high(p, u):
                    act.wait_ge(c.vt_done, p + 1)
                    if not (isinstance(p, int) and p < 2):
                        act.wait_ge(c.o_done, p - 1)
                    act.activation(v_split[:, u, 0], MB[:].rearrange("p (t f) -> p t f", t=NQ), ACT.Copy).then_inc(v_high, 1)

                def square(p):
                    act.wait_ge(c.o_done, p + 1)
                    act.activation(tmp[:, 2], OB[:], ACT.Square).then_inc(post_sq, 1)

                def head_norm(p):
                    act.wait_ge(post_mm, p + 1)
                    if not (isinstance(p, int) and p == 0):
                        act.wait_ge(post_t, p)
                    act.activation(rstd_h[:], TR[0][:], ACT.Ln, bias=eps_col).then_inc(post_ln, 1)
                    act.wait_ge(post_ln, p + 1)
                    act.activation(rstd_h[:], rstd_h[:], ACT.Exp, scale=-0.5).then_inc(post_r, 1)

                def high(p):
                    act.wait_ge(post_t, p + 1)
                    act.activation(ff_hi[:, bass.ds(p, 1)].rearrange("p o s -> p (o s)"), tmp[:, 0],
                                   ACT.Copy).then_inc(post_hi, 1)

                def group_sums(g0, g1, d0):
                    a, b = GROUPS[g0][0], GROUPS[g1 - 1][1]
                    act.wait_ge(c.lse_kept, b)
                    act.activation(lse_sm[:, a // 2:b // 2], lse_sm[:, a // 2:b // 2], ACT.Ln).then_inc(grp_a, 1)
                    act.wait_ge(grp_d, d0 + 3)
                    act.activation(lhe[:, 1, :, a:b], lhe[:, 1, :, a:b], ACT.Exp).then_inc(grp_a, 1)
                    act.wait_ge(grp_d, d0 + 4)
                    act.activation(grp[:, 1, :, g0:g1], grp[:, 1, :, g0:g1], ACT.Ln).then_inc(grp_a, 1)

                def pair(p, u, nxt):
                    exps(c, p, u, 0)
                    after = l == 1 and not (isinstance(p, int) and p == 0)
                    if after:
                        head_norm(p - 1)
                    if nxt is not None:
                        proj(nxt, 1 - u, 0)
                    copies(c, p, 0, pT)
                    if nxt is not None:
                        split_qk(p + 1, 1 - u, 0, nxt)
                    exps(c, p, u, 1)
                    if after:
                        high(p - 1)
                    if nxt is not None:
                        proj(nxt, 1 - u, 1)
                    copies(c, p, 1, pT)
                    if nxt is not None:
                        split_qk(p + 1, 1 - u, 1, nxt)
                    exps(c, p, u, 2)
                    exps(c, p, u, 3)
                    if nxt is not None:
                        proj(nxt, 1 - u, 2)
                    if l == 0 and isinstance(p, int) and p == NEAR - 1:
                        group_sums(0, 1, 0)
                    copies(c, p, 2, pT)
                    copies(c, p, 3, pT)
                    if l == 1:
                        if nxt is not None:
                            v_split_high(p + 1, 1 - u)
                        square(p)

                for j in range(3):
                    proj(0, 0, j)
                    if j < 2:
                        split_qk(0, 0, j, 0)
                if l == 1:
                    v_split_high(0, 0)
                pair(0, 0, 1)
                if l == 0:
                    pair(1, 1, 2)
                    pair(2, 0, 3)
                with act.Fori(1 - l, 3) as i:
                    pair(2 * i + 1, 1, (i + 1,))
                    pair(2 * i + 2, 0, (i + 1,))
                pair(7, 1, None)
                if l == 0:
                    group_sums(1, 3, 6)
                    act.wait_ge(grp_d, 12)
                    act.activation(grp[:, 2], grp[:, 2], ACT.Exp).then_inc(grp_a, 1)
                    for p in range(PAIRS):
                        act.wait_ge(gated, p + 1)
                        act.activation(ff_hi[:, p], tmp[:, p % 2], ACT.Copy).then_inc(gate_hi, 1)
                else:
                    head_norm(PAIRS - 1)
                    high(PAIRS - 1)
                splits_x(T_WO[l], ("mlp2a", "mlp2b")[l])
                root(3 + 2 * l)
                for n in range(NF2 // KD):
                    t = T_MLP2[l] + 2 * KD * n
                    f0 = NF2 * l + KD * n
                    with act.Fori(0, KD // 2) as i:
                        for p_ in range(2):
                            split_hi(i + t // 2 + 1, p_)
                            act.wait_ge(tile_done, 2 * i + t + p_ + 1)
                            act.wait_ge(ff_ready, 2 * i + f0 + NF1 + p_ - 1)
                            act.activation(tmp[:, p_], G[p_][:], ACT.Relu).then_inc(evac[p_], 1)
                            act.wait_ge(u_ready, 2 * i + f0 + p_ + 1)
                            act.activation(ff_hi[:, bass.ds(2 * i + p_, 1)].rearrange("p o s -> p (o s)"), tmp[:, 2 + p_],
                                           ACT.Square).then_inc(ffh_ready, 1)
                    t += KD
                    if n < NF2 // KD - 1:
                        splits(t, t + KD)
                    else:
                        splits_x(t, ("mix2b", "final")[l])
            root(6)

        @block.vector
        def _(dve):
            def add_tiles(t0):
                with dve.Fori(0, KD // 2) as i:
                    for p_ in range(2):
                        dve.wait_ge(tile_done, 2 * i + t0 + p_ + 1)
                        xs = x[:, bass.ds(2 * i + p_, 1)].rearrange("p o s -> p (o s)")
                        dve.tensor_tensor(xs, xs, G[p_][:], ALU.add).then_inc(evac[p_], 1)

            def low_x(i, k, n, g0):
                at_k = bass.ds(2 * i + k, 1)
                if g0 is not None:
                    dve.wait_ge(xh_ready, 2 * i + KD * n + k + 1)
                    dve.scalar_tensor_tensor(out=xn_lo[:, at_k].rearrange("p o s -> p (o s)"),
                                             in0=x[:, at_k].rearrange("p o s -> p (o s)"),
                                             scalar=par[:, bass.ds(2 * i + g0 + k, 1)],
                                             in1=xn_hi[:, at_k].rearrange("p o s -> p (o s)").bitcast(F32),
                                             op0=ALU.mult, op1=ALU.subtract).then_inc(xn_ready, 1)
                dve.wait_ge(sq_ready, 2 * i + KD * n + k + 1)
                if not (isinstance(i, int) and n == 0 and i == 0 and k == 0):
                    dve.wait_ge(acc_done, 2 * i + KD * n + k)
                dve.tensor_tensor(acc, acc, tmp[:, k], ALU.add).then_inc(acc_done, 1)

            def add_tiles_x(t0, n, name):
                dve.memset(acc, 0.0).then_inc(acc_zero, 1)
                dve.wait_ge(acc_zero, n + 1)
                with dve.Fori(0, KD // 2) as i:
                    for p_ in range(2):
                        dve.wait_ge(tile_done, 2 * i + t0 + p_ + 1)
                        xs = x[:, bass.ds(2 * i + p_, 1)].rearrange("p o s -> p (o s)")
                        dve.tensor_tensor(xs, xs, G[p_][:], ALU.add).then_inc(evac[p_], 1)
                        low_x(i, p_, n, None if name == "final" else _cols[name][0])
                inverse(n)

            def inverse(n):
                dve.wait_ge(ss_done, n + 1)
                dve.tensor_scalar(inv_tok, MB[:, 0:NQ], EPS, None, ALU.add).then_inc(eps_added, 1)
                dve.wait_ge(eps_added, n + 1)
                dve.reciprocal(inv_tok, inv_tok).then_inc(inv_ready, 1)

            def maxima(c, p, q_, n, sink=None):
                a, b = c.ranges(p, n)
                w = (b - a) * P
                off = (a - n + NQ - 1) * P
                ho = c.halves_out
                for h in range(2):
                    s = 2 * n + h
                    dve.wait_ge(c.scored, 8 * p + s + 1)
                    if not (isinstance(p, int) and p == 0 and n < 2):
                        dve.wait_ge(c.turned, ho * (4 * p + n - 2) + min(h, ho - 1) + 1)
                    dve.memset(small[:, 104 + 8 * q_ + s:105 + 8 * q_ + s], 0.0)
                    add = (swa_bias[:, p % 2, h, off - 2 * P:off - 2 * P + w] if c is swa else
                           bias[:, q_, h, off:off + w])
                    dve.tensor_tensor_reduce(out=prob[:, n % 2, h, 0:w], in0=SC[h][:, 0:w], in1=add, scale=1.0, scalar=-3e38,
                                             op0=ALU.add, op1=ALU.max,
                                             accum_out=mx[:, q_, s:s + 1]).then_inc(c.maxed, 1)
                for h in range(2):
                    s = 2 * n + h
                    dve.wait_ge(c.maxed, 8 * p + s + 1)
                    if sink is None:
                        ins = dve.tensor_scalar(nm[:, q_, s:s + 1], mx[:, q_, s:s + 1], -1.0, None, ALU.mult)
                    else:
                        ins = dve.tensor_scalar(nm[:, q_, s:s + 1], mx[:, q_, s:s + 1], sink(h), -1.0, ALU.max, ALU.mult)
                    ins.then_inc(c.negated, 1)

            def scale(c, p, q_, n, sink=None):
                a, b = c.ranges(p, n)
                s = slice(2 * n, 2 * n + 2)
                per = {swa: 2, att[0]: 1, att[1]: 3}[c]
                base = per * (4 * p + n)
                dve.wait_ge(c.expd, 8 * p + 2 * n + 2)
                if sink is not None:
                    dve.tensor_tensor(sm[:, q_, s], sm[:, q_, s], es[:, q_, s], ALU.add).then_inc(c.recd, 1)
                    dve.wait_ge(c.recd, base + 1)
                dve.reciprocal(rc[:, q_, s], sm[:, q_, s]).then_inc(c.recd, 1)
                dve.wait_ge(c.recd, base + (2 if sink is not None else 1))
                pr = [prob[:, n % 2, h, 0:(b - a) * P] for h in range(2)]
                rs = [rc[:, q_, 2 * n + h:2 * n + h + 1] for h in range(2)]
                if c is att[1]:
                    dve.tensor_scalar(rs[1], rs[1], neg_lam, None, ALU.mult).then_inc(c.recd, 1)
                    dve.tensor_scalar(pr[0], pr[0], rs[0], None, ALU.mult).then_inc(c.recd, 1)
                    dve.wait_ge(c.recd, base + 3)
                    dve.scalar_tensor_tensor(out=pr[0], in0=pr[1], scalar=rs[1], in1=pr[0], op0=ALU.mult,
                                             op1=ALU.add).then_inc(c.scaled, 1)
                else:
                    for h in range(2):
                        dve.tensor_scalar(pr[h], pr[h], rs[h], None, ALU.mult).then_inc(c.scaled, 1)

            def dlink(ins):
                link("dve", dve, ins)

            dve.memset(small[:, 0:96], 0.0)
            dve.memset(small[:, 96:128], EPS).then_inc(const_ready, 1)
            dve.memset(v_tok[:], 0.0).then_inc(const_ready, 1)
            dve.memset(acc, 0.0).then_inc(acc_zero, 1)
            dve.wait_ge(const_ready, 2)
            dve.wait_ge(acc_zero, 1)
            dve.wait_ge(par_in, 16)
            for k in range(KD):
                for i, (a, b) in enumerate(X_PARTS):
                    if k == a:
                        dve.wait_ge(x_in_done[i], 16)
                low_x(k // 2, k % 2, 0, _cols["mix_norm"][0])
            dve.wait_ge(glr_split, 1)
            dve.tensor_tensor(glr_w[:, 1], pcol("w_glr"), glr_w[:, 0].bitcast(F32), ALU.subtract).then_inc(glr_split, 1)
            inverse(0)
            dve.wait_ge(loaded, 32)
            dve.wait_ge(tab_mm, 1)
            for b in range(2):
                dve.tensor_copy(table_sb[:, 1, b * S:(b + 1) * S], SC[b][0:16])
                ins = dve.tensor_tensor(table_sb[:, 0, b * S:(b + 1) * S], SC[b][0:16],
                                        bucket[0:16, 1024 + b * S:1024 + (b + 1) * S], ALU.add)
                ins.then_inc(tab_sb, 1)
            dve.tensor_tensor(class_sb, OB[0:16, 0:256], bucket[0:16, 2304:2560], ALU.add).then_inc(tab_sb, 1)
            dve.tensor_scalar(pcol("q_norm"), pcol("q_norm"), 0.125, None, ALU.mult)
            dve.tensor_scalar(pcol("subln"), pcol("subln"), 1.0 - LAMBDA_INIT, None, ALU.mult)
            lam = pcol("lam").rearrange("p (i d) -> p i d", i=4)
            lam_prod = lhe[:].rearrange("p a n h -> p (a n h)").rearrange("p (i d) -> p i d", i=2)
            dlink(dve.tensor_tensor(lam_prod, lam[:, 0::2], lam[:, 1::2], ALU.mult))
            dve.tensor_reduce(lam_s[:, 0:2], lam_prod, mybir.AxisListType.X, ALU.add).then_inc(lam_sum, 1)

            def project(t):
                dve.wait_ge(tile_done, t + 1)
                dve.tensor_tensor(z[:, t], G[t % 2][:], rstd[:], ALU.mult).then_inc(evac[t % 2], 1)

            def swa_norm(i):
                dve.wait_ge(swn_r, i + 1)
                zi = z[:, i + 1 if i else 0]
                g = pcol("k_norm") if i == 0 else pcol("q_norm")
                dlink(dve.reciprocal(rstd_h[:], rstd_h[:]))
                dve.scalar_tensor_tensor(out=zi, in0=zi, scalar=g, in1=rstd_h[:], op0=ALU.mult, op1=ALU.mult).then_inc(swn_done, 1)

            dve.wait_ge(rstd_ready, 1)
            project(0)
            project(1)
            dve.wait_ge(glr_done, 1)
            dve.tensor_tensor(qkv[0:16, 0, 2], MB[0:16], rstd[0:16], ALU.mult).then_inc(glr_read, 1)
            project(2)
            dve.wait_ge(gate_in, 1)
            for j in range(2):
                b = pcol("b_alpha", j, j + 1)
                dve.tensor_scalar(qkv[:, j, 0], TR[j][:], b, 0.0, ALU.add, ALU.min).then_inc(gate_abs, 1)
            project(3)
            for j in range(2):
                dve.wait_ge(gate_log, j + 1)
                dlink(dve.tensor_tensor(qkv[:, j, 1], qkv[:, j, 0], qkv[:, j, 1], ALU.subtract))
                dve.tensor_tensor_scan(qkv[:, j, 0], ccol("reset"), qkv[:, j, 1], 0.0, ALU.mult, ALU.add).then_inc(decay_sum, 1)
                dve.wait_ge(decay_sum, j + 1)
                v = qkv[:, j, 0].rearrange("p (c t) -> p c t", t=CHUNK)
                dve.tensor_tensor(qkv[:, j, 2].rearrange("p (c t) -> p c t", t=CHUNK),
                                  v[:, :, CHUNK - 1:CHUNK].broadcast_to([P, NCH, CHUNK]), v, ALU.subtract).then_inc(decay_diff, 1)
            for t in range(4, 8):
                swa_norm(t - 4)
                project(t)
            dve.wait_ge(swv_t, 1)
            vt = MB[:].rearrange("p (t f) -> p t f", t=NQ)
            dve.tensor_copy(v_tok[:, 0, 0, :, 0:64], vt[:, :, 0:64])
            dve.tensor_copy(v_tok[:, 0, 1, :, 64:128], vt[:, :, 64:128]).then_inc(swv_done, 1)
            dve.wait_ge(tables_saved, 48)

            def keys(j):
                dve.wait_ge(decay_exp, j + 1)
                dve.scalar_tensor_tensor(out=z[:, Z_GQ + j], in0=z[:, Z_GQ + j], scalar=0.125, in1=tmp[:, 2 + j],
                                         op0=ALU.mult, op1=ALU.mult).then_inc(gla_keys, 1)
                dve.tensor_tensor(qkv[:, j, 1], z[:, Z_GK + j], qkv[:, j, 1], ALU.mult).then_inc(gla_keys, 1)
                dve.wait_ge(key_exp, j + 1)
                dve.tensor_tensor(qkv[:, j, 2], z[:, Z_GK + j], qkv[:, j, 2], ALU.mult).then_inc(gla_keys, 1)

            def token_major(p, n):
                h = 4 * (p - 2) + n
                if 0 <= h < GH + 2:
                    dve.wait_ge(turned_in, h + 1)
                    dst = gv_tok[:, h] if h < GH else kd_tok[h - GH]
                    dve.tensor_copy(dst, MB[:].rearrange("p (t f) -> p t f", t=NQ)).then_inc(turned_out, 1)

            for p in range(4):
                a, b = SWA_TILES[p]

                def sink(h, p=p):
                    return pcol("sinks", 2 * p + h, 2 * p + h + 1)
                dve.wait_ge(bias_in[p % 2], 16 * (p // 2 + 1))
                maxima(swa, p, 0, 0, sink)
                scale(swa, p, 0, 0, sink)
                project(a)
                if p == 0:
                    swa_norm(4)
                maxima(swa, p, 0, 1, sink)
                scale(swa, p, 0, 1, sink)
                project(a + 1)
                if p == 1:
                    keys(0)
                token_major(p, 0)
                maxima(swa, p, 0, 2, sink)
                scale(swa, p, 0, 2, sink)
                token_major(p, 1)
                if b - a == 3:
                    project(a + 2)
                if p == 1:
                    keys(1)
                maxima(swa, p, 0, 3, sink)
                scale(swa, p, 0, 3, sink)
                token_major(p, 2)
                dve.wait_ge(swa_hi, p + 1)
                dve.tensor_tensor(ff_lo[:, GH + p], OB[:], ff_hi[:, GH + p].bitcast(F32), ALU.subtract).then_inc(swa_lo, 1)
                token_major(p, 3)
            dve.wait_ge(lam_exp, 1)
            dlink(dve.tensor_tensor(neg_lam, lam_s[:, 3:4], lam_s[:, 2:3], ALU.subtract))
            dlink(dve.tensor_scalar(neg_lam, neg_lam, -LAMBDA_INIT, None, ALU.add))
            for i in range(GH):
                dve.wait_ge(gla_a, i + 1)
                dve.tensor_tensor(tmp[:, i].rearrange("p (t s) -> p t s", t=NQ),
                                  (TR[0], TR[1], OB, MB)[i][:].rearrange("p (t s) -> p t s", t=NQ),
                                  ccol("gla_mask").rearrange("p (o s) -> p o s", o=1).broadcast_to([P, NQ, P]),
                                  ALU.mult).then_inc(gla_masked, 1)
            dlink(dve.memset(state[:, :, 0], 0.0))
            for c in range(NCH - 1):
                for j in range(2):
                    i = 2 * c + j
                    dve.wait_ge(state_in, i + 1)
                    if c:
                        dve.wait_ge(state_out, 2 * (i - 1))
                    for h in range(2):
                        r = slice(64 * h, 64 * h + 64)
                        dve.scalar_tensor_tensor(out=state[r, j, c + 1], in0=state[r, j, c], scalar=decay[r, j, c:c + 1],
                                                 in1=(SC, TR)[j][c % 2][r, P * h:P * h + P], op0=ALU.mult,
                                                 op1=ALU.add).then_inc(state_out, 1)

            def gla_low(i):
                dve.wait_ge(gla_hi, i + 1)
                dve.tensor_tensor(ff_lo[:, i], tmp[:, i], ff_hi[:, i].bitcast(F32), ALU.subtract).then_inc(gla_lo, 1)

            dve.wait_ge(gates_on, GH)
            for i in range(GH):
                dve.wait_ge(gla_r, i + 1)
                dlink(dve.scalar_tensor_tensor(out=tmp[:, i], in0=gla_bank[i][:], scalar=pcol("gla_norm"), in1=gla_rstd[i],
                                               op0=ALU.mult, op1=ALU.mult))
                dve.tensor_tensor(tmp[:, i], tmp[:, i], z[:, Z_GR + i], ALU.mult).then_inc(gla_t, 1)
                if i >= 1:
                    gla_low(i - 1)
            gla_low(GH - 1)
            dve.wait_ge(gla_lo, GH)

            dve.memset(v_tok[:, 1], 0.0)
            add_tiles_x(T_OUT, 1, "ffn_norm")
            dve.wait_ge(rstd_ready, 2)
            t = T_MLP1
            for a, b in CHUNKS1:
                with dve.Fori(0, b - a) as i:
                    f, m = i + a, i + t // 2
                    for p_ in range(2):
                        cs = [par[:, bass.ds(_cols["conv_w"][0] + 2 * NF1 * j + 2 * f + p_, 1)] for j in range(2)]
                        u = tmp[:, 2 + p_]
                        dve.wait_ge(tile_done, 2 * m + p_ + 1)
                        dve.tensor_tensor(u, G[p_][:], rstd[:], ALU.mult).then_inc(evac[p_], 1)
                        dve.wait_ge(conv_0, 2 * f + p_ + 1)
                        dve.scalar_tensor_tensor(out=tmp[:, p_, 1:S], in0=u[:, 0:S - 1], scalar=cs[1], in1=tmp[:, p_, 1:S],
                                                 op0=ALU.mult, op1=ALU.add).then_inc(conv_1, 1)
                        dve.wait_ge(conv_1, 2 * f + p_ + 1)
                        dve.scalar_tensor_tensor(out=tmp[:, p_, 2:S], in0=u[:, 0:S - 2], scalar=cs[0], in1=tmp[:, p_, 2:S],
                                                 op0=ALU.mult, op1=ALU.add).then_inc(conv_2, 1)
                    dve.wait_ge(silu_done, f + 1)
                    dve.wait_ge(conv_2, 2 * f + 2)
                    dve.tensor_tensor(tmp[:, 1], tmp[:, 0], tmp[:, 1], ALU.mult).then_inc(f_made, 1)
                    dve.wait_ge(ffh_ready, f + 1)
                    dve.tensor_tensor(ff_lo[:, bass.ds(i, 1)].rearrange("p o s -> p (o s)"), tmp[:, 1],
                                      ff_hi[:, bass.ds(i, 1)].rearrange("p o s -> p (o s)").bitcast(F32),
                                      ALU.subtract).then_inc(ff_ready, 1)
                t += 2 * (b - a)
                if b < NF1:
                    add_tiles(t)
                else:
                    add_tiles_x(t, 2, "mix2a")
                t += KD

            for l in range(2):
                c = att[l]
                dve.wait_ge(rstd_ready, 3 + 2 * l)

                def project(p, u, j):
                    m, p_ = qkv_tile(l, p, u, j)
                    dve.wait_ge(tile_done, 2 * m + p_ + 1)
                    dst = qkv[:, u, j].rearrange("p (n s) -> p n s", n=NQ)
                    order = "p (n s) -> p n s" if l == 1 or near(p) else "p (s n) -> p n s"
                    src, rs = G[p_][:].rearrange(order, n=NQ), rstd[:].rearrange(order, n=NQ)
                    if j == 0:
                        dst = dst[:, :, ::-1]
                    dve.scalar_tensor_tensor(out=dst, in0=src, scalar=(0.125 if j == 0 else 1.0), in1=rs, op0=ALU.mult,
                                             op1=ALU.mult).then_inc(evac[p_], 1)

                def split_qk(p, u, j):
                    if l == 1:
                        dve.wait_ge(qk_high, 2 * p + j + 1)
                        dve.tensor_tensor(qk_split[:, u, j, 1], qkv[:, u, j], qk_split[:, u, j, 0].bitcast(F32),
                                          ALU.subtract).then_inc(qk_low, 1)

                def turned_low(p, n):
                    if l == 1:
                        dve.wait_ge(c.copied, 4 * p + n + 1)
                        cols = slice(n * P, (n + 1) * P)
                        dve.tensor_tensor(pT_split[:, 1, :, cols], TR[n % 2][:].rearrange("p (k s) -> p k s", k=NQ),
                                          pT_split[:, 0, :, cols].bitcast(F32), ALU.subtract).then_inc(pt_low, 1)

                def head_out(p):
                    dve.wait_ge(post_r, p + 1)
                    if not (isinstance(p, int) and p == 0):
                        dve.wait_ge(post_lo, p + PAIRS)
                    dve.scalar_tensor_tensor(out=tmp[:, 0], in0=OB[:], scalar=pcol("subln"), in1=rstd_h[:],
                                             op0=ALU.mult, op1=ALU.mult).then_inc(post_t, 1)

                def head_low(p):
                    dve.wait_ge(post_hi, p + 1)
                    at_p = bass.ds(p, 1)
                    dve.tensor_tensor(ff_lo[:, at_p].rearrange("p o s -> p (o s)"), tmp[:, 0],
                                      ff_hi[:, at_p].rearrange("p o s -> p (o s)").bitcast(F32),
                                      ALU.subtract).then_inc(post_lo, 1)

                def v_copy(p, u):
                    dve.wait_ge(c.vt_done, p + 1)
                    if l == 0 and not (isinstance(p, int) and p < 2):
                        dve.wait_ge(c.o_done, p - 1)
                    vt = MB[:].rearrange("p (t f) -> p t f", t=NQ)
                    if l == 0:
                        dve.tensor_copy(v_tok[:, u, 0, :, 0:64], vt[:, :, 0:64])
                        ins = dve.tensor_copy(v_tok[:, u, 1, :, 64:128], vt[:, :, 64:128])
                    else:
                        dve.wait_ge(v_high, p + 1)
                        ins = dve.tensor_tensor(v_split[:, u, 1], vt, v_split[:, u, 0].bitcast(F32), ALU.subtract)
                    ins.then_inc(c.v_ready, 1)

                def group_sums(g0, g1, a0):
                    ha, hb = GROUPS[g0][0], GROUPS[g1 - 1][1]
                    pa, pb = ha // 2, hb // 2
                    gs = list(enumerate(GROUPS))[g0:g1]
                    dve.wait_ge(grp_a, a0 + 1)
                    dlink(dve.tensor_tensor(lse_sm[:, pa:pb], lse_sm[:, pa:pb], lse_nm[:, pa:pb], ALU.subtract))
                    dve.tensor_copy(lhe[:, 0, :, ha:hb].rearrange("p n (q h) -> p q n h", h=2),
                                    lse_sm[:, pa:pb].rearrange("p q (n h) -> p q n h", h=2)).then_inc(grp_d, 1)
                    dve.wait_ge(grp_d, 2 * a0 + 1)
                    for g, (a, b) in gs:
                        ins = dve.tensor_reduce(grp[:, 0, :, g:g + 1].rearrange("p n o -> p (n o)"), lhe[:, 0, :, a:b],
                                                mybir.AxisListType.X, ALU.max)
                    ins.then_inc(grp_d, 1)
                    dve.wait_ge(grp_d, 2 * a0 + 2)
                    for g, (a, b) in gs:
                        ins = dve.tensor_tensor(lhe[:, 1, :, a:b], lhe[:, 0, :, a:b],
                                                grp[:, 0, :, g:g + 1].broadcast_to([P, NQ, b - a]), ALU.subtract)
                    ins.then_inc(grp_d, 1)
                    dve.wait_ge(grp_a, a0 + 2)
                    for g, (a, b) in gs:
                        ins = dve.tensor_reduce(grp[:, 1, :, g:g + 1].rearrange("p n o -> p (n o)"), lhe[:, 1, :, a:b],
                                                mybir.AxisListType.X, ALU.add)
                    ins.then_inc(grp_d, 1)
                    dve.wait_ge(grp_a, a0 + 3)
                    dlink(dve.tensor_tensor(grp[:, 1, :, g0:g1], grp[:, 1, :, g0:g1], grp[:, 0, :, g0:g1], ALU.add))
                    for g, (a, b) in gs:
                        ins = dve.tensor_scalar(grp[:, 1, :, g:g + 1], grp[:, 1, :, g:g + 1], -math.log(b - a), None, ALU.add)
                    return ins

                def pair(p, u, nxt):
                    dve.wait_ge(bias_in[u], 16 * (2 + 4 * l) + (16 * (p // 2 + 1) if isinstance(p, int) else 16 * nxt_of(p, u)))
                    after = l == 1 and not (isinstance(p, int) and p == 0)
                    maxima(c, p, u, 0)
                    scale(c, p, u, 0)
                    if after:
                        head_out(p - 1)
                    if nxt is not None:
                        project(nxt, 1 - u, 0)
                    maxima(c, p, u, 1)
                    turned_low(p, 0)
                    scale(c, p, u, 1)
                    if after:
                        head_low(p - 1)
                    if nxt is not None:
                        split_qk(p + 1, 1 - u, 0)
                        project(nxt, 1 - u, 1)
                    maxima(c, p, u, 2)
                    turned_low(p, 1)
                    maxima(c, p, u, 3)
                    scale(c, p, u, 2)
                    scale(c, p, u, 3)
                    last_near = l == 0 and isinstance(p, int) and p == NEAR - 1
                    if l == 0:
                        at_p = bass.ds(p, 1)
                        dve.tensor_copy(lse_nm[:, at_p].rearrange("p o s -> p (o s)"), nm[:, u]).then_inc(c.lse_kept, 1)
                        dve.tensor_copy(lse_sm[:, at_p].rearrange("p o s -> p (o s)"), sm[:, u]).then_inc(c.lse_kept, 1)
                    if last_near:
                        group_sums(0, 1, 0).then_inc(grp_d, 1)
                    if nxt is not None:
                        split_qk(p + 1, 1 - u, 1)
                        project(nxt, 1 - u, 2)
                    turned_low(p, 2)
                    turned_low(p, 3)
                    if last_near:
                        dve.wait_ge(grp_t, 1)
                        dve.tensor_copy(near_row.rearrange("p (n s) -> p n s", n=NQ)[:, :, ::-1],
                                        SC[1][0:1].rearrange("p (s n) -> p n s", n=NQ)).then_inc(grp_row, 1)
                    if l == 0:
                        dve.wait_ge(c.o_done, p + 1)
                        o = oT[:, at_p].rearrange("p o s -> p (o s)")
                        if near(p):
                            dve.tensor_copy(o, OB[:]).then_inc(c.o_read, 1)
                        else:
                            dve.tensor_copy(o.rearrange("p (s n) -> p n s", n=NQ),
                                            OB[:].rearrange("p (n s) -> p n s", n=NQ)).then_inc(c.o_read, 1)
                    if last_near:
                        dve.wait_ge(grp_t, 2)
                        dve.tensor_copy(grp[:, 1, :, 0:1].rearrange("p n o -> p (n o)"), SC[0][:, 0:NQ]).then_inc(grp_d, 1)
                    if nxt is not None:
                        v_copy(p + 1, 1 - u)

                loop = {}

                def nxt_of(p, u):
                    return loop["i"] + (1 if u == 1 else 2)

                for j in range(3):
                    project(0, 0, j)
                    if j < 2:
                        split_qk(0, 0, j)
                v_copy(0, 0)
                pair(0, 0, 1)
                if l == 0:
                    pair(1, 1, 2)
                    pair(2, 0, 3)
                with dve.Fori(1 - l, 3) as i:
                    loop["i"] = i
                    pair(2 * i + 1, 1, (i + 1,))
                    pair(2 * i + 2, 0, (i + 1,))
                pair(7, 1, None)

                if l == 0:
                    dlink(group_sums(1, 3, 3))
                    m3 = small[:, 88:92]
                    dve.tensor_reduce(m3, grp[:, 1], mybir.AxisListType.X, ALU.max).then_inc(grp_d, 1)
                    dve.wait_ge(grp_d, 11)
                    dve.tensor_tensor(grp[:, 2], grp[:, 1], m3.rearrange("p (n o) -> p n o", o=1).broadcast_to([P, NQ, 3]),
                                      ALU.subtract).then_inc(grp_d, 1)
                    dve.wait_ge(grp_a, 7)
                    s3 = small[:, 92:96]
                    dlink(dve.tensor_reduce(s3, grp[:, 2], mybir.AxisListType.X, ALU.add))
                    dve.reciprocal(s3, s3).then_inc(grp_d, 1)
                    dve.wait_ge(grp_d, 13)
                    dve.scalar_tensor_tensor(out=grp[:, 5], in0=grp[:, 2], scalar=3.0,
                                             in1=s3.rearrange("p (n o) -> p n o", o=1).broadcast_to([P, NQ, 3]),
                                             op0=ALU.mult, op1=ALU.mult).then_inc(grp_d, 1)
                    dve.wait_ge(grp_t, 3)
                    dve.tensor_copy(tmp[0:3, 3].rearrange("p (s n) -> p n s", n=NQ),
                                    MB[0:3].rearrange("p (n s) -> p n s", n=NQ)).then_inc(grp_row, 1)

                    def low(p):
                        dve.wait_ge(gate_hi, p + 1)
                        dve.tensor_tensor(ff_lo[:, p], tmp[:, p % 2], ff_hi[:, p].bitcast(F32), ALU.subtract).then_inc(post_lo, 1)

                    for p in range(PAIRS):
                        i = sum(p >= first for first in GATES) - 1
                        dve.wait_ge(gate_mm, i + 1)
                        if p >= 2:
                            dve.wait_ge(post_lo, p - 1)
                        dve.tensor_tensor(tmp[:, p % 2], oT[:, p], gate_bank[i][:], ALU.mult).then_inc(gated, 1)
                        if p >= 1:
                            low(p - 1)
                    low(PAIRS - 1)
                else:
                    head_out(PAIRS - 1)
                    head_low(PAIRS - 1)
                add_tiles_x(T_WO[l], 3 + 2 * l, ("mlp2a", "mlp2b")[l])
                dve.wait_ge(rstd_ready, 4 + 2 * l)
                for n in range(NF2 // KD):
                    t = T_MLP2[l] + 2 * KD * n
                    f0 = NF2 * l + KD * n

                    def low2(i, p_):
                        dve.wait_ge(ffh_ready, 2 * i + f0 + NF1 + p_ + 1)
                        at_f = bass.ds(2 * i + p_, 1)
                        dve.tensor_tensor(ff_lo[:, at_f].rearrange("p o s -> p (o s)"), tmp[:, p_],
                                          ff_hi[:, at_f].rearrange("p o s -> p (o s)").bitcast(F32),
                                          ALU.subtract).then_inc(ff_ready, 1)
                    with dve.Fori(0, KD // 2) as i:
                        for p_ in range(2):
                            dve.wait_ge(evac[p_], i + t // 2 + 1)
                            dve.tensor_tensor(tmp[:, 2 + p_], tmp[:, p_], rstd[:], ALU.mult).then_inc(u_ready, 1)
                            dve.wait_ge(u_ready, 2 * i + f0 + p_ + 1)
                            dve.tensor_tensor(tmp[:, p_], tmp[:, 2 + p_], tmp[:, 2 + p_], ALU.mult).then_inc(squared, 1)
                            dve.wait_ge(squared, 2 * i + f0 + p_ + 1)
                            low2(i, p_)
                    if n < NF2 // KD - 1:
                        add_tiles(t + KD)
                    else:
                        add_tiles_x(t + KD, 4 + 2 * l, ("mix2b", "final")[l])
            dve.wait_ge(rstd_ready, 7)
            dve.wait_ge(scaled_out, KD)
            for k in range(OUT_DVE):
                dve.tensor_tensor(z[:, k], z[:, k], rstd[:], ALU.mult).then_inc(final_ready, 1)


def _buckets():
    nb, me = 16, 8

    def one_hot(rel):
        n = np.abs(rel)
        nf = np.maximum(n, 1).astype(np.float32)
        large = me + (np.log(nf / np.float32(me)) / np.float32(math.log(1024 / me)) * np.float32(nb - me)).astype(np.int32)
        bucket = np.where(rel > 0, nb, 0) + np.where(n < me, n, np.minimum(large, nb - 1))
        return (bucket[None] == np.arange(32)[:, None]).astype(np.float32)

    def masks(rel):
        n = np.abs(rel)
        rows = [np.where((n % dil == 0) & (n <= win // 2), 0.0, NEG) for win, dil, nh in
                ((128, 1, 6), (512, 4, 5), (2048, 16, 5)) for _ in range(nh)]
        return np.pad(np.stack(rows), ((0, 16), (0, 0)))
    every = np.arange(1024) - (S - 1)
    own = DIL * (np.arange(256) - (P - 1))
    return np.concatenate([one_hot(every), masks(every), one_hot(own), masks(own)], axis=1).astype(np.float32)


def _swa_table():
    dist = (WIN + np.arange(P)[:, None] - np.arange(2 * P)[None]).astype(np.float32)
    rows = []
    for h in (0, 4, 1, 5, 2, 6, 3, 7):
        slope = np.float32(2.0 ** (-(h + 1)))
        rows.append(np.where((dist >= 0) & (dist < WIN), -slope * dist, np.float32(NEG)))
    return np.ascontiguousarray(np.stack(rows).reshape(4, 2, P, 2 * P).transpose(0, 2, 1, 3).astype(np.float32))


def _constants():
    c = np.zeros((P, N_CON), np.float32)

    def put(name, a):
        s, e = _ccols[name]
        c[:a.shape[0], s:e] = a
    put("ident", np.eye(P))
    put("flip", np.eye(P)[::-1])
    put("mean_d", np.full((P, P), 1.0 / D))
    put("mean_128", np.full((P, P), 1.0 / 128))
    put("mean_64", np.kron(np.eye(2), np.full((64, 64), 1.0 / 64)))
    i = np.arange(P)
    put("gla_mask", (i[:, None] <= i[None, :]) & (i[:, None] // CHUNK == i[None, :] // CHUNK))
    put("reset", np.tile((np.arange(S) % CHUNK != 0)[None], (P, 1)))
    return c


def _tiles(w):
    k, n = w.shape
    return w.reshape(k // P, P, n // P, P).transpose(2, 1, 0, 3).reshape(n // P, P, (k // P) * P)


def _weights(i):
    w = i["w_in"][0]
    parts = np.split(w, np.cumsum([256, 256, 512, 512, 16, 512, 128])[:7], axis=1)
    gq, gk, gv, gr, _, sq, sk, sv = parts
    heads = sq.reshape(D, 8, 64)[:, [0, 4, 1, 5, 2, 6, 3, 7]].reshape(D, 512)
    seq = [_tiles(np.concatenate([sk, sv, heads, gq, gk, gv, gr], axis=1))]
    wo = i["w_out"][0]
    low = wo[512:].reshape(8, 64, D)[[0, 4, 1, 5, 2, 6, 3, 7]].reshape(512, D)
    seq.append(_tiles(np.concatenate([wo[:512], low])))
    up = i["w_up"][0].reshape(D, 2, NF1, P).transpose(0, 2, 1, 3).reshape(D, 2 * FF1)
    up, down = _tiles(up), i["w_down"][0]
    for a, b in CHUNKS1:
        seq.append(up[2 * a:2 * b])
        t = _tiles(down[a * P:b * P])
        seq.append(np.pad(t, ((0, 0), (0, 0), (0, D - t.shape[2]))))
    for l, (qkv, wo) in enumerate((("a_w_qkv_2", "a_w_o_2"), ("b_w_qkv_2", "b_w_o_2"))):
        w = i[qkv][0].reshape(D, 3, PAIRS, P).transpose(0, 2, 1, 3).reshape(D, 3 * D)
        seq += [_tiles(w), _tiles(i[wo][0])]
        up, down = _tiles(i["mlp_w_in_2"][l]), i["mlp_w_out_2"][l]
        for n in range(NF2 // KD):
            seq += [up[KD * n:KD * n + KD], _tiles(down[D * n:D * n + D])]
    return np.concatenate(seq)


def _params(i):
    p = np.zeros((P, N_PAR), np.float32)

    def put(name, a):
        s, e = _cols[name]
        p[:a.shape[0], s:e] = a

    def cols(v):
        return v.reshape(-1, P).T
    put("mix_norm", cols(i["mix_norm"][0]))
    put("ffn_norm", cols(i["ffn_norm"][0]))
    for l in range(2):
        put(("mix2a", "mix2b")[l], cols(i["norm_mix_g_2"][l]))
        put(("mlp2a", "mlp2b")[l], cols(i["norm_mlp_g_2"][l]))
    put("final", cols(i["norm_final_g_2"]))
    cw = i["conv_w"][0].reshape(3, 2, NF1, P)
    put("conv_w", cw.transpose(3, 0, 2, 1).reshape(P, -1))
    put("conv_b", i["conv_b"][0].reshape(2, NF1, P).transpose(2, 1, 0).reshape(P, -1))
    put("b_alpha", cols(i["b_alpha"][0]))
    put("gla_norm", i["gla_norm"][0][:, None])
    put("q_norm", np.tile(i["q_norm"][0], 2)[:, None])
    put("k_norm", np.tile(i["k_norm"][0], 2)[:, None])
    put("subln", i["b_subln_g_2"][0][:, None])
    put("sinks", np.tile(i["sinks"][0][[0, 4, 1, 5, 2, 6, 3, 7]][None], (P, 1)))
    put("lam", np.tile(i["b_lambda_2"][0].reshape(1, 256), (P, 1)))
    glr = np.zeros((KD, P, 32), np.float32)
    glr[:, :, :16] = i["w_in"][0][:, 1536:1552].reshape(KD, P, 16)
    put("w_glr", glr.transpose(1, 0, 2).reshape(P, -1))
    put("w_alpha", i["w_alpha2"][0])
    put("rel_bias", i["rel_bias_2"])
    return p


def kernel(**inputs):
    import concourse.bacc as bacc
    from concourse.bass_utils import run_bass_kernel_spmd

    i = {k: np.asarray(v) for k, v in inputs.items()}
    arrays = {
        "x_in": np.ascontiguousarray(i["x"][0].reshape(S, KD, P).transpose(2, 1, 0)),
        "params": _params(i),
        "consts": _constants(),
        "sel": (np.repeat([0] * 6 + [1] * 5 + [2] * 5, 64)[None] == np.arange(3)[:, None]).astype(np.float32),
        "buckets": _buckets(),
        "swa_table": _swa_table(),
        "weights": _weights(i),
    }
    nc = bacc.Bacc("TRN2", target_bir_lowering=False, num_devices=1)
    args = [nc.dram_tensor(n, a.shape, F32, kind="ExternalInput").ap() for n, a in arrays.items()]
    tables = [nc.dram_tensor(f"table{l}", (16, w), F32, kind="Internal").ap() for l, w in enumerate((1024, 1024, 256))]
    out = nc.dram_tensor("out", (P, KD, S), F32, kind="ExternalOutput").ap()
    program(nc, *args, tables, out)
    r = run_bass_kernel_spmd(nc, [arrays], core_ids=[0])
    return r.results[0]["out"].transpose(2, 1, 0).reshape(1, S, D)
```
